# Optimizing a Trainium2 kernel written in Bass

```python
import math
import jax, jax.numpy as jnp
from jax import lax
import numpy as np

D_MODEL = 1024
BATCH = 1
SEQ = 256
DEPTH = 1

CHUNK = 64
N_MEM = 256
EPS = 1e-6
SB_HEADS = 8
SB_HEAD_DIM = 64
SB_WIDTH = SB_HEADS * SB_HEAD_DIM
SB_Q_BLOCK = 128
GDN_HEADS = 4
GDN_HEAD_DIM = 128
GDN_WIDTH = GDN_HEADS * GDN_HEAD_DIM
CONV_WIDTH = 4
X_HEADS = 4
X_HEAD_DIM = D_MODEL // X_HEADS
PEER_HEADS = 8
PEER_KEYS = 128
PEER_EXPERTS = PEER_KEYS * PEER_KEYS
PEER_TOPK = 16
PEER_QDIM = 256
PEER_TOKEN_BLOCK = 128
IN_SPLIT_SIZES = (SB_WIDTH, SB_WIDTH, SB_WIDTH, GDN_WIDTH, GDN_WIDTH, GDN_WIDTH, GDN_WIDTH,
                  GDN_HEADS, GDN_HEADS, D_MODEL, D_MODEL)
IN_COLS = 3 * SB_WIDTH + 4 * GDN_WIDTH + 2 * GDN_HEADS + 2 * D_MODEL


def rmsnorm(x, g):
    xf = x.astype(jnp.float32)
    y = xf * lax.rsqrt(jnp.mean(xf * xf, axis=-1, keepdims=True) + EPS)
    return (y * g.astype(jnp.float32)).astype(x.dtype)

def l2norm(x):
    xf = x.astype(jnp.float32)
    return xf * lax.rsqrt(jnp.sum(xf * xf, axis=-1, keepdims=True) + EPS)

def causal_dwconv(x, w):
    K = w.shape[0]
    S = x.shape[1]
    xp = jnp.pad(x, ((0, 0), (K - 1, 0), (0, 0)))
    return sum(xp[:, j:j + S] * w[j] for j in range(K))

def stick_breaking_attention(q, k, v):
    S, d = q.shape[2], q.shape[3]
    scale = d ** -0.5
    outs = []
    for i in range(S // SB_Q_BLOCK):
        q0 = i * SB_Q_BLOCK
        kv_len = q0 + SB_Q_BLOCK
        qb = q[:, :, q0:kv_len]
        kb = k[:, :, :kv_len]
        vb = v[:, :, :kv_len]
        z = jnp.einsum('bhqd,bhkd->bhqk', qb, kb).astype(jnp.float32) * scale
        qpos = q0 + jnp.arange(SB_Q_BLOCK)[:, None]
        kpos = jnp.arange(kv_len)[None, :]
        mask = kpos < qpos
        log_keep = jnp.where(mask, jax.nn.log_sigmoid(-z), 0.0)
        after = lax.cumsum(log_keep, axis=3, reverse=True) - log_keep
        a = jnp.where(mask, jnp.exp(jax.nn.log_sigmoid(z) + after), 0.0)
        outs.append(jnp.einsum('bhqk,bhkd->bhqd', a.astype(v.dtype), vb))
    return jnp.concatenate(outs, axis=2)

def gated_delta_rule(q, k, v, beta, g):
    B, S, H, dk = q.shape
    dv = v.shape[-1]
    N, C = S // CHUNK, CHUNK
    f32 = jnp.float32

    def chunk4(t):
        return jnp.moveaxis(t.astype(f32).reshape(B, N, C, H, t.shape[-1]), 3, 1)

    def chunk3(t):
        return jnp.moveaxis(t.astype(f32).reshape(B, N, C, H), 3, 1)

    q = chunk4(q) * (dk ** -0.5)
    k = chunk4(k)
    v = chunk4(v)
    beta = chunk3(beta)
    gc = jnp.cumsum(chunk3(g), axis=-1)
    idx = jnp.arange(C)
    incl = idx[:, None] >= idx[None, :]
    strict = idx[:, None] > idx[None, :]
    decay = jnp.exp(jnp.where(incl, gc[..., :, None] - gc[..., None, :], -jnp.inf))
    kb = k * beta[..., None]
    vb = v * beta[..., None]
    a = jnp.where(strict, jnp.einsum('bhncd,bhnmd->bhncm', kb, k) * decay, 0.0)
    eye = jnp.eye(C, dtype=f32)
    rhs = jnp.concatenate([vb, kb * jnp.exp(gc)[..., None]], axis=-1)
    sol = lax.linalg.triangular_solve(a + eye, rhs, left_side=True, lower=True, unit_diagonal=True)
    u = sol[..., :dv]
    w = sol[..., dv:]
    qk = jnp.einsum('bhncd,bhnmd->bhncm', q, k) * decay
    q_dec = q * jnp.exp(gc)[..., None]
    k_dec = k * jnp.exp(gc[..., -1:] - gc)[..., None]
    chunk_decay = jnp.exp(gc[..., -1])
    xs = tuple(jnp.moveaxis(t, 2, 0) for t in (q_dec, k_dec, u, w, qk, chunk_decay))

    def step(state, inp):
        qd, kd, u_n, w_n, qk_n, cd = inp
        v_new = u_n - jnp.einsum('bhcd,bhde->bhce', w_n, state)
        o = jnp.einsum('bhcd,bhde->bhce', qd, state) + jnp.einsum('bhcm,bhme->bhce', qk_n, v_new)
        state = state * cd[..., None, None] + jnp.einsum('bhcd,bhce->bhde', kd, v_new)
        return state, o

    state0 = jnp.zeros((B, H, dk, dv), f32)
    _, o = lax.scan(step, state0, xs)
    return jnp.transpose(o, (1, 0, 3, 2, 4)).reshape(B, S, H, dv)

def token_mixer(xn, w_in, gdn_conv, gdn_a_log, gdn_dt_bias, gdn_norm_g, w_sb_up, w_gdn_up, w_mix_out):
    B, S, _ = xn.shape
    proj = xn @ w_in
    offs = [int(o) for o in np.cumsum(IN_SPLIT_SIZES)[:-1]]
    (sb_q, sb_k, sb_v, g_q, g_k, g_v, g_z, g_b, g_a, gate_sb, gate_gdn) = jnp.split(proj, offs, axis=-1)

    def heads_sb(t):
        return t.reshape(B, S, SB_HEADS, SB_HEAD_DIM).transpose(0, 2, 1, 3)
    o_sb = stick_breaking_attention(heads_sb(sb_q), heads_sb(sb_k), heads_sb(sb_v))
    o_sb = o_sb.transpose(0, 2, 1, 3).reshape(B, S, SB_WIDTH)

    qkv = jax.nn.silu(causal_dwconv(jnp.concatenate([g_q, g_k, g_v], axis=-1), gdn_conv))
    cq, ck, cv = jnp.split(qkv, 3, axis=-1)
    cq = l2norm(cq.reshape(B, S, GDN_HEADS, GDN_HEAD_DIM))
    ck = l2norm(ck.reshape(B, S, GDN_HEADS, GDN_HEAD_DIM))
    cv = cv.reshape(B, S, GDN_HEADS, GDN_HEAD_DIM)
    beta = jax.nn.sigmoid(g_b.astype(jnp.float32))
    g = -jnp.exp(gdn_a_log.astype(jnp.float32)) * jax.nn.softplus(g_a.astype(jnp.float32) + gdn_dt_bias.astype(jnp.float32))
    o_g = gated_delta_rule(cq, ck, cv, beta, g).astype(xn.dtype)
    o_g = rmsnorm(o_g, gdn_norm_g) * jax.nn.silu(g_z.reshape(B, S, GDN_HEADS, GDN_HEAD_DIM))
    o_g = o_g.reshape(B, S, GDN_WIDTH)

    merged = jax.nn.sigmoid(gate_sb) * (o_sb @ w_sb_up) + jax.nn.sigmoid(gate_gdn) * (o_g @ w_gdn_up)
    return merged @ w_mix_out

def memory_cross_attention(hn, mn, w_cq, w_ckv, w_co):
    B, S, _ = hn.shape
    M = mn.shape[1]
    q = (hn @ w_cq).reshape(B, S, X_HEADS, X_HEAD_DIM)
    k, v = jnp.split(mn @ w_ckv, 2, axis=-1)
    k = k.reshape(B, M, X_HEADS, X_HEAD_DIM)
    v = v.reshape(B, M, X_HEADS, X_HEAD_DIM)
    s = jnp.einsum('bshd,bmhd->bhsm', q, k).astype(jnp.float32) * (X_HEAD_DIM ** -0.5)
    p = jax.nn.softmax(s, axis=-1).astype(v.dtype)
    o = jnp.einsum('bhsm,bmhd->bshd', p, v).reshape(B, S, D_MODEL)
    return o @ w_co

def peer(xn, w_pq, subkeys, peer_u, peer_v):
    B, S, D = xn.shape
    T = B * S
    xt = xn.reshape(T, D)
    q = (xt @ w_pq).reshape(T, PEER_HEADS, 2, PEER_QDIM // 2)
    s = jnp.einsum('thpd,hpnd->thpn', q, subkeys).astype(jnp.float32)
    top_s, top_i = lax.top_k(s, PEER_TOPK)
    cand_s = top_s[:, :, 0, :, None] + top_s[:, :, 1, None, :]
    cand_i = top_i[:, :, 0, :, None] * PEER_KEYS + top_i[:, :, 1, None, :]
    kk = PEER_TOPK * PEER_TOPK
    best_s, best_pos = lax.top_k(cand_s.reshape(T, PEER_HEADS, kk), PEER_TOPK)
    expert = jnp.take_along_axis(cand_i.reshape(T, PEER_HEADS, kk), best_pos, axis=-1)
    gate = jax.nn.softmax(best_s, axis=-1).astype(xn.dtype)
    nb = T // PEER_TOKEN_BLOCK

    def block(args):
        xb, eb, gb = args
        act = jax.nn.gelu(jnp.einsum('thkd,td->thk', peer_u[eb], xb), approximate=False) * gb
        return jnp.einsum('thk,thkd->td', act, peer_v[eb])

    out = lax.map(block, (xt.reshape(nb, PEER_TOKEN_BLOCK, D),
                          expert.reshape(nb, PEER_TOKEN_BLOCK, PEER_HEADS, PEER_TOPK),
                          gate.reshape(nb, PEER_TOKEN_BLOCK, PEER_HEADS, PEER_TOPK)))
    return out.reshape(B, S, D)

def first_inputs(seed: int = 0) -> dict:
    key = jax.random.key(seed)
    ks = jax.random.split(key, 24)
    f32 = jnp.float32

    def nrm(k, shape, scale):
        return jax.random.normal(k, shape, f32) * scale

    def gain(k, shape):
        return 1.0 + 0.02 * jax.random.normal(k, shape, f32)

    L, D = DEPTH, D_MODEL
    a_log = jnp.log(jax.random.uniform(ks[5], (L, GDN_HEADS), f32, 1.0, 16.0))
    dt = jnp.exp(jax.random.uniform(ks[6], (L, GDN_HEADS), f32, math.log(1e-3), math.log(1e-1)))
    dt_bias = dt + jnp.log(-jnp.expm1(-dt))
    return {
        "x": nrm(ks[0], (BATCH, SEQ, D), 1.0),
        "mem": nrm(ks[1], (BATCH, N_MEM, D), 1.0),
        "g_mix": gain(ks[2], (L, D)),
        "w_in": nrm(ks[3], (L, D, IN_COLS), D ** -0.5),
        "gdn_conv": nrm(ks[4], (L, CONV_WIDTH, 3 * GDN_WIDTH), CONV_WIDTH ** -0.5),
        "gdn_a_log": a_log,
        "gdn_dt_bias": dt_bias,
        "gdn_norm_g": gain(ks[7], (L, GDN_HEAD_DIM)),
        "w_sb_up": nrm(ks[8], (L, SB_WIDTH, D), SB_WIDTH ** -0.5),
        "w_gdn_up": nrm(ks[9], (L, GDN_WIDTH, D), GDN_WIDTH ** -0.5),
        "w_mix_out": nrm(ks[10], (L, D, D), D ** -0.5),
        "g_cross": gain(ks[11], (L, D)),
        "g_mem": gain(ks[12], (L, D)),
        "w_cq": nrm(ks[13], (L, D, D), D ** -0.5),
        "w_ckv": nrm(ks[14], (L, D, 2 * D), D ** -0.5),
        "w_co": nrm(ks[15], (L, D, D), D ** -0.5),
        "g_peer": gain(ks[16], (L, D)),
        "w_pq": nrm(ks[17], (L, D, PEER_HEADS * PEER_QDIM), D ** -0.5),
        "peer_subkeys": nrm(ks[18], (L, PEER_HEADS, 2, PEER_KEYS, PEER_QDIM // 2), (PEER_QDIM // 2) ** -0.5),
        "peer_u": nrm(ks[19], (L, PEER_EXPERTS, D), D ** -0.5),
        "peer_v": nrm(ks[20], (L, PEER_EXPERTS, D), PEER_HEADS ** -0.5),
        "g_final": gain(ks[21], (D,)),
    }

def first_block(x, mem, g_mix, w_in, gdn_conv, gdn_a_log, gdn_dt_bias, gdn_norm_g, w_sb_up, w_gdn_up,
              w_mix_out, g_cross, g_mem, w_cq, w_ckv, w_co, g_peer, w_pq, peer_subkeys, peer_u, peer_v,
              g_final):
    for l in range(DEPTH):
        x = x + token_mixer(rmsnorm(x, g_mix[l]), w_in[l], gdn_conv[l], gdn_a_log[l], gdn_dt_bias[l],
                            gdn_norm_g[l], w_sb_up[l], w_gdn_up[l], w_mix_out[l])
        x = x + memory_cross_attention(rmsnorm(x, g_cross[l]), rmsnorm(mem, g_mem[l]),
                                       w_cq[l], w_ckv[l], w_co[l])
        x = x + peer(rmsnorm(x, g_peer[l]), w_pq[l], peer_subkeys[l], peer_u[l], peer_v[l])
    return rmsnorm(x, g_final)


DEPTH_2 = 2

D_FF = 2816
NSA_HEADS = 8
NSA_KV_GROUPS = 2
HEAD_DIM = 64
NSA_WIDTH = NSA_HEADS * HEAD_DIM
KV_WIDTH = NSA_KV_GROUPS * HEAD_DIM
CMP_BLOCK = 32
CMP_STRIDE = 16
CMP_HIDDEN = 128
SLC_BLOCK = 64
RATIO = SLC_BLOCK // CMP_STRIDE
SLC_TOP_N = 16
WINDOW = 512
Q_BLOCK = 128
FORCE_BONUS = 1e4
CONV_WIDTH_2 = 512
CONV_K = 3
IN_SIZES = (NSA_WIDTH, 3 * NSA_HEADS, KV_WIDTH, KV_WIDTH, KV_WIDTH, KV_WIDTH,
            KV_WIDTH, KV_WIDTH, CONV_WIDTH_2, CONV_WIDTH_2, CONV_WIDTH_2)
IN_COLS_2 = sum(IN_SIZES)
IN_SPLITS = tuple(int(s) for s in np.cumsum(IN_SIZES)[:-1])
MIX_OUT = NSA_WIDTH + CONV_WIDTH_2
RWKV_HEAD = 64
RWKV_HEADS = D_MODEL // RWKV_HEAD
DECAY_LORA = 64
AAA_LORA = 64
GATE_LORA = 128
LNX_EPS = 64e-5


def rmsnorm_2(x, g):
    xf = x.astype(jnp.float32)
    y = xf * lax.rsqrt(jnp.mean(xf * xf, -1, keepdims=True) + EPS)
    return (y * g.astype(jnp.float32)).astype(x.dtype)

def macaron_half_ffn(x, pre_g, post_g, w_gate, w_up, w_down):
    h = rmsnorm_2(x, pre_g)
    h = (jax.nn.silu(h @ w_gate) * (h @ w_up)) @ w_down
    return x + 0.5 * rmsnorm_2(h, post_g)

def alibi_slopes(n):
    return 2.0 ** (-8.0 * jnp.arange(1, n + 1, dtype=jnp.float32) / n)

def masked_softmax(s, mask):
    s = jnp.where(mask, s.astype(jnp.float32), -jnp.inf)
    m = jnp.max(s, -1, keepdims=True)
    m = jnp.where(jnp.isfinite(m), m, 0.0)
    p = jnp.exp(s - m)
    return p / jnp.maximum(jnp.sum(p, -1, keepdims=True), 1e-30)

def compress_blocks(kv, pe, w1, w2):
    B, S, G, Dh = kv.shape
    halves = kv.reshape(B, S // CMP_STRIDE, CMP_STRIDE, G, Dh)
    blocks = jnp.concatenate([halves[:, :-1], halves[:, 1:]], axis=2)
    blocks = blocks + pe[None, None, :, None, :]
    nc = blocks.shape[1]
    flat = blocks.transpose(0, 1, 3, 2, 4).reshape(B, nc, G, CMP_BLOCK * Dh)
    return jax.nn.gelu(flat @ w1) @ w2

def nsa_attention(q, gates, kc, vc, k_slc, v_slc, k_win, v_win):
    B, S, H, Dh = q.shape
    G = kc.shape[2]
    R = H // G
    n_cmp = kc.shape[1]
    n_slc = S // SLC_BLOCK
    top_n = min(SLC_TOP_N, n_slc)
    slopes = alibi_slopes(H).reshape(G, R)
    cmp_end = jnp.arange(n_cmp) * CMP_STRIDE + (CMP_BLOCK - 1)
    qg = q.reshape(B, S, G, R, Dh) * (Dh ** -0.5)
    gg = gates.reshape(B, S, G, R, 3)
    kb = k_slc.reshape(B, n_slc, SLC_BLOCK, G, Dh).transpose(0, 3, 1, 2, 4)
    vb = v_slc.reshape(B, n_slc, SLC_BLOCK, G, Dh).transpose(0, 3, 1, 2, 4)
    gather = jax.vmap(jax.vmap(lambda blocks, ix: blocks[ix]))
    kw = jnp.pad(k_win, ((0, 0), (WINDOW, 0), (0, 0), (0, 0)))
    vw = jnp.pad(v_win, ((0, 0), (WINDOW, 0), (0, 0), (0, 0)))
    j = jnp.arange(n_slc)
    offs = jnp.arange(SLC_BLOCK)
    woffs = jnp.arange(Q_BLOCK + WINDOW) - WINDOW

    def query_block(qi):
        q0 = qi * Q_BLOCK
        t = q0 + jnp.arange(Q_BLOCK)
        qb = lax.dynamic_slice_in_dim(qg, q0, Q_BLOCK, axis=1)
        gb = lax.dynamic_slice_in_dim(gg, q0, Q_BLOCK, axis=1)
        d_cmp = t[:, None] - cmp_end[None, :]
        s = jnp.einsum("btgrd,bngd->bgrtn", qb, kc) - slopes[:, :, None, None] * d_cmp
        p_cmp = masked_softmax(s, d_cmp >= 0)
        o_cmp = jnp.einsum("bgrtn,bngd->btgrd", p_cmp.astype(vc.dtype), vc)
        imp = jnp.pad(p_cmp.sum(2), ((0, 0), (0, 0), (0, 0), (0, 1)))
        imp = imp.reshape(B, G, Q_BLOCK, n_slc, RATIO)
        last = imp[..., RATIO - 1]
        prev = jnp.pad(last, ((0, 0), (0, 0), (0, 0), (1, 0)))[..., :-1]
        imp = imp.sum(-1) - 0.5 * last + 0.5 * prev
        blk_t = (t // SLC_BLOCK)[:, None]
        forced = (j == 0) | (j == blk_t) | (j == blk_t - 1)
        imp = jnp.where(forced, imp + FORCE_BONUS, imp)
        imp = jnp.where(j <= blk_t, imp, -jnp.inf)
        _, idx = lax.top_k(imp, top_n)
        ks = gather(kb, idx)
        vs = gather(vb, idx)
        d_slc = t[:, None, None] - (idx[..., None] * SLC_BLOCK + offs)
        s = jnp.einsum("btgrd,bgtnld->bgrtnl", qb, ks) - slopes[:, :, None, None, None] * d_slc[:, :, None]
        mask = jnp.broadcast_to((d_slc >= 0)[:, :, None], s.shape)
        p = masked_softmax(s.reshape(B, G, R, Q_BLOCK, -1), mask.reshape(B, G, R, Q_BLOCK, -1))
        o_slc = jnp.einsum("bgrtm,bgtmd->btgrd", p.astype(vs.dtype),
                           vs.reshape(B, G, Q_BLOCK, top_n * SLC_BLOCK, Dh))
        kwb = lax.dynamic_slice_in_dim(kw, q0, Q_BLOCK + WINDOW, axis=1)
        vwb = lax.dynamic_slice_in_dim(vw, q0, Q_BLOCK + WINDOW, axis=1)
        kpos = q0 + woffs
        d_win = t[:, None] - kpos[None, :]
        mask = (d_win >= 0) & (d_win < WINDOW) & (kpos[None, :] >= 0)
        s = jnp.einsum("btgrd,bsgd->bgrts", qb, kwb) - slopes[:, :, None, None] * d_win
        p = masked_softmax(s, mask)
        o_win = jnp.einsum("bgrts,bsgd->btgrd", p.astype(vwb.dtype), vwb)
        return gb[..., 0:1] * o_cmp + gb[..., 1:2] * o_slc + gb[..., 2:3] * o_win

    out = lax.map(query_block, jnp.arange(S // Q_BLOCK))
    return out.transpose(1, 0, 2, 3, 4, 5).reshape(B, S, H * Dh)

def short_conv(b_gate, c_gate, u, conv_w, conv_b):
    z = c_gate * u
    y = lax.conv_general_dilated(z, conv_w[:, None, :].astype(z.dtype), window_strides=(1,),
                                 padding=[(CONV_K - 1, 0)],
                                 dimension_numbers=("NWC", "WIO", "NWC"),
                                 feature_group_count=z.shape[-1])
    return b_gate * (y + conv_b)

def nsa_shortconv_mixer(h, w_in, cmp_pe_k, cmp_w1_k, cmp_w2_k, cmp_pe_v, cmp_w1_v, cmp_w2_v,
                        conv_w, conv_b, w_out):
    B, S, _ = h.shape
    q, g, kc, vc, ks, vs, kw, vw, cb, cc, cu = jnp.split(h @ w_in, IN_SPLITS, axis=-1)
    kv = lambda t: t.reshape(B, S, NSA_KV_GROUPS, HEAD_DIM)
    kc = compress_blocks(kv(kc), cmp_pe_k, cmp_w1_k, cmp_w2_k)
    vc = compress_blocks(kv(vc), cmp_pe_v, cmp_w1_v, cmp_w2_v)
    o_nsa = nsa_attention(q.reshape(B, S, NSA_HEADS, HEAD_DIM),
                          jax.nn.sigmoid(g).reshape(B, S, NSA_HEADS, 3),
                          kc, vc, kv(ks), kv(vs), kv(kw), kv(vw))
    o_conv = short_conv(cb, cc, cu, conv_w, conv_b)
    return jnp.concatenate([o_nsa.astype(h.dtype), o_conv], axis=-1) @ w_out

def rwkv7_mixer(h, mu, w_r, w_k, w_v, w_o, w0, w_dec1, w_dec2, a0, w_a1, w_a2,
                w_g1, w_g2, k_k, k_a, r_k, lnx_g, lnx_b):
    B, S, D = h.shape
    H, N = RWKV_HEADS, RWKV_HEAD
    xx = jnp.pad(h, ((0, 0), (1, 0), (0, 0)))[:, :-1] - h
    xr, xw, xk, xv, xa, xg = [h + xx * mu[i] for i in range(6)]
    r = xr @ w_r
    k = xk @ w_k
    v = xv @ w_v
    w_log = -jax.nn.softplus(-(w0 + jnp.tanh(xw @ w_dec1) @ w_dec2)) - 0.5
    a = jax.nn.sigmoid(a0 + (xa @ w_a1) @ w_a2)
    g = jax.nn.sigmoid(xg @ w_g1) @ w_g2
    kk = (k * k_k).reshape(B, S, H, N).astype(jnp.float32)
    kk = kk * lax.rsqrt(jnp.maximum(jnp.sum(kk * kk, -1, keepdims=True), 1e-12))
    k = k * (1.0 + (a - 1.0) * k_a)
    decay = jnp.exp(-jnp.exp(w_log.astype(jnp.float32)))
    heads = lambda t: t.reshape(B, S, H, N).astype(jnp.float32).transpose(1, 0, 2, 3)
    xs = (heads(r), heads(decay), heads(k), heads(v), kk.transpose(1, 0, 2, 3), heads(a))

    def step(state, inp):
        r_t, w_t, k_t, v_t, kk_t, a_t = inp
        sa = jnp.einsum("bhij,bhj->bhi", state, -kk_t)
        state = (state * w_t[:, :, None, :] + sa[..., None] * (kk_t * a_t)[:, :, None, :]
                 + v_t[..., None] * k_t[:, :, None, :])
        return state, jnp.einsum("bhij,bhj->bhi", state, r_t)

    state0 = jnp.zeros((B, H, N, N), jnp.float32)
    _, y = lax.scan(step, state0, xs)
    y = y.transpose(1, 0, 2, 3)
    mean = jnp.mean(y, -1, keepdims=True)
    var = jnp.mean(jnp.square(y - mean), -1, keepdims=True)
    y = ((y - mean) * lax.rsqrt(var + LNX_EPS)).reshape(B, S, D) * lnx_g + lnx_b
    rh, kh, vh = (t.reshape(B, S, H, N).astype(jnp.float32) for t in (r, k, v))
    bonus = (jnp.sum(rh * kh * r_k, -1, keepdims=True) * vh).reshape(B, S, D)
    return ((y + bonus).astype(h.dtype) * g) @ w_o

def second_inputs(seed: int = 0) -> dict:
    key = jax.random.key(seed)
    keys = iter(jax.random.split(key, 80))

    def nrm(shape, scale):
        return jax.random.normal(next(keys), shape, jnp.float32) * scale

    def unif(shape, lo, hi):
        return jax.random.uniform(next(keys), shape, jnp.float32, lo, hi)

    def gain(n=D_MODEL):
        return 1.0 + nrm((n,), 0.05)

    inp = {"x": nrm((BATCH, SEQ, D_MODEL), 1.0)}

    def add_ffn(p):
        inp[p + "_pre_g"] = gain()
        inp[p + "_post_g"] = gain()
        inp[p + "_w_gate"] = nrm((D_MODEL, D_FF), D_MODEL ** -0.5)
        inp[p + "_w_up"] = nrm((D_MODEL, D_FF), D_MODEL ** -0.5)
        inp[p + "_w_down"] = nrm((D_FF, D_MODEL), D_FF ** -0.5)

    add_ffn("l0_ffn1")
    inp["l0_mix_pre_g"] = gain()
    inp["l0_mix_post_g"] = gain()
    inp["l0_w_in"] = nrm((D_MODEL, IN_COLS_2), D_MODEL ** -0.5)
    for kvn in ("k", "v"):
        inp["l0_cmp_pe_" + kvn] = nrm((CMP_BLOCK, HEAD_DIM), 0.1)
        inp["l0_cmp_w1_" + kvn] = nrm((CMP_BLOCK * HEAD_DIM, CMP_HIDDEN), (CMP_BLOCK * HEAD_DIM) ** -0.5)
        inp["l0_cmp_w2_" + kvn] = nrm((CMP_HIDDEN, HEAD_DIM), CMP_HIDDEN ** -0.5)
    inp["l0_conv_w"] = nrm((CONV_K, CONV_WIDTH_2), 0.5)
    inp["l0_conv_b"] = nrm((CONV_WIDTH_2,), 0.02)
    inp["l0_w_out"] = nrm((MIX_OUT, D_MODEL), MIX_OUT ** -0.5)
    add_ffn("l0_ffn2")
    add_ffn("l1_ffn1")
    inp["l1_mix_pre_g"] = gain()
    inp["l1_mix_post_g"] = gain()
    inp["l1_mu"] = unif((6, D_MODEL), 0.0, 1.0)
    inp["l1_w_r"] = nrm((D_MODEL, D_MODEL), D_MODEL ** -0.5)
    inp["l1_w_k"] = nrm((D_MODEL, D_MODEL), D_MODEL ** -0.5)
    inp["l1_w_v"] = nrm((D_MODEL, D_MODEL), D_MODEL ** -0.5)
    inp["l1_w_o"] = nrm((D_MODEL, D_MODEL), D_MODEL ** -0.5)
    inp["l1_w0"] = unif((D_MODEL,), -6.0, 1.0)
    inp["l1_w_dec1"] = nrm((D_MODEL, DECAY_LORA), D_MODEL ** -0.5)
    inp["l1_w_dec2"] = nrm((DECAY_LORA, D_MODEL), 0.1 * DECAY_LORA ** -0.5)
    inp["l1_a0"] = nrm((D_MODEL,), 0.5)
    inp["l1_w_a1"] = nrm((D_MODEL, AAA_LORA), D_MODEL ** -0.5)
    inp["l1_w_a2"] = nrm((AAA_LORA, D_MODEL), 0.5 * AAA_LORA ** -0.5)
    inp["l1_w_g1"] = nrm((D_MODEL, GATE_LORA), D_MODEL ** -0.5)
    inp["l1_w_g2"] = nrm((GATE_LORA, D_MODEL), GATE_LORA ** -0.5)
    inp["l1_k_k"] = 0.85 + nrm((D_MODEL,), 0.05)
    inp["l1_k_a"] = 1.0 + nrm((D_MODEL,), 0.05)
    inp["l1_r_k"] = nrm((RWKV_HEADS, RWKV_HEAD), 0.1)
    inp["l1_lnx_g"] = gain()
    inp["l1_lnx_b"] = nrm((D_MODEL,), 0.02)
    add_ffn("l1_ffn2")
    return inp

def second_block(x,
              l0_ffn1_pre_g, l0_ffn1_post_g, l0_ffn1_w_gate, l0_ffn1_w_up, l0_ffn1_w_down,
              l0_mix_pre_g, l0_mix_post_g, l0_w_in,
              l0_cmp_pe_k, l0_cmp_w1_k, l0_cmp_w2_k, l0_cmp_pe_v, l0_cmp_w1_v, l0_cmp_w2_v,
              l0_conv_w, l0_conv_b, l0_w_out,
              l0_ffn2_pre_g, l0_ffn2_post_g, l0_ffn2_w_gate, l0_ffn2_w_up, l0_ffn2_w_down,
              l1_ffn1_pre_g, l1_ffn1_post_g, l1_ffn1_w_gate, l1_ffn1_w_up, l1_ffn1_w_down,
              l1_mix_pre_g, l1_mix_post_g, l1_mu, l1_w_r, l1_w_k, l1_w_v, l1_w_o,
              l1_w0, l1_w_dec1, l1_w_dec2, l1_a0, l1_w_a1, l1_w_a2, l1_w_g1, l1_w_g2,
              l1_k_k, l1_k_a, l1_r_k, l1_lnx_g, l1_lnx_b,
              l1_ffn2_pre_g, l1_ffn2_post_g, l1_ffn2_w_gate, l1_ffn2_w_up, l1_ffn2_w_down):
    layers = [
        dict(ffn1=(l0_ffn1_pre_g, l0_ffn1_post_g, l0_ffn1_w_gate, l0_ffn1_w_up, l0_ffn1_w_down),
             norms=(l0_mix_pre_g, l0_mix_post_g),
             mixer=nsa_shortconv_mixer,
             mix=(l0_w_in, l0_cmp_pe_k, l0_cmp_w1_k, l0_cmp_w2_k, l0_cmp_pe_v, l0_cmp_w1_v,
                  l0_cmp_w2_v, l0_conv_w, l0_conv_b, l0_w_out),
             ffn2=(l0_ffn2_pre_g, l0_ffn2_post_g, l0_ffn2_w_gate, l0_ffn2_w_up, l0_ffn2_w_down)),
        dict(ffn1=(l1_ffn1_pre_g, l1_ffn1_post_g, l1_ffn1_w_gate, l1_ffn1_w_up, l1_ffn1_w_down),
             norms=(l1_mix_pre_g, l1_mix_post_g),
             mixer=rwkv7_mixer,
             mix=(l1_mu, l1_w_r, l1_w_k, l1_w_v, l1_w_o, l1_w0, l1_w_dec1, l1_w_dec2, l1_a0,
                  l1_w_a1, l1_w_a2, l1_w_g1, l1_w_g2, l1_k_k, l1_k_a, l1_r_k, l1_lnx_g, l1_lnx_b),
             ffn2=(l1_ffn2_pre_g, l1_ffn2_post_g, l1_ffn2_w_gate, l1_ffn2_w_up, l1_ffn2_w_down)),
    ]
    for i in range(DEPTH_2):
        p = layers[i]
        x = macaron_half_ffn(x, *p["ffn1"])
        pre_g, post_g = p["norms"]
        x = x + rmsnorm_2(p["mixer"](rmsnorm_2(x, pre_g), *p["mix"]), post_g)
        x = macaron_half_ffn(x, *p["ffn2"])
    return x


def setup_inputs(seed=0):
    out = dict(first_inputs(seed))
    for name, value in second_inputs(seed + 1).items():
        if name != "x":
            out[name + "_2"] = value
    return out


def reference(
    x, mem, g_mix, w_in, gdn_conv, gdn_a_log, gdn_dt_bias, gdn_norm_g, w_sb_up, w_gdn_up,
    w_mix_out, g_cross, g_mem, w_cq, w_ckv, w_co, g_peer, w_pq, peer_subkeys, peer_u, peer_v,
    g_final, l0_ffn1_pre_g_2, l0_ffn1_post_g_2, l0_ffn1_w_gate_2, l0_ffn1_w_up_2,
    l0_ffn1_w_down_2, l0_mix_pre_g_2, l0_mix_post_g_2, l0_w_in_2, l0_cmp_pe_k_2, l0_cmp_w1_k_2,
    l0_cmp_w2_k_2, l0_cmp_pe_v_2, l0_cmp_w1_v_2, l0_cmp_w2_v_2, l0_conv_w_2, l0_conv_b_2,
    l0_w_out_2, l0_ffn2_pre_g_2, l0_ffn2_post_g_2, l0_ffn2_w_gate_2, l0_ffn2_w_up_2,
    l0_ffn2_w_down_2, l1_ffn1_pre_g_2, l1_ffn1_post_g_2, l1_ffn1_w_gate_2, l1_ffn1_w_up_2,
    l1_ffn1_w_down_2, l1_mix_pre_g_2, l1_mix_post_g_2, l1_mu_2, l1_w_r_2, l1_w_k_2, l1_w_v_2,
    l1_w_o_2, l1_w0_2, l1_w_dec1_2, l1_w_dec2_2, l1_a0_2, l1_w_a1_2, l1_w_a2_2, l1_w_g1_2,
    l1_w_g2_2, l1_k_k_2, l1_k_a_2, l1_r_k_2, l1_lnx_g_2, l1_lnx_b_2, l1_ffn2_pre_g_2,
    l1_ffn2_post_g_2, l1_ffn2_w_gate_2, l1_ffn2_w_up_2, l1_ffn2_w_down_2,
):
    x = first_block(
        x, mem, g_mix, w_in, gdn_conv, gdn_a_log, gdn_dt_bias, gdn_norm_g, w_sb_up, w_gdn_up,
        w_mix_out, g_cross, g_mem, w_cq, w_ckv, w_co, g_peer, w_pq, peer_subkeys, peer_u,
        peer_v, g_final,
    )
    return second_block(
        x, l0_ffn1_pre_g_2, l0_ffn1_post_g_2, l0_ffn1_w_gate_2, l0_ffn1_w_up_2,
        l0_ffn1_w_down_2, l0_mix_pre_g_2, l0_mix_post_g_2, l0_w_in_2, l0_cmp_pe_k_2,
        l0_cmp_w1_k_2, l0_cmp_w2_k_2, l0_cmp_pe_v_2, l0_cmp_w1_v_2, l0_cmp_w2_v_2, l0_conv_w_2,
        l0_conv_b_2, l0_w_out_2, l0_ffn2_pre_g_2, l0_ffn2_post_g_2, l0_ffn2_w_gate_2,
        l0_ffn2_w_up_2, l0_ffn2_w_down_2, l1_ffn1_pre_g_2, l1_ffn1_post_g_2, l1_ffn1_w_gate_2,
        l1_ffn1_w_up_2, l1_ffn1_w_down_2, l1_mix_pre_g_2, l1_mix_post_g_2, l1_mu_2, l1_w_r_2,
        l1_w_k_2, l1_w_v_2, l1_w_o_2, l1_w0_2, l1_w_dec1_2, l1_w_dec2_2, l1_a0_2, l1_w_a1_2,
        l1_w_a2_2, l1_w_g1_2, l1_w_g2_2, l1_k_k_2, l1_k_a_2, l1_r_k_2, l1_lnx_g_2, l1_lnx_b_2,
        l1_ffn2_pre_g_2, l1_ffn2_post_g_2, l1_ffn2_w_gate_2, l1_ffn2_w_up_2, l1_ffn2_w_down_2,
    )


_drawn_inputs = setup_inputs


def setup_inputs(seed=0):
    import zlib

    import numpy as np

    out = dict(_drawn_inputs(seed))
    spreads = {}
    factors = {'g_cross': 3.41,
     'l0_cmp_pe_k_2': 8.0,
     'l1_ffn1_post_g_2': 2.889,
     'l1_w_dec1_2': 8.0,
     'l1_w_dec2_2': 8.0,
     'l1_k_k_2': 2.915,
     'l1_lnx_b_2': 5.228,
     'l1_ffn2_pre_g_2': 3.286,
     'l1_ffn2_post_g_2': 4.484}
    for name, (base, spread) in spreads.items():
        noise = np.random.default_rng([zlib.crc32(name.encode()), seed]).standard_normal(out[name].shape)
        drawn = base * np.exp(spread * noise) if base else spread * noise
        out[name] = __import__('jax').numpy.asarray(drawn.astype(out[name].dtype))
    for name, factor in factors.items():
        out[name] = (out[name] * factor).astype(out[name].dtype)
    return out
```

```python
from contextlib import ExitStack

import numpy as np

import concourse.bass as bass
from concourse import mybir

F32 = mybir.dt.float32
U32 = mybir.dt.uint32
ACT = mybir.ActivationFunctionType
ALU = mybir.AluOpType
AX = mybir.AxisListType

P = 128
D = 1024
T = 256
KT = D // P
TB = T // P
EPS = 1e-6

SB_HEADS, SB_DIM = 8, 64
GDN_HEADS, GDN_DIM = 4, 128
CONV_TAPS = 4
X_HEADS, X_DIM = 4, 256
PEER_HEADS, PEER_KEYS, TOPK = 8, 128, 16
EXPERTS = PEER_KEYS * PEER_KEYS
SLOTS = PEER_HEADS * TOPK

D_FF = 2816
FT = D_FF // P
NSA_HEADS, NSA_GROUPS, NSA_DIM = 8, 2, 64
NSA_REP = NSA_HEADS // NSA_GROUPS
CMP_BLOCK, CMP_STRIDE = 32, 16
N_CMP = (T - CMP_BLOCK) // CMP_STRIDE + 1
CONV2_TAPS = 3
RW_HEADS, RW_DIM = 16, 64
LORA, GATE_LORA = 64, 128
LNX_EPS = 64e-5
NEG = -1e30
CLAMP = -1e20

RING = 10
CHUNK = 8 * P
LEVELS = 7
GATHER_RING = 8

CONST_TILES = ["ones", "identity", "head_ones", "upto", "neg_suffix", "neg_ones", "strict",
               "negated_strict"] + [f"level{i}" for i in range(LEVELS)]
CONST_ROWS = CONST_TILES + ["causal0", "causal1a", "causal1b", "misc"]

COLUMNS = [("g_mix", 8), ("g_cross", 8), ("g_mem", 8), ("g_peer", 8), ("g_final", 8),
           ("gdn_norm_g", 1), ("gdn_conv", 12 * CONV_TAPS)]
for _l in ("l0", "l1"):
    for _f in ("ffn1", "ffn2", "mix"):
        COLUMNS += [(f"{_l}_{_f}_pre_g_2", 8), (f"{_l}_{_f}_post_g_2", 8)]
COLUMNS += [("l1_mu_2", 48), ("l1_w0_2", 8), ("l1_a0_2", 8), ("l1_k_k_2", 8), ("l1_k_a_2", 8),
            ("l1_r_k_2", 8), ("l1_lnx_g_2", 8), ("l1_lnx_b_2", 8),
            ("l0_conv_w_2", 4 * CONV2_TAPS), ("l0_conv_b_2", 4)]
COLUMN_AT = {}
for _n, _c in COLUMNS:
    COLUMN_AT[_n] = (sum(c for _, c in COLUMNS[:len(COLUMN_AT)]), _c)
N_COLUMNS = sum(c for _, c in COLUMNS)

STREAM = [("w_in", 44), ("w_up_pair", 8), ("w_mix_out", 8), ("w_cq", 8), ("w_ckv", 16),
          ("w_co", 8), ("w_pq", 16), ("subkeys", 2), ("l0_ffn1", 3 * FT), ("l0_in", 22),
          ("l0_out", 8), ("l0_ffn2", 3 * FT), ("l1_ffn1", 3 * FT), ("l1_rkv", 24),
          ("l1_o", 8), ("l1_ffn2", 3 * FT)]


def const_tiles():
    s, t = np.arange(P)[:, None], np.arange(P)[None, :]
    tiles = {
        "ones": np.ones((P, P)), "identity": s == t, "head_ones": s // 64 == t // 64,
        "upto": s <= t, "neg_suffix": -1.0 * (s >= t), "neg_ones": -np.ones((P, P)),
        "strict": s < t, "negated_strict": -1.0 * (s < t),
        "causal0": np.where(t <= s, t - s, NEG),
        "causal1a": t - (P + s) + 0.0,
        "causal1b": np.where(t <= s, t - s, NEG),
    }
    for i in range(LEVELS):
        b = 1 << i
        tiles[f"level{i}"] = (s // (2 * b) == t // (2 * b)) & ((s // b) % 2 == 0) & ((t // b) % 2 == 1)
    misc = np.zeros((P, P))
    for tb in range(TB):
        ends = np.arange(N_CMP) * CMP_STRIDE + CMP_BLOCK - 1
        far = tb * P + np.arange(P)[:, None] - ends[None, :]
        misc[:, N_CMP * tb:N_CMP * (tb + 1)] = np.where(far >= 0, -far, NEG)
    misc[:, 32:48] = np.arange(16)[None, :]
    tiles["misc"] = misc
    return np.stack([np.asarray(tiles[n], np.float32) for n in CONST_ROWS], axis=1)


class Signals:

    def __init__(self, bank):
        self.bank, self.names = bank, {}

    def __getitem__(self, name):
        if name not in self.names:
            self.names[name] = self.bank[len(self.names)]
        return self.names[name]


class Steps:

    def __init__(self, engine, semaphore):
        self.engine, self.semaphore, self.count = engine, semaphore, 0

    def did(self, instruction):
        instruction.then_inc(self.semaphore, 1)
        self.count += 1

    def settle(self):
        self.engine.wait_ge(self.semaphore, self.count)


class Weights:

    def __init__(self, nc, ctx, dram):
        self.ring = ctx.enter_context(nc.sbuf_tensor("weight_ring", [P, RING, CHUNK], F32))
        self.filled = [ctx.enter_context(nc.semaphore(f"weights_filled{i}")) for i in range(RING)]
        self.used = ctx.enter_context(nc.semaphore("weights_used"))
        self.plan = [dram[name][c] for name, n in STREAM for c in range(n)]
        self.loaded = self.taken = 0

    def load_ahead(self, sp, first, count):
        for c in range(self.loaded, min(first + count + RING, len(self.plan))):
            if c >= RING:
                sp.wait_ge(self.used, c - RING + 1)
            sp.dma_start(self.ring[:, c % RING, :], self.plan[c]).then_inc(self.filled[c % RING], 16)
            self.loaded = c + 1

    def arrived(self, pe):
        c = self.taken
        self.taken += 1
        pe.wait_ge(self.filled[c % RING], 16 * (c // RING + 1))
        return self.ring[:, c % RING, :].rearrange("p (k n) -> p k n", n=P)


class Kernel:

    def __init__(self, nc, ctx, dram):
        self.nc, self.ctx, self.dram = nc, ctx, dram
        self.banks = [[ctx.enter_context(nc.semaphore(f"stage{b}_{i}")) for i in range(56)]
                      for b in range(2)]
        self.stage_number, self.previous, self.tensors = 0, None, 0
        self.output_stored = ctx.enter_context(nc.semaphore("output_stored"))
        self.rows_ready = [ctx.enter_context(nc.semaphore(f"rows_ready{i}")) for i in range(GATHER_RING)]
        self.w = Weights(nc, ctx, dram)
        self.ps = ctx.enter_context(nc.psum_tensor("ps", [P, 8, 512], F32))
        self.consts = self.sbuf(ctx, "consts", len(CONST_ROWS), P)
        self.columns = self.sbuf(ctx, "columns", N_COLUMNS)
        self.x = self.sbuf(ctx, "x_residual", KT, T)
        self.xn = self.sbuf(ctx, "x_normed", KT, T)

    def sbuf(self, ctx, name, *shape, dtype=F32):
        self.tensors += 1
        return ctx.enter_context(self.nc.sbuf_tensor(f"{name}_{self.tensors}", [P, *shape], dtype))

    def const(self, name):
        return self.consts[:, CONST_ROWS.index(name), :]

    def column(self, name, tile):
        at, _ = COLUMN_AT[name]
        return self.columns[:, at + tile:at + tile + 1]

    def stage(self):
        signals = Signals(self.banks[self.stage_number % 2])
        stale, self.previous = self.previous, signals
        self.stage_number += 1
        return signals, (stale.names.values() if stale else [])


def clear(sp, stale):
    for s in stale:
        sp.sem_clear(s)


def over(ap, n):
    return ap.unsqueeze(1).broadcast_to([ap.shape[0], n, ap.shape[1]])


def load_constants(k):
    S, stale = k.stage()
    with k.nc.Block() as block:
        @block.sync
        def _(sp):
            sp.dma_start(k.x[:, :, :], k.dram["x"]).then_inc(S["loads"], 16)
            sp.dma_start(k.consts[:, :, :], k.dram["consts"]).then_inc(S["loads"], 16)
            sp.dma_start(k.columns[:, :], k.dram["columns"]).then_inc(S["loads"], 16)
            k.w.load_ahead(sp, 0, 0)
            sp.wait_ge(S["loads"], 48)


def rmsnorm(k, src, gain, dst, residual=False):
    S, stale = k.stage()
    with ExitStack() as ctx:
        squares = k.sbuf(ctx, "squares", KT, T)
        scale = k.sbuf(ctx, "scale", 2, T)
        with k.nc.Block() as block:
            @block.sync
            def _(sp):
                clear(sp, stale)

            @block.scalar
            def _(act):
                for half in range(2):
                    part = slice(4 * half, 4 * half + 4)
                    act.activation(squares[:, part, :], src[:, part, :], ACT.Square)\
                       .then_inc(S["squares_ready"], 1)
                act.wait_ge(S["mean_ready"], 1)
                act.activation(scale[:, 1, :], scale[:, 0, :], ACT.Sqrt).then_inc(S["root_ready"], 1)

            @block.tensor
            def _(pe):
                for t in range(KT):
                    if t % 4 == 0:
                        pe.wait_ge(S["squares_ready"], t // 4 + 1)
                    last = pe.matmul(k.ps[:, 7, 0:T], k.const("ones"), squares[:, t, :],
                                     start=t == 0, stop=t == KT - 1)
                last.then_inc(S["sum_ready"], 1)

            @block.vector
            def _(v):
                own = Steps(v, S["vector_steps"])
                v.wait_ge(S["sum_ready"], 1)
                v.tensor_scalar(scale[:, 0, :], k.ps[:, 7, 0:T], 1.0 / D, EPS, ALU.mult, ALU.add)\
                 .then_inc(S["mean_ready"], 1)
                v.wait_ge(S["root_ready"], 1)
                own.did(v.reciprocal(scale[:, 0, :], scale[:, 1, :]))
                own.settle()
                if residual:
                    if residual != 1:
                        own.did(v.tensor_scalar(scale[:, 0, :], scale[:, 0, :], residual, None, ALU.mult))
                        own.settle()
                    own.did(v.tensor_tensor(squares[:, :, :], src[:, :, :], over(scale[:, 0, :], KT),
                                            ALU.mult))
                    own.settle()
                    for t in range(KT):
                        v.scalar_tensor_tensor(dst[:, t, :], squares[:, t, :], k.column(gain, t),
                                               dst[:, t, :], ALU.mult, ALU.add)
                else:
                    for t in range(KT):
                        v.scalar_tensor_tensor(dst[:, t, :], src[:, t, :], k.column(gain, t),
                                               scale[:, 0, :], ALU.mult, ALU.mult)


def project(k, pe, S, count, moving, drained, banks=4, name=""):
    for i in range(count):
        if i >= banks:
            pe.wait_ge(drained, i - banks + 1)
        tiles = k.w.arrived(pe)
        for t in range(KT):
            last = pe.matmul(k.ps[:, i % banks, 0:T], tiles[:, t, :], moving[:, t, :],
                             start=t == 0, stop=t == KT - 1)
        last.then_inc(k.w.used, 1)


def project_residual(k, moving):
    S, stale = k.stage()
    first = k.w.taken
    with k.nc.Block() as block:
        @block.sync
        def _(sp):
            clear(sp, stale)
            k.w.load_ahead(sp, first, KT)

        @block.tensor
        def _(pe):
            project(k, pe, S, KT, moving, S["tile_added"])

        @block.vector
        def _(v):
            for i in range(KT):
                v.wait_ge(k.w.used, first + i + 1)
                v.tensor_tensor(k.x[:, i, :], k.x[:, i, :], k.ps[:, i % 4, 0:T], ALU.add)\
                 .then_inc(S["tile_added"], 1)


def project_in(k, m):
    S, stale = k.stage()
    first = k.w.taken
    n_copy, n_tok, n_silu, n_gate = 20, 4, 4, 16
    with k.nc.Block() as block:
        @block.sync
        def _(sp):
            clear(sp, stale)
            sp.dma_start(m["w_ba"][:, :, :], k.dram["w_ba"]).then_inc(S["small_loaded"], 16)
            sp.dma_start(m["rows"][:, :], k.dram["gdn_rows"]).then_inc(S["small_loaded"], 16)
            k.w.load_ahead(sp, first, 44)

        @block.tensor
        def _(pe):
            pe.wait_ge(S["small_loaded"], 32)
            for tb in range(TB):
                for t in range(KT):
                    last = pe.matmul(k.ps[:, 6, 8 * tb:8 * tb + 8], k.xn[:, t, P * tb:P * tb + P],
                                     m["w_ba"][:, t, :], start=t == 0, stop=t == KT - 1)
            last.then_inc(S["ba_ready"], 1)
            for i in range(44):
                if i >= 4:
                    if i - 4 < n_copy + n_tok:
                        pe.wait_ge(S["copied"], i - 3)
                    else:
                        pe.wait_ge(S["activated"], i - 3 - n_copy - n_tok)
                tiles = k.w.arrived(pe)
                if n_copy <= i < n_copy + n_tok:
                    for tb in range(TB):
                        for t in range(KT):
                            last = pe.matmul(k.ps[:, i % 4, P * tb:P * tb + P],
                                             k.xn[:, t, P * tb:P * tb + P], tiles[:, t, :],
                                             start=t == 0, stop=t == KT - 1)
                else:
                    for t in range(KT):
                        last = pe.matmul(k.ps[:, i % 4, 0:T], tiles[:, t, :], k.xn[:, t, :],
                                         start=t == 0, stop=t == KT - 1)
                last.then_inc(k.w.used, 1)

        @block.vector
        def _(v):
            own = Steps(v, S["vector_steps"])
            pad = CONV_TAPS - 1
            v.memset(m["conv_in"][:, :, 0:pad], 0.0)
            b, a = m["beta"], m["decay"]
            v.wait_ge(S["ba_ready"], 1)
            ba = k.ps[:, 6, 0:16].rearrange("p (b c) -> p b c", b=TB)
            v.tensor_copy(b[:, :, :], ba[:, :, 0:4]).then_inc(S["beta_in"], 1)
            own.did(v.tensor_tensor(a[:, 0], ba[:, :, 4:8], over(m["rows"][:, 4:8], TB), ALU.add))
            own.settle()
            own.did(v.tensor_scalar(a[:, 1], a[:, 0], -1.0, None, ALU.mult))
            own.settle()
            v.tensor_tensor(a[:, 2], a[:, 0], a[:, 1], ALU.min).then_inc(S["minus_abs"], 1)
            for i in range(n_copy + n_tok):
                v.wait_ge(k.w.used, first + i + 1)
                if i < 12:
                    out = m["conv_in"][:, i, pad:pad + T]
                elif i < n_copy:
                    out = m["sb_qk"][:, i - 12, :]
                else:
                    c = i - n_copy
                    out = m["sb_v"][:, :, P * c:P * c + P]
                src = k.ps[:, i % 4, 0:T]
                if i >= n_copy:
                    src = src.rearrange("p (b n) -> p b n", b=TB)
                v.tensor_copy(out, src).then_inc(S["copied"], 1)
            v.wait_ge(S["softplus_log"], 1)
            own.did(v.scalar_tensor_tensor(a[:, 0], a[:, 0], 0.0, a[:, 2], ALU.max, ALU.add))
            own.settle()
            own.did(v.scalar_tensor_tensor(a[:, 1], a[:, 0], -1.0, over(m["rows"][:, 0:4], TB),
                                           ALU.mult, ALU.mult))

        @block.scalar
        def _(act):
            a = m["decay"]
            act.wait_ge(S["small_loaded"], 32)
            act.activation(m["rows"][:, 0:4], m["rows"][:, 0:4], ACT.Exp)
            act.wait_ge(S["minus_abs"], 1)
            act.activation(a[:, 2], a[:, 2], ACT.Exp).then_inc(S["softplus_exp"], 1)
            act.wait_ge(S["softplus_exp"], 1)
            act.activation(a[:, 2], a[:, 2], ACT.Ln, bias=1.0).then_inc(S["softplus_log"], 1)
            for i in range(n_copy + n_tok, n_copy + n_tok + n_silu):
                act.wait_ge(k.w.used, first + i + 1)
                act.activation(m["z"][:, i - n_copy - n_tok, :], k.ps[:, i % 4, 0:T], ACT.Silu)\
                   .then_inc(S["activated"], 1)
            act.wait_ge(S["beta_in"], 1)
            act.activation(m["beta"][:, :, :], m["beta"][:, :, :], ACT.Sigmoid)
            for i in range(28, 28 + n_gate):
                act.wait_ge(k.w.used, first + i + 1)
                act.activation(m["gates"][:, i - 28, :], k.ps[:, i % 4, 0:T], ACT.Sigmoid)\
                   .then_inc(S["activated"], 1)


def stick_breaking(k, m):
    S, stale = k.stage()
    H, SEG = SB_HEADS, 3 * P
    with ExitStack() as ctx:
        z = k.sbuf(ctx, "z_scaled", H, SEG)
        w = k.sbuf(ctx, "softplus", H, SEG)
        a = k.sbuf(ctx, "weights", H, SEG)
        mask = k.sbuf(ctx, "segment_mask", SEG)

        def half(h):
            return slice(64 * (h % 2), 64 * (h % 2) + 64)

        with k.nc.Block() as block:
            @block.sync
            def _(sp):
                clear(sp, stale)

            @block.tensor
            def _(pe):
                for h in range(H):
                    if h >= 2:
                        pe.wait_ge(S["z_out"], h - 1)
                    q, kk = m["sb_qk"][half(h), h // 2, :], m["sb_qk"][half(h), 4 + h // 2, :]
                    pe.matmul(k.ps[:, h % 2, 0:T], kk[:, 0:P], q, start=True, stop=True)
                    pe.matmul(k.ps[:, h % 2, T:SEG], kk[:, P:T], q[:, P:T], start=True, stop=True)\
                      .then_inc(S["z_ready"], 1)
                for h in range(H):
                    pe.wait_ge(S["softplus_ready"], h + 1)
                    if h >= 2:
                        pe.wait_ge(S["logs_ready"], h - 1)
                    r = k.ps[:, 2 + h % 2, :]
                    pe.matmul(r[:, 0:P], k.const("neg_suffix"), w[:, h, 0:P], start=True, stop=True)
                    pe.matmul(r[:, P:T], k.const("neg_suffix"), w[:, h, P:T], start=True, stop=False)
                    pe.matmul(r[:, P:T], k.const("neg_ones"), w[:, h, T:SEG], start=False, stop=True)
                    pe.matmul(r[:, T:SEG], k.const("neg_suffix"), w[:, h, T:SEG], start=True, stop=True)\
                      .then_inc(S["sums_ready"], 1)
                for h in range(H):
                    pe.wait_ge(S["weights_ready"], h + 1)
                    if h >= 2:
                        pe.wait_ge(S["head_out"], h - 1)
                    o = k.ps[half(h), 4 + h % 2, :]
                    v0, v1 = (m["sb_v"][:, b, 64 * h:64 * h + 64] for b in range(TB))
                    pe.matmul(o[:, 0:P], v0, a[:, h, 0:P], start=True, stop=True)
                    pe.matmul(o[:, P:T], v0, a[:, h, P:T], start=True, stop=False)
                    pe.matmul(o[:, P:T], v1, a[:, h, T:SEG], start=False, stop=True)\
                      .then_inc(S["output_ready"], 1)

            @block.scalar
            def _(act):
                for h in range(H):
                    act.wait_ge(S["z_ready"], h + 1)
                    act.activation(z[:, h, :], k.ps[:, h % 2, 0:SEG], ACT.Copy, scale=SB_DIM ** -0.5)\
                       .then_inc(S["z_out"], 1)
                for h in range(H):
                    act.wait_ge(S["minus_abs"], h + 1)
                    act.activation(w[:, h, :], w[:, h, :], ACT.Exp).then_inc(S["exps"], 1)
                for h in range(H):
                    act.wait_ge(S["exps"], h + 1)
                    act.activation(w[:, h, :], w[:, h, :], ACT.Ln, bias=1.0).then_inc(S["log_ready"], 1)
                for h in range(H):
                    act.wait_ge(S["logs_ready"], h + 1)
                    act.activation(a[:, h, :], a[:, h, :], ACT.Exp).then_inc(S["exp_ready"], 1)
                for h in range(H):
                    act.wait_ge(S["output_ready"], h + 1)
                    act.activation(m["o_sb"][half(h), h // 2, :], k.ps[half(h), 4 + h % 2, 0:T], ACT.Copy)\
                       .then_inc(S["head_out"], 1)

            @block.vector
            def _(v):
                own = Steps(v, S["vector_steps"])
                own.did(v.tensor_copy(mask[:, 0:P], k.const("strict")))
                own.did(v.tensor_copy(mask[:, P:T], k.const("ones")))
                own.did(v.tensor_copy(mask[:, T:SEG], k.const("strict")))
                for h in range(H):
                    v.wait_ge(S["z_out"], h + 1)
                    own.did(v.tensor_scalar(w[:, h, :], z[:, h, :], -1.0, None, ALU.mult))
                    own.settle()
                    v.tensor_tensor(w[:, h, :], w[:, h, :], z[:, h, :], ALU.min)\
                     .then_inc(S["minus_abs"], 1)
                for h in range(H):
                    v.wait_ge(S["log_ready"], h + 1)
                    own.did(v.scalar_tensor_tensor(w[:, h, :], z[:, h, :], 0.0, w[:, h, :],
                                                   ALU.max, ALU.add))
                    own.settle()
                    v.tensor_tensor(w[:, h, :], w[:, h, :], mask[:, :], ALU.mult)\
                     .then_inc(S["softplus_ready"], 1)
                for h in range(H):
                    v.wait_ge(S["sums_ready"], h + 1)
                    v.tensor_tensor(a[:, h, :], z[:, h, :], k.ps[:, 2 + h % 2, 0:SEG], ALU.add)\
                     .then_inc(S["logs_ready"], 1)
                for h in range(H):
                    v.wait_ge(S["exp_ready"], h + 1)
                    v.scalar_tensor_tensor(a[:, h, :], a[:, h, :], 1.0, mask[:, :], ALU.min, ALU.mult)\
                     .then_inc(S["weights_ready"], 1)


def gdn_conv(k, m):
    S, stale = k.stage()
    y = m["qkv"]
    with ExitStack() as ctx:
        sq = k.sbuf(ctx, "squares", KT, T)
        with k.nc.Block() as block:
            @block.sync
            def _(sp):
                clear(sp, stale)

            @block.vector
            def _(v):
                own = Steps(v, S["vector_steps"])
                for group in range(3):
                    for tap in range(CONV_TAPS):
                        own.settle()
                        for i in range(4 * group, 4 * group + 4):
                            x = m["conv_in"][:, i, tap:tap + T]
                            g = k.column("gdn_conv", CONV_TAPS * i + tap)
                            if tap == 0:
                                ins = v.tensor_scalar(y[:, i, :], x, g, None, ALU.mult)
                            else:
                                ins = v.scalar_tensor_tensor(y[:, i, :], x, g, y[:, i, :], ALU.mult, ALU.add)
                            own.did(ins)
                for i in range(KT):
                    v.wait_ge(S["sums"], i + 1)
                    v.tensor_scalar(sq[:, i, :], k.ps[:, i % 8, 0:T], 1.0, EPS, ALU.mult, ALU.add)\
                     .then_inc(S["eps_added"], 1)
                v.wait_ge(S["roots"], 1)
                own.did(v.reciprocal(sq[:, :, :], sq[:, :, :]))
                own.settle()
                own.did(v.scalar_tensor_tensor(y[:, 0:4, :], y[:, 0:4, :], GDN_DIM ** -0.5, sq[:, 0:4, :],
                                               ALU.mult, ALU.mult))
                own.did(v.tensor_tensor(y[:, 4:8, :], y[:, 4:8, :], sq[:, 4:8, :], ALU.mult))

            @block.scalar
            def _(act):
                for group in range(3):
                    act.wait_ge(S["vector_steps"], 4 * CONV_TAPS * (group + 1))
                    act.activation(y[:, 4 * group:4 * group + 4, :], y[:, 4 * group:4 * group + 4, :],
                                   ACT.Silu).then_inc(S["silu"], 1)
                for group in range(2):
                    act.wait_ge(S["silu"], group + 1)
                    act.activation(sq[:, 4 * group:4 * group + 4, :], y[:, 4 * group:4 * group + 4, :],
                                   ACT.Square).then_inc(S["squares"], 1)
                act.wait_ge(S["eps_added"], KT)
                act.activation(sq[:, :, :], sq[:, :, :], ACT.Sqrt).then_inc(S["roots"], 1)

            @block.tensor
            def _(pe):
                for i in range(KT):
                    pe.wait_ge(S["squares"], i // 4 + 1)
                    pe.matmul(k.ps[:, i % 8, 0:T], k.const("ones"), sq[:, i, :], start=True, stop=True)\
                      .then_inc(S["sums"], 1)


def invert_tensor(k, pe, S, lt, x, u, lm, pc, groups):
    n = LEVELS * groups

    def first_product(i):
        g = i % groups
        pe.wait_ge(S["level_masked"], i + 1)
        if i >= groups:
            pe.wait_ge(S["inverse_updated"], i - groups + 1)
        for h in range(4):
            last = pe.matmul(k.ps[:, 3 * (i % 2), P * h:P * h + P], lm[:, i % 2, h, :], x[:, g, h, :],
                             start=True, stop=True)
        last.then_inc(S["product_ready"], 1)

    first_product(0)
    for i in range(n):
        g = i % groups
        if i + 1 < n and groups > 1:
            first_product(i + 1)
        pe.wait_ge(S["product_copied"], i + 1)
        if i >= 2:
            pe.wait_ge(S["inverse_updated"], i - 1)
        for h in range(4):
            pe.matmul(k.ps[:, 3 * (i % 2) + 1, P * h:P * h + P], u[:, g, h, :], pc[:, i % 2, h, :],
                      start=True, stop=True)
            last = pe.matmul(k.ps[:, 3 * (i % 2) + 2, P * h:P * h + P], pc[:, i % 2, h, :], u[:, g, h, :],
                             start=True, stop=True)
        last.then_inc(S["updates_ready"], 1)


def invert_scalar(k, act, S, pc, groups):
    for i in range(LEVELS * groups):
        act.wait_ge(S["product_ready"], i + 1)
        if i >= 2:
            act.wait_ge(S["updates_ready"], i - 1)
        act.activation(pc[:, i % 2, :, :], k.ps[:, 3 * (i % 2), :].rearrange("p (h n) -> p h n", h=4),
                       ACT.Copy).then_inc(S["product_copied"], 1)


def invert_vector(k, v, S, lt, x, u, lm, groups):
    n = LEVELS * groups

    def mask(i):
        v.tensor_tensor(lm[:, i % 2, :, :], lt[:, i % groups, :, :],
                        over(k.const(f"level{i // groups}"), 4), ALU.mult).then_inc(S["level_masked"], 1)

    mask(0)
    mask(1)
    for i in range(n):
        g = i % groups
        v.wait_ge(S["updates_ready"], i + 1)
        for dst, bank in ((x, 1), (u, 2)):
            last = v.tensor_tensor(dst[:, g, :, :], dst[:, g, :, :],
                                   k.ps[:, 3 * (i % 2) + bank, :].rearrange("p (h n) -> p h n", h=4),
                                   ALU.subtract)
        last.then_inc(S["inverse_updated"], 1)
        if i + 2 < n:
            mask(i + 2)


def four(ap):
    return ap.rearrange("p (h n) -> p h n", h=4)


def gdn_chunks(k, m):
    S, stale = k.stage()
    H = GDN_HEADS
    q, kk, vv = (lambda h: m["qkv"][:, h, :]), (lambda h: m["qkv"][:, 4 + h, :]), (lambda h: m["qkv"][:, 8 + h, :])
    with ExitStack() as ctx:
        sb = lambda name, *shape: k.sbuf(ctx, name, *shape)
        wide_g, wide_b = sb("wide_g", 2, H, P), sb("wide_beta", 2, H, P)
        sums = sb("gc_columns", 2, H)
        edge = sb("exp_gc_columns", 2, H)
        decay = sb("decay_t", 2, H, P)
        grown = sb("exp_gc_rows", 2, H, P)
        lt, qk_t = sb("lt", 2, H, P), sb("qk_t", 2, H, P)
        x, u = sb("inverse", 2, H, P), sb("inverse_t", 2, H, P)
        lm, pc = sb("level", 2, H, P), sb("product", 2, H, P)
        k_beta, v_beta, k_dec = sb("k_beta", 2, H, P), sb("v_beta", 2, H, P), sb("k_dec", 2, H, P)
        w_t, uu = sb("w_t", H, P), sb("u", 2, H, P)
        q_dec, state = sb("q_dec", H, P), sb("state", H, P)

        with k.nc.Block() as block:
            @block.sync
            def _(sp):
                clear(sp, stale)

            @block.tensor
            def _(pe):
                for tb in range(TB):
                    tok = slice(P * tb, P * tb + P)
                    if tb:
                        pe.wait_ge(S["scores_read"], tb)
                    pe.wait_ge(S["wide"], tb + 1)
                    for h in range(H):
                        cols = slice(P * h, P * h + P)
                        pe.matmul(k.ps[:, 0, cols], wide_g[:, tb, h, :], k.const("upto"), start=True, stop=True)
                        pe.matmul(k.ps[:, 1, cols], wide_b[:, tb, h, :], k.const("identity"), start=True, stop=True)
                        pe.matmul(k.ps[:, 2, cols], kk(h)[:, tok], kk(h)[:, tok], start=True, stop=True)
                        pe.matmul(k.ps[:, 3, cols], kk(h)[:, tok], q(h)[:, tok], start=True, stop=True)
                    pe.matmul(k.ps[:, 4, 0:H], k.const("upto"), m["decay"][:, 1, tb, :],
                              start=True, stop=True).then_inc(S["scores_ready"], 1)
                for tb in range(TB):
                    tok = slice(P * tb, P * tb + P)
                    if tb:
                        pe.wait_ge(S["tokens_out"], tb)
                    for h in range(H):
                        cols = slice(P * h, P * h + P)
                        pe.transpose(k.ps[:, 6, cols], kk(h)[:, tok], k.const("identity"))
                        last = pe.transpose(k.ps[:, 7, cols], vv(h)[:, tok], k.const("identity"))
                    last.then_inc(S["tokens_ready"], 1)
                pe.wait_ge(S["scores_read"], TB)
                invert_tensor(k, pe, S, lt, x, u, lm, pc, 2)
                pe.wait_ge(S["tokens_out"], TB)
                pe.wait_ge(S["inverse_updated"], LEVELS * 2)
                for h in range(H):
                    cols = slice(P * h, P * h + P)
                    pe.matmul(k.ps[:, 0, cols], u[:, 0, h, :], v_beta[:, 0, h, :], start=True, stop=True)
                    pe.matmul(k.ps[:, 1, cols], u[:, 1, h, :], v_beta[:, 1, h, :], start=True, stop=True)
                    last = pe.matmul(k.ps[:, 2, cols], k_beta[:, 1, h, :], u[:, 1, h, :], start=True, stop=True)
                last.then_inc(S["solved"], 1)
                pe.wait_ge(S["solution_out"], 1)
                for h in range(H):
                    cols = slice(P * h, P * h + P)
                    pe.matmul(k.ps[:, 3, cols], uu[:, 0, h, :], qk_t[:, 0, h, :], start=True, stop=True)
                    last = pe.matmul(k.ps[:, 4, cols], k_dec[:, 0, h, :], uu[:, 0, h, :], start=True, stop=True)
                last.then_inc(S["state_ready"], 1)
                pe.wait_ge(S["state_out"], 1)
                for h in range(H):
                    last = pe.matmul(k.ps[:, 5, P * h:P * h + P], w_t[:, h, :], state[:, h, :], start=True, stop=True)
                last.then_inc(S["recalled"], 1)
                pe.wait_ge(S["corrected"], 1)
                for h in range(H):
                    cols = slice(P * h, P * h + P)
                    pe.matmul(k.ps[:, 6, cols], state[:, h, :], q_dec[:, h, :], start=True, stop=False)
                    last = pe.matmul(k.ps[:, 6, cols], uu[:, 1, h, :], qk_t[:, 1, h, :], start=False, stop=True)
                last.then_inc(S["outputs_ready"], 1)

            @block.scalar
            def _(act):
                for tb in range(TB):
                    act.wait_ge(S["scores_ready"], tb + 1)
                    act.activation(grown[:, tb, :, :], four(k.ps[:, 0, :]), ACT.Exp)\
                       .then_inc(S["grown"], 1)
                    act.wait_ge(S["log_decay"], tb + 1)
                    act.activation(decay[:, tb, :, :], decay[:, tb, :, :], ACT.Exp).then_inc(S["decays"], 1)
                    act.activation(edge[:, tb, :], sums[:, tb, :], ACT.Exp).then_inc(S["decays"], 1)
                invert_scalar(k, act, S, pc, 2)
                act.wait_ge(S["solved"], 1)
                act.activation(uu[:, 0, :, :], four(k.ps[:, 0, :]), ACT.Copy)
                act.activation(uu[:, 1, :, :], four(k.ps[:, 1, :]), ACT.Copy)
                act.activation(w_t[:, :, :], four(k.ps[:, 2, :]), ACT.Copy).then_inc(S["solution_out"], 1)
                act.wait_ge(S["state_ready"], 1)
                act.activation(state[:, :, :], four(k.ps[:, 4, :]), ACT.Copy).then_inc(S["state_out"], 1)
                act.activation(m["o_gdn"][:, :, 0:P], four(k.ps[:, 3, :]), ACT.Copy)
                act.wait_ge(S["outputs_ready"], 1)
                act.activation(m["o_gdn"][:, :, P:T], four(k.ps[:, 6, :]), ACT.Copy)

            @block.vector
            def _(v):
                own = Steps(v, S["vector_steps"])
                for tb in range(TB):
                    for h in range(H):
                        v.tensor_scalar(wide_g[:, tb, h, :], k.const("ones"), m["decay"][:, 1, tb, h:h + 1],
                                        None, ALU.mult)
                        last = v.tensor_scalar(wide_b[:, tb, h, :], k.const("ones"),
                                               m["beta"][:, tb, h:h + 1], None, ALU.mult)
                    last.then_inc(S["wide"], 1)
                    v.tensor_copy(x[:, tb, :, :], over(k.const("identity"), H))
                    v.tensor_copy(u[:, tb, :, :], over(k.const("identity"), H))
                for tb in range(TB):
                    v.wait_ge(S["scores_ready"], tb + 1)
                    own.did(v.tensor_copy(sums[:, tb, :], k.ps[:, 4, 0:H]))
                    own.settle()
                    v.wait_ge(S["grown"], tb + 1)
                    for h in range(H):
                        last = v.tensor_scalar(decay[:, tb, h, :], k.ps[:, 0, P * h:P * h + P],
                                               sums[:, tb, h:h + 1], 0.0, ALU.subtract, ALU.min)
                    last.then_inc(S["log_decay"], 1)
                    v.wait_ge(S["decays"], 2 * tb + 1)
                    own.did(v.tensor_tensor(lt[:, tb, :, :], four(k.ps[:, 2, :]), decay[:, tb, :, :], ALU.mult))
                    own.did(v.tensor_tensor(qk_t[:, tb, :, :], four(k.ps[:, 3, :]), decay[:, tb, :, :], ALU.mult))
                    own.settle()
                    own.did(v.tensor_tensor(lt[:, tb, :, :], lt[:, tb, :, :], four(k.ps[:, 1, :]), ALU.mult))
                    own.did(v.tensor_tensor(qk_t[:, tb, :, :], qk_t[:, tb, :, :], over(k.const("upto"), H), ALU.mult))
                    own.settle()
                    v.tensor_tensor(lt[:, tb, :, :], lt[:, tb, :, :], over(k.const("strict"), H), ALU.mult)\
                     .then_inc(S["scores_read"], 1)
                for tb in range(TB):
                    v.wait_ge(S["tokens_ready"], tb + 1)
                    v.wait_ge(S["decays"], 2 * tb + 2)
                    own.did(v.tensor_tensor(edge[:, tb, :], edge[:, tb, :], m["beta"][:, tb, :], ALU.mult))
                    own.settle()
                    for h in range(H):
                        cols = slice(P * h, P * h + P)
                        v.tensor_scalar(k_beta[:, tb, h, :], k.ps[:, 6, cols], edge[:, tb, h:h + 1], None, ALU.mult)
                        v.tensor_scalar(k_dec[:, tb, h, :], k.ps[:, 6, cols], decay[:, tb, h, P - 1:P], None, ALU.mult)
                        last = v.tensor_scalar(v_beta[:, tb, h, :], k.ps[:, 7, cols], m["beta"][:, tb, h:h + 1],
                                               None, ALU.mult)
                    last.then_inc(S["tokens_out"], 1)
                v.tensor_tensor(q_dec[:, :, :], m["qkv"][:, 0:4, P:T], grown[:, 1, :, :], ALU.mult)
                v.wait_ge(S["scores_read"], TB)
                invert_vector(k, v, S, lt, x, u, lm, 2)
                v.wait_ge(S["recalled"], 1)
                v.tensor_tensor(uu[:, 1, :, :], uu[:, 1, :, :], four(k.ps[:, 5, :]), ALU.subtract)\
                 .then_inc(S["corrected"], 1)


def gdn_gate(k, m):
    S, stale = k.stage()
    o = m["o_gdn"]
    with ExitStack() as ctx:
        sq = k.sbuf(ctx, "squares", 4, T)
        with k.nc.Block() as block:
            @block.sync
            def _(sp):
                clear(sp, stale)

            @block.scalar
            def _(act):
                act.activation(sq[:, :, :], o[:, :, :], ACT.Square).then_inc(S["squares"], 1)
                act.wait_ge(S["means"], 4)
                act.activation(sq[:, :, :], sq[:, :, :], ACT.Sqrt).then_inc(S["roots"], 1)

            @block.tensor
            def _(pe):
                pe.wait_ge(S["squares"], 1)
                for i in range(4):
                    pe.matmul(k.ps[:, i, 0:T], k.const("ones"), sq[:, i, :], start=True, stop=True)\
                      .then_inc(S["sums"], 1)

            @block.vector
            def _(v):
                own = Steps(v, S["vector_steps"])
                for i in range(4):
                    v.wait_ge(S["sums"], i + 1)
                    v.tensor_scalar(sq[:, i, :], k.ps[:, i, 0:T], 1.0 / GDN_DIM, EPS, ALU.mult, ALU.add)\
                     .then_inc(S["means"], 1)
                v.wait_ge(S["roots"], 1)
                own.did(v.reciprocal(sq[:, :, :], sq[:, :, :]))
                own.settle()
                own.did(v.scalar_tensor_tensor(o[:, :, :], o[:, :, :], k.column("gdn_norm_g", 0), sq[:, :, :],
                                               ALU.mult, ALU.mult))
                own.settle()
                v.tensor_tensor(o[:, :, :], o[:, :, :], m["z"][:, :, :], ALU.mult)


def merge_branches(k, m):
    S, stale = k.stage()
    first = k.w.taken
    with ExitStack() as ctx:
        part = k.sbuf(ctx, "gated", 2, T)
        with k.nc.Block() as block:
            @block.sync
            def _(sp):
                clear(sp, stale)
                k.w.load_ahead(sp, first, KT)

            @block.tensor
            def _(pe):
                for i in range(KT):
                    if i >= 4:
                        pe.wait_ge(S["tile_merged"], i - 3)
                    tiles = k.w.arrived(pe)
                    for b, src in enumerate((m["o_sb"], m["o_gdn"])):
                        for t in range(4):
                            last = pe.matmul(k.ps[:, i % 4, T * b:T * b + T], tiles[:, 4 * b + t, :],
                                             src[:, t, :], start=t == 0, stop=t == 3)
                    last.then_inc(k.w.used, 1)

            @block.vector
            def _(v):
                own = Steps(v, S["vector_steps"])
                for i in range(KT):
                    v.wait_ge(k.w.used, first + i + 1)
                    if i:
                        v.wait_ge(S["tile_merged"], i)
                    for b in range(2):
                        own.did(v.tensor_tensor(part[:, b, :], m["gates"][:, KT * b + i, :],
                                                k.ps[:, i % 4, T * b:T * b + T], ALU.mult))
                    own.settle()
                    v.tensor_tensor(k.xn[:, i, :], part[:, 0, :], part[:, 1, :], ALU.add)\
                     .then_inc(S["tile_merged"], 1)


def token_mixer(k):
    with ExitStack() as ctx:
        sb = lambda name, *shape: k.sbuf(ctx, name, *shape)
        m = {"w_ba": sb("w_ba", KT, 8), "rows": sb("gdn_rows", 8),
             "beta": sb("beta", TB, 4), "decay": sb("decay", 3, TB, 4),
             "z": sb("z_silu", 4, T), "gates": sb("gates", 16, T),
             "o_sb": sb("o_sb", 4, T), "o_gdn": sb("o_gdn", 4, T), "qkv": sb("qkv", 12, T),
             "sb_qk": sb("sb_qk", 8, T), "sb_v": sb("sb_v", TB, 512),
             "conv_in": sb("conv_in", 12, T + CONV_TAPS - 1)}
        rmsnorm(k, k.x, "g_mix", k.xn)
        project_in(k, m)
        stick_breaking(k, m)
        gdn_conv(k, m)
        gdn_chunks(k, m)
        gdn_gate(k, m)
        merge_branches(k, m)
    with ExitStack() as ctx:
        project_residual(k, k.xn)


def cross_attention(k):
    with ExitStack() as ctx:
        q, kk = k.sbuf(ctx, "xq", KT, T), k.sbuf(ctx, "xk", KT, T)
        v_tok, o = k.sbuf(ctx, "xv", TB, D), k.sbuf(ctx, "xo", KT, T)
        mem, mem_n = k.sbuf(ctx, "mem", KT, T), k.sbuf(ctx, "mem_normed", KT, T)
        load_memory(k, mem)
        rmsnorm(k, k.x, "g_cross", k.xn)
        rmsnorm(k, mem, "g_mem", mem_n)
        cross_project(k, q, kk, v_tok, mem_n)
        cross_heads(k, q, kk, v_tok, o)
        project_residual(k, o)


def load_memory(k, mem):
    S, stale = k.stage()
    with k.nc.Block() as block:
        @block.sync
        def _(sp):
            clear(sp, stale)
            sp.dma_start(mem[:, :, :], k.dram["mem"]).then_inc(S["loaded"], 16)
            sp.wait_ge(S["loaded"], 16)


def cross_project(k, q, kk, v_tok, mem_n):
    S, stale = k.stage()
    first = k.w.taken
    with k.nc.Block() as block:
        @block.sync
        def _(sp):
            clear(sp, stale)
            k.w.load_ahead(sp, first, 3 * KT)

        @block.tensor
        def _(pe):
            for i in range(3 * KT):
                if i >= 4:
                    pe.wait_ge(S["copied"], i - 3)
                tiles = k.w.arrived(pe)
                if i < 2 * KT:
                    moving = k.xn if i < KT else mem_n
                    for t in range(KT):
                        last = pe.matmul(k.ps[:, i % 4, 0:T], tiles[:, t, :], moving[:, t, :],
                                         start=t == 0, stop=t == KT - 1)
                else:
                    for tb in range(TB):
                        for t in range(KT):
                            last = pe.matmul(k.ps[:, i % 4, P * tb:P * tb + P],
                                             mem_n[:, t, P * tb:P * tb + P], tiles[:, t, :],
                                             start=t == 0, stop=t == KT - 1)
                last.then_inc(k.w.used, 1)

        @block.vector
        def _(v):
            for i in range(3 * KT):
                v.wait_ge(k.w.used, first + i + 1)
                src = k.ps[:, i % 4, 0:T]
                if i < KT:
                    out = q[:, i, :]
                elif i < 2 * KT:
                    out = kk[:, i - KT, :]
                else:
                    c = i - 2 * KT
                    out, src = v_tok[:, :, P * c:P * c + P], src.rearrange("p (b n) -> p b n", b=TB)
                v.tensor_copy(out, src).then_inc(S["copied"], 1)


def cross_heads(k, q, kk, v_tok, o):
    S, stale = k.stage()
    N = X_HEADS * TB
    with ExitStack() as ctx:
        p = k.sbuf(ctx, "probs", N, T)
        p_t = k.sbuf(ctx, "probs_t", X_HEADS, TB, T)
        top, total = k.sbuf(ctx, "row_max", N), k.sbuf(ctx, "row_sum", N)
        with k.nc.Block() as block:
            @block.sync
            def _(sp):
                clear(sp, stale)

            @block.tensor
            def _(pe):
                for i in range(N):
                    h, tb = i // TB, i % TB
                    if i >= 4:
                        pe.wait_ge(S["scores_out"], i - 3)
                    for c in range(2):
                        last = pe.matmul(k.ps[:, i % 4, 0:T], q[:, 2 * h + c, P * tb:P * tb + P],
                                         kk[:, 2 * h + c, :], start=c == 0, stop=c == 1)
                    last.then_inc(S["scores_ready"], 1)
                for i in range(N):
                    h, tb = i // TB, i % TB
                    pe.wait_ge(S["probs_ready"], i + 1)
                    if i >= 2:
                        pe.wait_ge(S["transposed_out"], i - 1)
                    for mb in range(TB):
                        last = pe.transpose(k.ps[:, 4 + i % 2, P * mb:P * mb + P],
                                            p[:, i, P * mb:P * mb + P], k.const("identity"))
                    last.then_inc(S["transposed"], 1)
                for h in range(X_HEADS):
                    pe.wait_ge(S["transposed_out"], TB * (h + 1))
                    for c in range(2):
                        n = 2 * h + c
                        if n >= 2:
                            pe.wait_ge(S["outputs_out"], n - 1)
                        for mb in range(TB):
                            last = pe.matmul(k.ps[:, 6 + n % 2, 0:T], v_tok[:, mb, P * n:P * n + P],
                                             p_t[:, h, mb, :], start=mb == 0, stop=mb == 1)
                        last.then_inc(S["outputs_ready"], 1)

            @block.vector
            def _(v):
                own = Steps(v, S["vector_steps"])
                for i in range(N):
                    v.wait_ge(S["scores_ready"], i + 1)
                    own.did(v.reduce_max(top[:, i:i + 1], k.ps[:, i % 4, 0:T], AX.X))
                    own.settle()
                    v.tensor_scalar(top[:, i:i + 1], top[:, i:i + 1], -X_DIM ** -0.5, None, ALU.mult)\
                     .then_inc(S["max_ready"], 1)
                for i in range(N):
                    v.wait_ge(S["scores_out"], i + 1)
                    own.did(v.reciprocal(total[:, i:i + 1], total[:, i:i + 1]))
                    own.settle()
                    v.tensor_scalar(p[:, i, :], p[:, i, :], total[:, i:i + 1], None, ALU.mult)\
                     .then_inc(S["probs_ready"], 1)
                for i in range(N):
                    h, tb = i // TB, i % TB
                    v.wait_ge(S["transposed"], i + 1)
                    v.tensor_copy(p_t[:, h, :, P * tb:P * tb + P],
                                  k.ps[:, 4 + i % 2, 0:T].rearrange("p (b n) -> p b n", b=TB))\
                     .then_inc(S["transposed_out"], 1)

            @block.scalar
            def _(act):
                for i in range(N):
                    act.wait_ge(S["max_ready"], i + 1)
                    act.activation(p[:, i, :], k.ps[:, i % 4, 0:T], ACT.Exp, bias=top[:, i:i + 1],
                                   scale=X_DIM ** -0.5, accum_out=total[:, i:i + 1])\
                       .then_inc(S["scores_out"], 1)
                for n in range(KT):
                    act.wait_ge(S["outputs_ready"], n + 1)
                    act.activation(o[:, n, :], k.ps[:, 6 + n % 2, 0:T], ACT.Copy)\
                       .then_inc(S["outputs_out"], 1)


def peer(k):
    with ExitStack() as ctx:
        scores = k.sbuf(ctx, "key_scores", TB, 2 * PEER_HEADS, PEER_KEYS)
        tokens = k.sbuf(ctx, "x_tokens", TB, D)
        rmsnorm(k, k.x, "g_peer", k.xn)
        peer_scores(k, scores, tokens)
        experts = k.sbuf(ctx, "experts", TB, SLOTS, dtype=U32)
        gates = k.sbuf(ctx, "expert_gates", TB, SLOTS)
        peer_route(k, scores, experts, gates)
        peer_experts(k, tokens, experts, gates)


def peer_scores(k, scores, tokens):
    S, stale = k.stage()
    first = k.w.taken
    N = 2 * PEER_HEADS
    with ExitStack() as ctx:
        q = k.sbuf(ctx, "peer_q", N, T)
        with k.nc.Block() as block:
            @block.sync
            def _(sp):
                clear(sp, stale)
                k.w.load_ahead(sp, first, N + 2)

            @block.tensor
            def _(pe):
                for i in range(N):
                    if i >= 4:
                        pe.wait_ge(S["copied"], i - 3)
                    tiles = k.w.arrived(pe)
                    for t in range(KT):
                        last = pe.matmul(k.ps[:, i % 4, 0:T], tiles[:, t, :], k.xn[:, t, :],
                                         start=t == 0, stop=t == KT - 1)
                    last.then_inc(k.w.used, 1)
                for i in range(4):
                    for t in range(4):
                        last = pe.transpose(k.ps[:, 4 + i, P * t:P * t + P],
                                            k.xn[:, 4 * (i % 2) + t, P * (i // 2):P * (i // 2) + P],
                                            k.const("identity"))
                    last.then_inc(S["transposed"], 1)
                pe.wait_ge(S["copied"], N)
                for i in range(N):
                    if i % KT == 0:
                        keys = k.w.arrived(pe)
                    if i >= 4:
                        pe.wait_ge(S["scores_out"], i - 3)
                    for tb in range(TB):
                        last = pe.matmul(k.ps[:, i % 4, P * tb:P * tb + P], q[:, i, P * tb:P * tb + P],
                                         keys[:, i % KT, :], start=True, stop=True)
                    last.then_inc(k.w.used if i % KT == KT - 1 else S["scores_made"], 1)

            @block.scalar
            def _(act):
                for i in range(4):
                    act.wait_ge(S["transposed"], i + 1)
                    act.activation(tokens[:, i // 2, 512 * (i % 2):512 * (i % 2) + 512], k.ps[:, 4 + i, :],
                                   ACT.Copy)

            @block.vector
            def _(v):
                for i in range(N):
                    v.wait_ge(k.w.used, first + i + 1)
                    v.tensor_copy(q[:, i, :], k.ps[:, i % 4, 0:T]).then_inc(S["copied"], 1)
                for i in range(N):
                    if i % KT == KT - 1:
                        v.wait_ge(k.w.used, first + N + i // KT + 1)
                    else:
                        v.wait_ge(S["scores_made"], i + 1 - i // KT)
                    v.tensor_copy(scores[:, :, i, :], k.ps[:, i % 4, 0:T].rearrange("p (b n) -> p b n", b=TB))\
                     .then_inc(S["scores_out"], 1)


def top16(v, own, values, spare, top, index, count):
    for i in range(count):
        own.did(v.max(top(i)[:, 0:8], values(i)))
    own.settle()
    for i in range(count):
        own.did(v.max_index(index(i)[:, 0:8], top(i)[:, 0:8], values(i)))
        own.did(v.match_replace(spare(i), top(i)[:, 0:8], values(i), -3e38))
    own.settle()
    for i in range(count):
        own.did(v.max(top(i)[:, 8:16], spare(i)))
    own.settle()
    for i in range(count):
        own.did(v.max_index(index(i)[:, 8:16], top(i)[:, 8:16], spare(i)))
    own.settle()


def peer_route(k, scores, experts, gates):
    S, stale = k.stage()
    H, K = PEER_HEADS, TOPK
    with ExitStack() as ctx:
        sb = lambda name, *shape, dtype=F32: k.sbuf(ctx, name, *shape, dtype=dtype)
        spare = sb("spare_scores", 2 * H, PEER_KEYS)
        top, top_at = sb("top", 2 * H, K), sb("top_at", 2 * H, K, dtype=U32)
        top_n = sb("top_numbers", 2 * H, K)
        sums, sums_spare = sb("pair_sums", H, K * K), sb("pair_sums_spare", H, K * K)
        best, best_at = sb("best", H, K), sb("best_at", H, K, dtype=U32)
        place = sb("best_place", 2, H * K, dtype=U32)
        place_f = sb("best_place_f", 2, H * K)
        hot = sb("one_hot", H * K, K)
        key = sb("key_numbers", 2, H * K)
        total = sb("gate_sum", H)
        iota = k.const("misc")[:, 32:48]
        with k.nc.Block() as block:
            @block.sync
            def _(sp):
                clear(sp, stale)

            @block.scalar
            def _(act):
                for tb in range(TB):
                    act.wait_ge(S["shifted"], tb + 1)
                    act.activation(gates[:, tb, :], gates[:, tb, :], ACT.Exp).then_inc(S["gate_exps"], 1)

            @block.vector
            def _(v):
                own = Steps(v, S["vector_steps"])
                for tb in range(TB):
                    top16(v, own, lambda i: scores[:, tb, i, :], lambda i: spare[:, i, :],
                          lambda i: top[:, i, :], lambda i: top_at[:, i, :], 2 * H)
                    own.did(v.tensor_copy(top_n[:, :, :], top_at[:, :, :]))
                    halves = top[:, :, :].rearrange("p (h two) i -> p h two i", two=2)
                    a = halves[:, :, 0, :].unsqueeze(3).broadcast_to([P, H, K, K])
                    b = halves[:, :, 1, :].unsqueeze(2).broadcast_to([P, H, K, K])
                    own.did(v.tensor_tensor(sums[:, :, :].rearrange("p h (i j) -> p h i j", i=K), a, b, ALU.add))
                    own.settle()
                    top16(v, own, lambda i: sums[:, i, :], lambda i: sums_spare[:, i, :],
                          lambda i: best[:, i, :], lambda i: best_at[:, i, :], H)
                    shifted = gates[:, tb, :].rearrange("p (h i) -> p h i", h=H)
                    v.tensor_tensor(shifted, best[:, :, :], best[:, :, 0:1].broadcast_to([P, H, K]), ALU.subtract)\
                     .then_inc(S["shifted"], 1)
                    flat_at = best_at[:, :, :].rearrange("p h i -> p (h i)")
                    own.did(v.tensor_scalar(place[:, 0, :], flat_at, 4, None, ALU.logical_shift_right))
                    own.did(v.tensor_scalar(place[:, 1, :], flat_at, K - 1, None, ALU.bitwise_and))
                    own.settle()
                    own.did(v.tensor_copy(place_f[:, :, :], place[:, :, :]))
                    own.settle()
                    numbers = top_n[:, :, :].rearrange("p (h two) i -> p h two i", two=2)
                    hot4 = hot[:, :, :].rearrange("p (h n) j -> p h n j", h=H)
                    for part in range(2):
                        own.did(v.tensor_tensor(hot[:, :, :], place_f[:, part, :].unsqueeze(2).broadcast_to([P, H * K, K]),
                                                over(iota, H * K), ALU.is_equal))
                        own.settle()
                        own.did(v.tensor_tensor(hot4, hot4, numbers[:, :, part, :].unsqueeze(2).broadcast_to([P, H, K, K]),
                                                ALU.mult))
                        own.settle()
                        own.did(v.tensor_reduce(key[:, part, :], hot[:, :, :], AX.X, ALU.add))
                        own.settle()
                    own.did(v.scalar_tensor_tensor(key[:, 0, :], key[:, 0, :], float(PEER_KEYS), key[:, 1, :],
                                                   ALU.mult, ALU.add))
                    own.settle()
                    own.did(v.tensor_copy(experts[:, tb, :], key[:, 0, :]))
                    v.wait_ge(S["gate_exps"], tb + 1)
                    own.did(v.tensor_reduce(total[:, :], shifted, AX.X, ALU.add))
                    own.settle()
                    own.did(v.reciprocal(total[:, :], total[:, :]))
                    own.settle()
                    own.did(v.tensor_tensor(shifted, shifted, total[:, :].unsqueeze(2).broadcast_to([P, H, K]),
                                            ALU.mult))


def peer_experts(k, tokens, experts, gates):
    S, stale = k.stage()
    R = GATHER_RING
    with ExitStack() as ctx:
        rows = k.sbuf(ctx, "expert_rows", R, D)
        dots = k.sbuf(ctx, "expert_dots", TB, SLOTS)
        waste = k.sbuf(ctx, "products", 2, D)
        out = k.sbuf(ctx, "expert_sums", TB, 2, D)
        gathers = [(table, tb, s) for table in ("peer_u", "peer_v") for tb in range(TB) for s in range(SLOTS)]
        rows_ready = k.rows_ready
        with k.nc.Block() as block:
            @block.sync
            def _(sp):
                clear(sp, stale)

            @block.gpsimd
            def _(pool):
                for i, (table, tb, s) in enumerate(gathers):
                    if i >= R:
                        pool.wait_ge(S["rows_used"], i - R + 1)
                    pool.indirect_dma_start(
                        out=rows[:, i % R, :], out_offset=None, in_=k.dram[table],
                        in_offset=bass.IndirectOffsetOnAxis(ap=experts[:, tb, s:s + 1], axis=0),
                    ).then_inc(rows_ready[i % R], 16)

            @block.scalar
            def _(act):
                for tb in range(TB):
                    act.wait_ge(S["rows_used"], SLOTS * (tb + 1))
                    act.activation(dots[:, tb, :], dots[:, tb, :], ACT.Gelu).then_inc(S["gelus"], 1)

            @block.vector
            def _(v):
                for i, (table, tb, s) in enumerate(gathers):
                    v.wait_ge(rows_ready[i % R], 16 * (i // R + 1))
                    row = rows[:, i % R, :]
                    if table == "peer_u":
                        if i >= 2:
                            v.wait_ge(S["rows_used"], i - 1)
                        v.tensor_tensor_reduce(out=waste[:, i % 2, :], in0=row, in1=tokens[:, tb, :], scale=1.0,
                                               scalar=0.0, op0=ALU.mult, op1=ALU.add,
                                               accum_out=dots[:, tb, s:s + 1]).then_inc(S["rows_used"], 1)
                        continue
                    if s == 0:
                        v.wait_ge(S["gelus"], tb + 1)
                        v.tensor_tensor(gates[:, tb, :], gates[:, tb, :], dots[:, tb, :], ALU.mult)\
                         .then_inc(S["weighted"], 1)
                        v.wait_ge(S["weighted"], tb + 1)
                    acc = out[:, tb, s % 2, :]
                    if s < 2:
                        ins = v.tensor_scalar(acc, row, gates[:, tb, s:s + 1], None, ALU.mult)
                    else:
                        v.wait_ge(S["rows_used"], i - 1)
                        ins = v.scalar_tensor_tensor(acc, row, gates[:, tb, s:s + 1], acc, ALU.mult, ALU.add)
                    ins.then_inc(S["rows_used"], 1)
                    if s == SLOTS - 1:
                        v.wait_ge(S["rows_used"], i + 1)
                        v.tensor_tensor(out[:, tb, 0, :], out[:, tb, 0, :], out[:, tb, 1, :], ALU.add)\
                         .then_inc(S["sums_ready"], 1)
                for tb in range(TB):
                    for half in range(2):
                        v.wait_ge(S["transposed"], 2 * tb + half + 1)
                        part = k.x[:, 4 * half:4 * half + 4, P * tb:P * tb + P]
                        v.tensor_tensor(part, part, four(k.ps[:, 2 * tb + half, :]), ALU.add)

            @block.tensor
            def _(pe):
                for tb in range(TB):
                    pe.wait_ge(S["sums_ready"], tb + 1)
                    for half in range(2):
                        for t in range(4):
                            at = P * (4 * half + t)
                            last = pe.transpose(k.ps[:, 2 * tb + half, P * t:P * t + P],
                                                out[:, tb, 0, at:at + P], k.const("identity"))
                        last.then_inc(S["transposed"], 1)


def ffn(k, name):
    rmsnorm(k, k.x, f"{name}_pre_g_2", k.xn)
    S, stale = k.stage()
    first = k.w.taken

    def up_done(f):
        return first + 2 * (f + 1) + max(f - 1, 0)

    with ExitStack() as ctx:
        gate, hidden = k.sbuf(ctx, "silu_gate", 2, T), k.sbuf(ctx, "hidden", 2, T)
        y = k.sbuf(ctx, "ffn_out", KT, T)
        acc = k.ps[:, 4:8, :].rearrange("p b (two n) -> p (b two) n", two=2)
        with k.nc.Block() as block:
            @block.sync
            def _(sp):
                clear(sp, stale)
                k.w.load_ahead(sp, first, 3 * FT)

            @block.tensor
            def _(pe):
                def down(f):
                    tiles = k.w.arrived(pe)
                    pe.wait_ge(S["hidden_ready"], f + 1)
                    for o in range(KT):
                        last = pe.matmul(acc[:, o, :], tiles[:, o, :], hidden[:, f % 2, :],
                                         start=f == 0 and o % 2 == 0, stop=f == FT - 1, skip_group_check=True)
                    last.then_inc(k.w.used, 1)

                for f in range(FT):
                    if f >= 2:
                        pe.wait_ge(S["hidden_ready"], f - 1)
                    for b in range(2):
                        tiles = k.w.arrived(pe)
                        for t in range(KT):
                            last = pe.matmul(k.ps[:, 2 * (f % 2) + b, 0:T], tiles[:, t, :], k.xn[:, t, :],
                                             start=t == 0, stop=t == KT - 1)
                        last.then_inc(k.w.used, 1)
                    if f:
                        down(f - 1)
                down(FT - 1)

            @block.scalar
            def _(act):
                for f in range(FT):
                    act.wait_ge(k.w.used, up_done(f) - 1)
                    if f >= 2:
                        act.wait_ge(S["hidden_ready"], f - 1)
                    act.activation(gate[:, f % 2, :], k.ps[:, 2 * (f % 2), 0:T], ACT.Silu)\
                       .then_inc(S["gate_ready"], 1)
                act.wait_ge(k.w.used, first + 3 * FT)
                for half in range(2):
                    act.activation(y[:, 4 * half:4 * half + 4, :], acc[:, 4 * half:4 * half + 4, :], ACT.Copy)

            @block.vector
            def _(v):
                for f in range(FT):
                    v.wait_ge(S["gate_ready"], f + 1)
                    v.wait_ge(k.w.used, up_done(f))
                    if f >= 2:
                        v.wait_ge(k.w.used, first + 3 * (f - 2) + 5)
                    v.tensor_tensor(hidden[:, f % 2, :], gate[:, f % 2, :], k.ps[:, 2 * (f % 2) + 1, 0:T],
                                    ALU.mult).then_inc(S["hidden_ready"], 1)
        rmsnorm(k, y, f"{name}_post_g_2", k.x, residual=0.5)


def project_to(k, moving, dst):
    S, stale = k.stage()
    first = k.w.taken
    with k.nc.Block() as block:
        @block.sync
        def _(sp):
            clear(sp, stale)
            k.w.load_ahead(sp, first, KT)

        @block.tensor
        def _(pe):
            project(k, pe, S, KT, moving, S["tile_out"])

        @block.vector
        def _(v):
            for i in range(KT):
                v.wait_ge(k.w.used, first + i + 1)
                v.tensor_copy(dst[:, i, :], k.ps[:, i % 4, 0:T]).then_inc(S["tile_out"], 1)


def nsa_mixer(k):
    with ExitStack() as ctx:
        sb = lambda name, *shape: k.sbuf(ctx, name, *shape)
        m = {"q": sb("nsa_q", 4, T), "cmp_in": sb("cmp_in", 2, T), "k_sw": sb("nsa_k", 2, T),
             "v_sw": sb("nsa_v", TB, 2, P), "conv": sb("conv_in2", 12, T), "w_g": sb("w_g", KT, 24),
             "gates": sb("nsa_gates", TB, 24), "o": sb("nsa_o", KT, T),
             "kc": sb("kc", N_CMP), "vc": sb("vc", P), "y": sb("mixer_out", KT, T)}
        rmsnorm(k, k.x, "l0_mix_pre_g_2", k.xn)
        nsa_project(k, m)
        nsa_compress(k, m)
        nsa_heads(k, m)
        short_conv(k, m)
        project_to(k, m["o"], m["y"])
        rmsnorm(k, m["y"], "l0_mix_post_g_2", k.x, residual=1)


def nsa_project(k, m):
    S, stale = k.stage()
    first = k.w.taken
    with k.nc.Block() as block:
        @block.sync
        def _(sp):
            clear(sp, stale)
            sp.dma_start(m["w_g"][:, :, :], k.dram["w_g"]).then_inc(S["small_loaded"], 16)
            k.w.load_ahead(sp, first, 22)

        @block.tensor
        def _(pe):
            pe.wait_ge(S["small_loaded"], 16)
            for tb in range(TB):
                for t in range(KT):
                    last = pe.matmul(k.ps[:, 6, 24 * tb:24 * tb + 24], k.xn[:, t, P * tb:P * tb + P],
                                     m["w_g"][:, t, :], start=t == 0, stop=t == KT - 1)
            last.then_inc(S["gates_ready"], 1)
            for i in range(22):
                if i >= 4:
                    pe.wait_ge(S["copied"], i - 3)
                tiles = k.w.arrived(pe)
                if i in (8, 9):
                    for tb in range(TB):
                        for t in range(KT):
                            last = pe.matmul(k.ps[:, i % 4, P * tb:P * tb + P],
                                             k.xn[:, t, P * tb:P * tb + P], tiles[:, t, :],
                                             start=t == 0, stop=t == KT - 1)
                else:
                    for t in range(KT):
                        last = pe.matmul(k.ps[:, i % 4, 0:T], tiles[:, t, :], k.xn[:, t, :],
                                         start=t == 0, stop=t == KT - 1)
                last.then_inc(k.w.used, 1)

        @block.scalar
        def _(act):
            act.wait_ge(S["gates_ready"], 1)
            act.activation(m["gates"][:, :, :], k.ps[:, 6, 0:48].rearrange("p (b n) -> p b n", b=TB), ACT.Sigmoid)

        @block.vector
        def _(v):
            for i in range(22):
                v.wait_ge(k.w.used, first + i + 1)
                src = k.ps[:, i % 4, 0:T]
                if i < 4:
                    ins = v.tensor_scalar(m["q"][:, i, :], src, NSA_DIM ** -0.5, None, ALU.mult)
                elif i < 8:
                    ins = v.tensor_copy(m["cmp_in" if i < 6 else "k_sw"][:, i % 2, :], src)
                elif i < 10:
                    ins = v.tensor_copy(m["v_sw"][:, :, i - 8, :], src.rearrange("p (b n) -> p b n", b=TB))
                else:
                    ins = v.tensor_copy(m["conv"][:, i - 10, :], src)
                ins.then_inc(S["copied"], 1)


def nsa_compress(k, m):
    S, stale = k.stage()
    L, HALF = CMP_BLOCK, CMP_STRIDE
    with ExitStack() as ctx:
        sb = lambda name, *shape: k.sbuf(ctx, name, *shape)
        w1, w2, pos = sb("cmp_w1", 2, L, P), sb("cmp_w2", 2, NSA_DIM), sb("cmp_pos", 2, L)
        blocks, hidden = sb("cmp_blocks", 2, L, N_CMP), sb("cmp_hidden", 4, N_CMP)
        with k.nc.Block() as block:
            @block.sync
            def _(sp):
                clear(sp, stale)
                sp.dma_start(pos[:, :, :], k.dram["cmp_pos"]).then_inc(S["pos_loaded"], 16)
                sp.dma_start(w1[:, :, :, :], k.dram["cmp_w1"]).then_inc(S["w1_loaded"], 16)
                sp.dma_start(w2[:, :, :], k.dram["cmp_w2"]).then_inc(S["w2_loaded"], 16)

            @block.vector
            def _(v):
                v.wait_ge(S["pos_loaded"], 16)
                for kv in range(2):
                    strided = m["cmp_in"][:, kv, :].rearrange("p (n s) -> p s n", s=HALF)
                    for a in range(2):
                        part = slice(HALF * a, HALF * a + HALF)
                        v.tensor_tensor(blocks[:, kv, part, :], strided[:, :, a:a + N_CMP],
                                        pos[:, kv, part].unsqueeze(2).broadcast_to([P, HALF, N_CMP]), ALU.add)\
                         .then_inc(S["blocks_ready"], 1)
                v.wait_ge(S["keys_ready"], 1)
                for g in range(NSA_GROUPS):
                    half = slice(64 * g, 64 * g + 64)
                    v.tensor_copy(m["kc"][half, :], k.ps[half, 4 + g, 0:N_CMP])
                v.tensor_copy(m["vc"][0:N_CMP, :], k.ps[0:N_CMP, 6, 0:P])

            @block.tensor
            def _(pe):
                pe.wait_ge(S["w1_loaded"], 16)
                for kv in range(2):
                    pe.wait_ge(S["blocks_ready"], 2 * kv + 2)
                    for g in range(NSA_GROUPS):
                        half = slice(64 * g, 64 * g + 64)
                        for i in range(L):
                            last = pe.matmul(k.ps[:, 2 * kv + g, 0:N_CMP], w1[half, kv, i, :], blocks[half, kv, i, :],
                                             start=i == 0, stop=i == L - 1)
                        last.then_inc(S["hidden_ready"], 1)
                pe.wait_ge(S["w2_loaded"], 16)
                pe.wait_ge(S["gelus"], 4)
                for g in range(NSA_GROUPS):
                    pe.matmul(k.ps[64 * g:64 * g + 64, 4 + g, 0:N_CMP], w2[:, 0, :], hidden[:, g, :],
                              start=True, stop=True)
                    last = pe.matmul(k.ps[0:N_CMP, 6, 64 * g:64 * g + 64], hidden[:, 2 + g, :], w2[:, 1, :],
                                     start=True, stop=True)
                last.then_inc(S["keys_ready"], 1)

            @block.scalar
            def _(act):
                for i in range(4):
                    act.wait_ge(S["hidden_ready"], i + 1)
                    act.activation(hidden[:, i, :], k.ps[:, i, 0:N_CMP], ACT.Gelu_apprx_tanh)\
                       .then_inc(S["gelus"], 1)


def nsa_heads(k, m):
    S, stale = k.stage()
    N = NSA_HEADS * TB
    CMP = 2 * T
    with ExitStack() as ctx:
        p = k.sbuf(ctx, "nsa_probs", N, CMP + 16)
        p_t = k.sbuf(ctx, "nsa_probs_t", 4, 4, P)
        c_t = k.sbuf(ctx, "nsa_cmp_t", 4, P)
        top, total = k.sbuf(ctx, "nsa_max", N, 3), k.sbuf(ctx, "nsa_sum", N, 3)

        def at(i):
            h, tb = i // TB, i % TB
            g = h // NSA_REP
            return h, tb, P * (tb + 1), slice(64 * g, 64 * g + 64), h % NSA_REP, slice(P * tb, P * tb + P)

        def wide(i, ap):
            return ap.rearrange("p (two n) -> p two n", two=2)[:, :, 0:at(i)[2]]

        with k.nc.Block() as block:
            @block.sync
            def _(sp):
                clear(sp, stale)

            @block.tensor
            def _(pe):
                for i in range(N):
                    h, tb, keys, half, j, tok = at(i)
                    if i >= 2:
                        pe.wait_ge(S["biased"], i - 1)
                    q = m["q"][half, j, tok]
                    for b in range(2):
                        pe.matmul(k.ps[:, i % 2, T * b:T * b + keys], q, m["k_sw"][half, b, 0:keys],
                                  start=True, stop=True)
                    pe.matmul(k.ps[:, 2 + i % 2, 0:N_CMP], q, m["kc"][half, :], start=True, stop=True)\
                      .then_inc(S["scores_ready"], 1)
                pe.wait_ge(S["biased"], N)
                for i in range(N + 1):
                    if i < N:
                        h, tb, keys, half, j, tok = at(i)
                        pe.wait_ge(S["probs_ready"], i + 1)
                        if i >= 2:
                            pe.wait_ge(S["transposed_out"], i - 1)
                        for b in range(2):
                            for c in range(tb + 1):
                                pe.transpose(k.ps[:, 4 + i % 2, P * (2 * b + c):P * (2 * b + c) + P],
                                             p[:, i, T * b + P * c:T * b + P * c + P], k.const("identity"))
                        pe.transpose(k.ps[0:N_CMP, 2 + i % 2, 0:P], p[:, i, CMP:CMP + N_CMP],
                                     k.const("identity")).then_inc(S["transposed"], 1)
                    if i:
                        n = i - 1
                        h, tb, keys, half, j, tok = at(n)
                        pe.wait_ge(S["transposed_out"], n + 1)
                        if n >= 2:
                            pe.wait_ge(S["outputs_out"], n - 1)
                        out = k.ps[half, 6 + n % 2, 0:P]
                        pe.matmul(out, m["vc"][0:N_CMP, half], c_t[0:N_CMP, n % 4, :], start=True, stop=False)
                        for b in range(2):
                            for c in range(tb + 1):
                                last = pe.matmul(out, m["v_sw"][:, c, b, half], p_t[:, n % 4, 2 * b + c, :],
                                                 start=False, stop=b == 1 and c == tb)
                        last.then_inc(S["outputs_ready"], 1)

            @block.vector
            def _(v):
                own = Steps(v, S["vector_steps"])
                for i in range(N):
                    h, tb, keys, half, j, tok = at(i)
                    slope = 2.0 ** -(h + 1)
                    v.wait_ge(S["scores_ready"], i + 1)
                    delta = k.consts[:, CONST_ROWS.index("causal0"), :] if tb == 0 else \
                        k.consts[:, CONST_ROWS.index("causal1a"):CONST_ROWS.index("causal1b") + 1, :]\
                         .rearrange("p a n -> p (a n)")
                    far = k.const("misc")[:, N_CMP * tb:N_CMP * tb + N_CMP]
                    v.scalar_tensor_tensor(wide(i, p[:, i, 0:CMP]), over(delta, 2), slope,
                                           wide(i, k.ps[:, i % 2, :]), ALU.mult, ALU.add)
                    v.scalar_tensor_tensor(p[:, i, CMP:CMP + N_CMP], far, slope, k.ps[:, 2 + i % 2, 0:N_CMP],
                                           ALU.mult, ALU.add).then_inc(S["biased"], 1)
                    v.wait_ge(S["biased"], i + 1)
                    own.did(v.reduce_max(top[:, i, 1:3], wide(i, p[:, i, 0:CMP]), AX.X))
                    own.did(v.reduce_max(top[:, i, 0:1], p[:, i, CMP:CMP + N_CMP], AX.X))
                    own.settle()
                    v.tensor_scalar(top[:, i, :], top[:, i, :], CLAMP, -1.0, ALU.max, ALU.mult)\
                     .then_inc(S["max_ready"], 1)
                for i in range(N):
                    h, tb, keys, half, j, tok = at(i)
                    v.wait_ge(S["exps_ready"], i + 1)
                    own.did(v.tensor_scalar(total[:, i, :], total[:, i, :], 1e-30, None, ALU.max))
                    own.settle()
                    own.did(v.reciprocal(total[:, i, :], total[:, i, :]))
                    own.settle()
                    own.did(v.tensor_tensor(total[:, i, :], total[:, i, :], m["gates"][:, tb, 3 * h:3 * h + 3], ALU.mult))
                    own.settle()
                    for b in range(2):
                        part = p[:, i, T * b:T * b + keys]
                        v.tensor_scalar(part, part, total[:, i, b + 1:b + 2], None, ALU.mult)
                    part = p[:, i, CMP:CMP + N_CMP]
                    v.tensor_scalar(part, part, total[:, i, 0:1], None, ALU.mult).then_inc(S["probs_ready"], 1)

            @block.scalar
            def _(act):
                for i in range(N):
                    h, tb, keys, half, j, tok = at(i)
                    act.wait_ge(S["max_ready"], i + 1)
                    for b, part in enumerate((p[:, i, CMP:CMP + N_CMP], p[:, i, 0:keys], p[:, i, T:T + keys])):
                        last = act.activation(part, part, ACT.Exp, bias=top[:, i, b:b + 1],
                                              accum_out=total[:, i, b:b + 1])
                    last.then_inc(S["exps_ready"], 1)
                for i in range(N + 1):
                    if i < N:
                        h, tb, keys, half, j, tok = at(i)
                        act.wait_ge(S["transposed"], i + 1)
                        if i >= 4:
                            act.wait_ge(S["outputs_ready"], i - 3)
                        act.activation(p_t[:, i % 4, :, :].rearrange("p (b c) n -> p b c n", b=2)[:, :, 0:tb + 1, :],
                                       k.ps[:, 4 + i % 2, :].rearrange("p (b c n) -> p b c n", b=2, c=2)[:, :, 0:tb + 1, :],
                                       ACT.Copy)
                        act.activation(c_t[0:N_CMP, i % 4, :], k.ps[0:N_CMP, 2 + i % 2, 0:P], ACT.Copy)\
                           .then_inc(S["transposed_out"], 1)
                    if i:
                        h, tb, keys, half, j, tok = at(i - 1)
                        act.wait_ge(S["outputs_ready"], i)
                        act.activation(m["o"][half, j, tok], k.ps[half, 6 + (i - 1) % 2, 0:P], ACT.Copy)\
                           .then_inc(S["outputs_out"], 1)


def short_conv(k, m):
    S, stale = k.stage()
    pad = CONV2_TAPS - 1
    c, o = m["conv"], m["o"]
    with ExitStack() as ctx:
        z = k.sbuf(ctx, "conv_z", 4, T + pad)
        with k.nc.Block() as block:
            @block.sync
            def _(sp):
                clear(sp, stale)

            @block.vector
            def _(v):
                own = Steps(v, S["vector_steps"])
                own.did(v.memset(z[:, :, 0:pad], 0.0))
                own.did(v.tensor_tensor(z[:, :, pad:pad + T], c[:, 4:8, :], c[:, 8:12, :], ALU.mult))
                for tap in range(CONV2_TAPS):
                    own.settle()
                    for i in range(4):
                        w, x, y = k.column("l0_conv_w_2", CONV2_TAPS * i + tap), z[:, i, tap:tap + T], o[:, 4 + i, :]
                        if tap == 0:
                            own.did(v.tensor_scalar(y, x, w, k.column("l0_conv_b_2", i), ALU.mult, ALU.add))
                        else:
                            own.did(v.scalar_tensor_tensor(y, x, w, y, ALU.mult, ALU.add))
                own.settle()
                v.tensor_tensor(o[:, 4:8, :], o[:, 4:8, :], c[:, 0:4, :], ALU.mult)


def rwkv_mixer(k):
    with ExitStack() as ctx:
        sb = lambda name, *shape: k.sbuf(ctx, name, *shape)
        m = {"v_tok": sb("v_tok", TB, D), "g": sb("rwkv_g", KT, T), "bonus": sb("bonus", KT, T),
             "ar": sb("a_and_r", KT, TB, 2, P), "bk": sb("b_and_k", 2, KT, T), "carry": sb("carry", KT)}
        with ExitStack() as early:
            eb = lambda name, *shape: k.sbuf(early, name, *shape)
            m |= {"h": eb("h_shifted", KT, T + 1), "sig": eb("decay_sigmoid", KT, T), "a": eb("rwkv_a", KT, T),
                  "r": eb("rwkv_r", KT, T), "k": eb("rwkv_k", KT, T), "v": eb("rwkv_v", KT, T)}
            rmsnorm(k, k.x, "l1_mix_pre_g_2", m["h"][:, :, 1:T + 1])
            m["rkv"] = (m["r"], m["k"], m["v"])
            rwkv_project(k, m)
            rwkv_prepare(k, m)
        m["bk_tok"] = sb("bk_tok", 2, D)
        rwkv_transpose(k, m)
        rwkv_chunks(k, m)
        rwkv_norm(k, m)
        project_to(k, k.xn, m["g"])
        rmsnorm(k, m["g"], "l1_mix_post_g_2", k.x, residual=1)


def rwkv_project(k, m):
    S, stale = k.stage()
    first = k.w.taken
    MU = (1, 4, 5, 0, 2, 3)
    with ExitStack() as ctx:
        sb = lambda name, *shape: k.sbuf(ctx, name, *shape)
        down = [sb("w_dec1", KT, LORA), sb("w_a1", KT, LORA), sb("w_g1", KT, GATE_LORA)]
        up = [sb("w_dec2", D), sb("w_a2", D), sb("w_g2", D)]
        low = sb("lora_hidden", 3, T)
        delta, mix = k.xn, (m["bonus"], m["bk"][:, 0, :, :])
        width = (LORA, LORA, GATE_LORA)
        with k.nc.Block() as block:
            @block.sync
            def _(sp):
                clear(sp, stale)
                for n, name in enumerate(("dec", "a", "g")):
                    sp.dma_start(down[n][:, :, :], k.dram[f"w_{name}1"]).then_inc(S["lora_loaded"], 16)
                    sp.dma_start(up[n][0:width[n], :], k.dram[f"w_{name}2"]).then_inc(S["lora_loaded"], 16)
                k.w.load_ahead(sp, first, 3 * KT)

            @block.vector
            def _(v):
                own = Steps(v, S["vector_steps"])
                h = m["h"]
                own.did(v.memset(h[:, :, 0:1], 0.0))
                own.settle()
                own.did(v.tensor_tensor(delta[:, :, :], h[:, :, 0:T], h[:, :, 1:T + 1], ALU.subtract))
                own.settle()
                for n in range(6):
                    if 2 <= n < 5:
                        v.wait_ge(S["mix_used"], n - 1)
                    for t in range(KT):
                        last = v.scalar_tensor_tensor(mix[n % 2][:, t, :], delta[:, t, :],
                                                      k.column("l1_mu_2", KT * MU[n] + t), h[:, t, 1:T + 1],
                                                      ALU.mult, ALU.add)
                    last.then_inc(S["mixed"], 1)
                    if n >= 3:
                        out = m["rkv"[n - 3]]
                        for t in range(KT):
                            c = KT * (n - 3) + t
                            v.wait_ge(k.w.used, first + c + 1)
                            v.tensor_copy(out[:, t, :], k.ps[:, c % 4, 0:T]).then_inc(S["copied"], 1)

            @block.tensor
            def _(pe):
                pe.wait_ge(S["lora_loaded"], 6 * 16)
                for n in range(3):
                    pe.wait_ge(S["mixed"], n + 1)
                    for t in range(KT):
                        last = pe.matmul(k.ps[0:width[n], 4 + n % 2, 0:T], down[n][:, t, :], mix[n % 2][:, t, :],
                                         start=t == 0, stop=t == KT - 1)
                    last.then_inc(S["mix_used"], 1)
                    pe.wait_ge(S["low_ready"], n + 1)
                    for t in range(KT):
                        c = KT * n + t
                        if c >= 2:
                            pe.wait_ge(S["lora_out"], c - 1)
                        pe.matmul(k.ps[:, 6 + c % 2, 0:T], up[n][0:width[n], P * t:P * t + P], low[0:width[n], n, :],
                                  start=True, stop=True).then_inc(S["lora_ready"], 1)
                for c in range(3 * KT):
                    n = 3 + c // KT
                    pe.wait_ge(S["mixed"], n + 1)
                    if c >= 4:
                        pe.wait_ge(S["copied"], c - 3)
                    tiles = k.w.arrived(pe)
                    for t in range(KT):
                        last = pe.matmul(k.ps[:, c % 4, 0:T], tiles[:, t, :], mix[n % 2][:, t, :],
                                         start=t == 0, stop=t == KT - 1)
                    last.then_inc(k.w.used, 1)

            @block.scalar
            def _(act):
                for n in range(3):
                    act.wait_ge(S["mix_used"], n + 1)
                    act.activation(low[0:width[n], n, :], k.ps[0:width[n], 4 + n % 2, 0:T],
                                   (ACT.Tanh, ACT.Copy, ACT.Sigmoid)[n]).then_inc(S["low_ready"], 1)
                    for t in range(KT):
                        c = KT * n + t
                        act.wait_ge(S["lora_ready"], c + 1)
                        src = k.ps[:, 6 + c % 2, 0:T]
                        if n == 0:
                            ins = act.activation(m["sig"][:, t, :], src, ACT.Sigmoid, bias=k.column("l1_w0_2", t))
                        elif n == 1:
                            ins = act.activation(m["a"][:, t, :], src, ACT.Sigmoid, bias=k.column("l1_a0_2", t))
                        else:
                            ins = act.activation(m["g"][:, t, :], src, ACT.Copy)
                        ins.then_inc(S["lora_out"], 1)


def rwkv_prepare(k, m):
    S, stale = k.stage()
    RATE = -float(np.exp(-0.5))
    with ExitStack() as ctx:
        sb = lambda name, *shape: k.sbuf(ctx, name, *shape)
        kk, tmp, run = sb("kk", KT, T), sb("tmp", KT, T), k.xn
        before = sb("decay_before", KT, T)
        with k.nc.Block() as block:
            @block.sync
            def _(sp):
                clear(sp, stale)

            @block.vector
            def _(v):
                own = Steps(v, S["vector_steps"])
                for t in range(KT):
                    v.tensor_scalar(kk[:, t, :], m["k"][:, t, :], k.column("l1_k_k_2", t), None, ALU.mult)\
                     .then_inc(S["kk_raw"], 1)
                for t in range(KT):
                    own.did(v.tensor_scalar(before[:, t, :], m["a"][:, t, :], -1.0, k.column("l1_k_a_2", t),
                                            ALU.add, ALU.mult))
                own.settle()
                own.did(v.scalar_tensor_tensor(m["k"][:, :, :], before[:, :, :], 1.0, m["k"][:, :, :],
                                               ALU.add, ALU.mult))
                own.settle()
                v.wait_ge(S["sums"], 8)
                for t in range(KT):
                    v.wait_ge(S["sums"], t + 1)
                    own.did(v.tensor_scalar(before[:, t, :], k.ps[:, t, 0:T], 1e-12, None, ALU.max))
                    v.scalar_tensor_tensor(tmp[:, t, :], m["r"][:, t, :], k.column("l1_r_k_2", t),
                                           m["k"][:, t, :], ALU.mult, ALU.mult).then_inc(S["rk_ready"], 1)
                own.settle()
                for c in range(2 * KT):
                    t, b = c // 2, slice(P * (c % 2), P * (c % 2) + P)
                    own.did(v.tensor_tensor_scan(run[:, t, b], k.const("ones"), m["sig"][:, t, b], 0.0,
                                                 ALU.mult, ALU.add))
                own.settle()
                v.wait_ge(S["roots"], 1)
                own.did(v.reciprocal(before[:, :, :], before[:, :, :]))
                own.settle()
                own.did(v.tensor_tensor(kk[:, :, :], kk[:, :, :], before[:, :, :], ALU.mult))
                own.settle()
                own.did(v.tensor_tensor(m["a"][:, :, :], m["a"][:, :, :], kk[:, :, :], ALU.mult))
                own.did(v.tensor_tensor(m["carry"][:, :], run[:, :, P - 1], run[:, :, P + 63], ALU.add))
                own.settle()
                own.did(v.tensor_tensor(m["carry"][:, :], m["carry"][:, :], run[:, :, 63], ALU.subtract))
                own.did(v.tensor_copy(before[:, :, 0:2], run[:, :, :].rearrange("p k (b n) -> p k b n", b=TB)[:, :, :, 63]))
                own.settle()
                middle = before[:, :, 0:2].unsqueeze(3).broadcast_to([P, KT, TB, P])
                run4 = run[:, :, :].rearrange("p k (b n) -> p k b n", b=TB)
                own.did(v.tensor_tensor(run4, run4, middle, ALU.subtract))
                own.settle()
                v.tensor_tensor(before[:, :, :], run[:, :, :], m["sig"][:, :, :], ALU.subtract)\
                 .then_inc(S["exponents_ready"], 1)
                for t in range(KT):
                    v.wait_ge(S["bonus_sums"], t + 1)
                    v.tensor_tensor(m["bonus"][:, t, :], m["v"][:, t, :], k.ps[:, t, 0:T], ALU.mult)
                v.wait_ge(S["exps_ready"], 3)
                ar = m["ar"]
                c4 = lambda ap: ap.rearrange("p k (b n) -> p k b n", b=TB)
                v.tensor_tensor(ar[:, :, :, 0, :], c4(kk[:, :, :]), c4(before[:, :, :]), ALU.mult)
                v.tensor_tensor(ar[:, :, :, 1, :], c4(m["r"][:, :, :]), c4(run[:, :, :]), ALU.mult)
                v.tensor_tensor(m["bk"][:, 0, :, :], m["a"][:, :, :], tmp[:, :, :], ALU.mult)
                v.tensor_tensor(m["bk"][:, 1, :, :], m["k"][:, :, :], tmp[:, :, :], ALU.mult)

            @block.scalar
            def _(act):
                for t in range(KT):
                    act.wait_ge(S["kk_raw"], t + 1)
                    act.activation(tmp[:, t, :], kk[:, t, :], ACT.Square).then_inc(S["squares"], 1)
                act.wait_ge(S["rk_ready"], KT)
                act.activation(before[:, :, :], before[:, :, :], ACT.Sqrt).then_inc(S["roots"], 1)
                act.wait_ge(S["exponents_ready"], 1)
                act.wait_ge(S["bonus_sums"], KT)
                act.activation(tmp[:, :, :], run[:, :, :], ACT.Exp, scale=-RATE).then_inc(S["inverse_exp"], 1)
                act.wait_ge(S["inverse_exp"], 1)
                act.activation(run[:, :, :], run[:, :, :], ACT.Exp, scale=RATE).then_inc(S["exps_ready"], 1)
                act.activation(before[:, :, :], before[:, :, :], ACT.Exp, scale=RATE).then_inc(S["exps_ready"], 1)
                act.activation(m["carry"][:, :], m["carry"][:, :], ACT.Exp, scale=RATE).then_inc(S["exps_ready"], 1)

            @block.tensor
            def _(pe):
                for t in range(KT):
                    pe.wait_ge(S["squares"], t + 1)
                    pe.matmul(k.ps[:, t, 0:T], k.const("head_ones"), tmp[:, t, :], start=True, stop=True)\
                      .then_inc(S["sums"], 1)
                for t in range(KT):
                    pe.wait_ge(S["rk_ready"], t + 1)
                    pe.matmul(k.ps[:, t, 0:T], k.const("head_ones"), tmp[:, t, :], start=True, stop=True)\
                      .then_inc(S["bonus_sums"], 1)


def rwkv_transpose(k, m):
    S, stale = k.stage()
    jobs = [(m["v"], m["v_tok"][:, tb, :], tb) for tb in range(TB)] + \
           [(m["bk"][:, i, :, :], m["bk_tok"][:, i, :], 0) for i in range(2)]
    with k.nc.Block() as block:
        @block.sync
        def _(sp):
            clear(sp, stale)

        @block.tensor
        def _(pe):
            for n, (src, _, tb) in enumerate(jobs):
                for half in range(2):
                    for t in range(4):
                        last = pe.transpose(k.ps[:, 2 * n + half, P * t:P * t + P],
                                            src[:, 4 * half + t, P * tb:P * tb + P], k.const("identity"))
                    last.then_inc(S["transposed"], 1)

        @block.vector
        def _(v):
            for n, (_, dst, _) in enumerate(jobs):
                for half in range(2):
                    v.wait_ge(S["transposed"], 2 * n + half + 1)
                    v.tensor_copy(dst[:, 512 * half:512 * half + 512], k.ps[:, 2 * n + half, :])


def rwkv_chunks(k, m):
    with ExitStack() as ctx:
        sb = lambda name, *shape: k.sbuf(ctx, name, *shape)
        m["scores"] = sb("scores_t", RW_HEADS, 4, P)
        m["quad_mask"] = sb("quad_mask", 4, P)
        m["inverse"], m["inverse_t"] = sb("inverse", 4, 4, P), sb("inverse_t", 4, 4, P)
        m["level"], m["product"] = sb("level", 2, 4, P), sb("product", 2, 4, P)
        m["rhs"], m["x"] = sb("rhs", 2, RW_HEADS // 2, RW_DIM), sb("minus_x", RW_HEADS, RW_DIM)
        m["state"] = sb("rwkv_state", KT, RW_DIM)
        for tb in range(TB):
            rwkv_chunk(k, m, tb)


def rwkv_chunk(k, m, tb):
    S, stale = k.stage()
    H, W = RW_HEADS, RW_DIM
    tok = slice(P * tb, P * tb + P)
    sc, x, u = m["scores"], m["inverse"], m["inverse_t"]
    lt = sc[:, :, 0, :].rearrange("p (g h) n -> p g h n", h=4)
    half = lambda h: slice(64 * (h % 2), 64 * (h % 2) + 64)
    with k.nc.Block() as block:
        @block.sync
        def _(sp):
            clear(sp, stale)

        @block.gpsimd
        def _(pool):
            if tb == 0:
                pool.memset(sc[:, :, :, :], 0.0).then_inc(S["scores_cleared"], 1)

        @block.tensor
        def _(pe):
            for h in range(H):
                if h >= 2:
                    pe.wait_ge(S["scores_out"], h - 1)
                ar = m["ar"][half(h), h // 2, tb, :, :].rearrange("p a n -> p (a n)")
                for i in range(2):
                    last = pe.matmul(k.ps[:, 6 + h % 2, T * i:T * i + T], m["bk"][half(h), i, h // 2, tok], ar,
                                     start=True, stop=True)
                last.then_inc(S["scores_ready"], 1)
            invert_tensor(k, pe, S, lt, x, u, m["level"], m["product"], 4)
            pe.wait_ge(S["inverse_updated"], 4 * LEVELS)
            for h in range(H):
                out = k.ps[:, h % 2, W * (h // 2):W * (h // 2) + W]
                last = pe.matmul(out, sc[:, h, 2, :], m["v_tok"][:, tb, W * h:W * h + W], start=True, stop=tb == 0)
                if tb:
                    last = pe.matmul(out, m["ar"][half(h), h // 2, tb, 0, :], m["state"][half(h), h // 2, :],
                                     start=False, stop=True)
            last.then_inc(S["rhs_ready"], 1)
            pe.wait_ge(S["rhs_out"], 1)
            for h in range(H):
                last = pe.matmul(k.ps[:, 2 + h // 8, W * (h % 8):W * (h % 8) + W], u[:, h // 4, h % 4, :],
                                 m["rhs"][:, h % 2, h // 2, :], start=True, stop=True)
            last.then_inc(S["x_ready"], 1)
            pe.wait_ge(S["x_out"], 1)
            for h in range(H):
                j = h // 2
                out = k.ps[half(h), 4 + j // 4, P * (j % 4):P * (j % 4) + P]
                pe.matmul(out, m["x"][:, h, :], sc[:, h, 1, :], start=True, stop=False)
                last = pe.matmul(out, m["v_tok"][:, tb, W * h:W * h + W], sc[:, h, 3, :], start=False, stop=tb == 0)
                if tb:
                    last = pe.matmul(out, m["state"][half(h), j, :], m["ar"][half(h), j, tb, 1, :],
                                     start=False, stop=True)
            last.then_inc(S["outputs_ready"], 1)
            if tb == 0:
                for h in range(H):
                    out = k.ps[half(h), 6, W * (h // 2):W * (h // 2) + W]
                    pe.matmul(out, m["bk_tok"][:, 0, W * h:W * h + W], m["x"][:, h, :], start=True, stop=False)
                    last = pe.matmul(out, m["bk_tok"][:, 1, W * h:W * h + W], m["v_tok"][:, 0, W * h:W * h + W],
                                     start=False, stop=True)
                last.then_inc(S["state_ready"], 1)

        @block.scalar
        def _(act):
            invert_scalar(k, act, S, m["product"], 4)
            act.wait_ge(S["x_ready"], 1)
            for i in range(2):
                last = act.activation(m["x"][:, 8 * i:8 * i + 8, :].rearrange("p h n -> p (h n)"), k.ps[:, 2 + i, :],
                                      ACT.Copy, scale=-1.0)
            last.then_inc(S["x_out"], 1)
            act.wait_ge(S["outputs_ready"], 1)
            for i in range(2):
                act.activation(k.xn[:, 4 * i:4 * i + 4, tok], four(k.ps[:, 4 + i, :]), ACT.Copy)

        @block.vector
        def _(v):
            own = Steps(v, S["vector_steps"])
            if tb == 0:
                for i, name in enumerate(("strict", "upto", "strict", "upto")):
                    own.did(v.tensor_copy(m["quad_mask"][:, i, :], k.const(name)))
            for g in range(4):
                own.did(v.tensor_copy(x[:, g, :, :], over(k.const("identity"), 4)))
                own.did(v.tensor_copy(u[:, g, :, :], over(k.const("identity"), 4)))
            own.settle()
            if tb == 0:
                v.wait_ge(S["scores_cleared"], 1)
            for h in range(H):
                v.wait_ge(S["scores_ready"], h + 1)
                v.copy_predicated(sc[:, h, :, :], m["quad_mask"][:, :, :].bitcast(U32), four(k.ps[:, 6 + h % 2, :]))\
                 .then_inc(S["scores_out"], 1)
            v.wait_ge(S["scores_out"], H)
            invert_vector(k, v, S, lt, x, u, m["level"], 4)
            v.wait_ge(S["rhs_ready"], 1)
            for i in range(2):
                last = v.tensor_copy(m["rhs"][:, i, :, :].rearrange("p h n -> p (h n)"), k.ps[:, i, :])
            last.then_inc(S["rhs_out"], 1)
            if tb == 0:
                v.wait_ge(S["state_ready"], 1)
                v.tensor_tensor(m["state"][:, :, :], k.ps[:, 6, :].rearrange("p (k n) -> p k n", n=W),
                                m["carry"][:, :].unsqueeze(2).broadcast_to([P, KT, W]), ALU.mult)


def rwkv_norm(k, m):
    S, stale = k.stage()
    y = k.xn
    with ExitStack() as ctx:
        tmp = k.sbuf(ctx, "tmp", KT, T)
        with k.nc.Block() as block:
            @block.sync
            def _(sp):
                clear(sp, stale)

            @block.tensor
            def _(pe):
                for t in range(KT):
                    pe.matmul(k.ps[:, t, 0:T], k.const("head_ones"), y[:, t, :], start=True, stop=True)\
                      .then_inc(S["sums"], 1)
                for t in range(KT):
                    pe.wait_ge(S["squares"], t + 1)
                    pe.matmul(k.ps[:, t, 0:T], k.const("head_ones"), tmp[:, t, :], start=True, stop=True)\
                      .then_inc(S["square_sums"], 1)

            @block.scalar
            def _(act):
                for t in range(KT):
                    act.wait_ge(S["centred"], t + 1)
                    act.activation(tmp[:, t, :], y[:, t, :], ACT.Square).then_inc(S["squares"], 1)
                act.wait_ge(S["variances"], KT)
                act.activation(tmp[:, :, :], tmp[:, :, :], ACT.Sqrt).then_inc(S["roots"], 1)

            @block.vector
            def _(v):
                own = Steps(v, S["vector_steps"])
                for t in range(KT):
                    v.wait_ge(S["sums"], t + 1)
                    v.scalar_tensor_tensor(y[:, t, :], k.ps[:, t, 0:T], -1.0 / RW_DIM, y[:, t, :],
                                           ALU.mult, ALU.add).then_inc(S["centred"], 1)
                for t in range(KT):
                    v.wait_ge(S["square_sums"], t + 1)
                    v.tensor_scalar(tmp[:, t, :], k.ps[:, t, 0:T], 1.0 / RW_DIM, LNX_EPS, ALU.mult, ALU.add)\
                     .then_inc(S["variances"], 1)
                v.wait_ge(S["roots"], 1)
                own.did(v.reciprocal(tmp[:, :, :], tmp[:, :, :]))
                own.settle()
                own.did(v.tensor_tensor(y[:, :, :], y[:, :, :], tmp[:, :, :], ALU.mult))
                own.settle()
                for t in range(KT):
                    own.did(v.tensor_scalar(y[:, t, :], y[:, t, :], k.column("l1_lnx_g_2", t),
                                            k.column("l1_lnx_b_2", t), ALU.mult, ALU.add))
                own.settle()
                own.did(v.tensor_tensor(y[:, :, :], y[:, :, :], m["bonus"][:, :, :], ALU.add))
                own.settle()
                v.tensor_tensor(y[:, :, :], y[:, :, :], m["g"][:, :, :], ALU.mult)


def store_output(k):
    S, stale = k.stage()
    with k.nc.Block() as block:
        @block.sync
        def _(sp):
            clear(sp, stale)
            sp.dma_start(k.dram["out"], k.x[:, :, :]).then_inc(k.output_stored, 16)
            sp.wait_ge(k.output_stored, 16)


def build(nc, dram):
    with ExitStack() as ctx:
        k = Kernel(nc, ctx, dram)
        load_constants(k)
        token_mixer(k)
        cross_attention(k)
        peer(k)
        rmsnorm(k, k.x, "g_final", k.x)
        ffn(k, "l0_ffn1")
        nsa_mixer(k)
        ffn(k, "l0_ffn2")
        ffn(k, "l1_ffn1")
        rwkv_mixer(k)
        ffn(k, "l1_ffn2")
        store_output(k)



def features(a):
    return a.reshape(-1, KT, P).transpose(2, 1, 0)


def column_tiles(w):
    return w.reshape(KT, P, -1, P).transpose(2, 1, 0, 3)


def ffn_chunks(gate, up, down):
    g, u, d = column_tiles(gate), column_tiles(up), down.reshape(FT, P, KT, P)
    order = [g[0], u[0]]
    for f in range(1, FT):
        order += [g[f], u[f], d[f - 1]]
    return np.stack(order + [d[FT - 1]])


def layouts(a):
    first = {n: v[0] for n, v in a.items() if v.ndim > 1 and v.shape[0] == 1}
    out = {"x": features(first["x"]), "mem": features(first["mem"]), "consts": const_tiles()}

    columns = []
    for name, tiles in COLUMNS:
        v = first[name] if name in first else a[name]
        if name == "gdn_conv":
            columns.append(v.reshape(CONV_TAPS, 12, P).transpose(2, 1, 0).reshape(P, -1))
        elif name == "l0_conv_w_2":
            columns.append(v.reshape(CONV2_TAPS, 4, P).transpose(2, 1, 0).reshape(P, -1))
        else:
            columns.append(v.reshape(tiles, P).T)
    out["columns"] = np.concatenate(columns, axis=1)

    w = first["w_in"]
    sq, sk, sv, gq, gk, gv, gz = (w[:, 512 * i:512 * i + 512] for i in range(7))
    ba, gates = w[:, 3584:3592], w[:, 3592:]
    out["w_in"] = column_tiles(np.concatenate([gq, gk, gv, sq, sk, sv, gz, gates], axis=1))
    out["w_ba"] = ba.reshape(KT, P, 8).transpose(1, 0, 2)
    rows = np.concatenate([first["gdn_a_log"], first["gdn_dt_bias"]])
    out["gdn_rows"] = np.broadcast_to(rows, (P, 8))
    out["w_up_pair"] = np.concatenate([first[n].reshape(4, P, KT, P).transpose(2, 1, 0, 3)
                                       for n in ("w_sb_up", "w_gdn_up")], axis=2)
    for name in ("w_mix_out", "w_cq", "w_ckv", "w_co", "w_pq"):
        out[name] = column_tiles(first[name])
    out["subkeys"] = first["peer_subkeys"].reshape(2, KT, P, P).transpose(0, 3, 1, 2)
    out["peer_u"], out["peer_v"] = first["peer_u"], first["peer_v"]

    for f in ("l0_ffn1", "l0_ffn2", "l1_ffn1", "l1_ffn2"):
        out[f] = ffn_chunks(a[f"{f}_w_gate_2"], a[f"{f}_w_up_2"], a[f"{f}_w_down_2"])

    w = a["l0_w_in_2"]
    q = w[:, :512].reshape(D, 2, 4, 64).transpose(0, 2, 1, 3).reshape(D, 512)
    kc, vc, ks, vs, kw, vw = (w[:, 536 + P * i:664 + P * i] for i in range(6))
    out["l0_in"] = column_tiles(np.concatenate([q, kc, vc, ks, kw, vs, vw, w[:, 1304:]], axis=1))
    out["w_g"] = w[:, 512:536].reshape(KT, P, 24).transpose(1, 0, 2)
    w = a["l0_w_out_2"]
    nsa_rows = w[:512].reshape(2, 4, 64, D).transpose(1, 0, 2, 3).reshape(512, D)
    out["l0_out"] = column_tiles(np.concatenate([nsa_rows, w[512:]]))
    twice = lambda v: np.concatenate([v, v], axis=0)
    out["cmp_w1"] = np.stack([twice(a[f"l0_cmp_w1_{n}_2"].reshape(CMP_BLOCK, 64, P).transpose(1, 0, 2))
                              for n in "kv"], axis=1)
    out["cmp_w2"] = np.stack([a[f"l0_cmp_w2_{n}_2"] for n in "kv"], axis=1)
    out["cmp_pos"] = np.stack([twice(a[f"l0_cmp_pe_{n}_2"].T) for n in "kv"], axis=1)

    out["l1_rkv"] = np.concatenate([column_tiles(a[f"l1_w_{n}_2"]) for n in "rkv"])
    out["l1_o"] = column_tiles(a["l1_w_o_2"])
    for n in ("dec", "a", "g"):
        out[f"w_{n}1"] = a[f"l1_w_{n}1_2"].reshape(KT, P, -1).transpose(1, 0, 2)
        out[f"w_{n}2"] = a[f"l1_w_{n}2_2"]
    for name, n in STREAM:
        assert out[name].shape[0] == n, name
        out[name] = out[name].reshape(n, P, CHUNK)
    return {n: np.ascontiguousarray(v) for n, v in out.items()}


def kernel(**inputs):
    from concourse import bacc
    from concourse.bass_utils import run_bass_kernel_spmd

    arrays = layouts({n: np.asarray(v) for n, v in inputs.items()})
    nc = bacc.Bacc("TRN2", target_bir_lowering=False, num_devices=1)
    dram = {n: nc.dram_tensor(f"in_{n}", v.shape, mybir.dt.from_np(v.dtype), kind="ExternalInput").ap()
            for n, v in arrays.items()}
    dram["out"] = nc.dram_tensor("out_x", (P, KT, T), F32, kind="ExternalOutput").ap()
    build(nc, dram)
    result = run_bass_kernel_spmd(nc, [{f"in_{n}": v for n, v in arrays.items()}], core_ids=[0])
    x = np.asarray(result.results[0]["out_x"])
    return np.ascontiguousarray(x.transpose(2, 1, 0).reshape(1, T, D))
```

```python
from contextlib import ExitStack

import numpy as np

import concourse.bass as bass
from concourse import mybir

F32 = mybir.dt.float32
F32R = mybir.dt.float32r
U32 = mybir.dt.uint32
ACT = mybir.ActivationFunctionType
ALU = mybir.AluOpType
AX = mybir.AxisListType

P = 128
D = 1024
T = 256
KT = D // P
TB = T // P
EPS = 1e-6

SB_HEADS, SB_DIM = 8, 64
GDN_HEADS, GDN_DIM = 4, 128
CONV_TAPS = 4
X_HEADS, X_DIM = 4, 256
PEER_HEADS, PEER_KEYS, TOPK = 8, 128, 16
EXPERTS = PEER_KEYS * PEER_KEYS
SLOTS = PEER_HEADS * TOPK

D_FF = 2816
FT = D_FF // P
NSA_HEADS, NSA_GROUPS, NSA_DIM = 8, 2, 64
NSA_REP = NSA_HEADS // NSA_GROUPS
CMP_BLOCK, CMP_STRIDE = 32, 16
N_CMP = (T - CMP_BLOCK) // CMP_STRIDE + 1
CONV2_TAPS = 3
RW_HEADS, RW_DIM = 16, 64
LORA, GATE_LORA = 64, 128
LNX_EPS = 64e-5
NEG = -1e30
CLAMP = -1e20

RING = 5
SPLIT = 3
CHUNK = 8 * P
LEVELS = 7
GATHER_RING = 8

CONST_TILES = ["ones", "identity", "head_ones", "upto", "neg_suffix", "neg_ones", "strict",
               "negated_strict"] + [f"level{i}" for i in range(LEVELS)]
CONST_ROWS = CONST_TILES + ["causal0", "causal1a", "causal1b", "misc"]

COLUMNS = [("g_mix", 8), ("g_cross", 8), ("g_mem", 8), ("g_peer", 8), ("g_final", 8),
           ("gdn_norm_g", 1), ("gdn_conv", 12 * CONV_TAPS)]
for _l in ("l0", "l1"):
    for _f in ("ffn1", "ffn2", "mix"):
        COLUMNS += [(f"{_l}_{_f}_pre_g_2", 8), (f"{_l}_{_f}_post_g_2", 8)]
COLUMNS += [("l1_mu_2", 48), ("l1_w0_2", 8), ("l1_a0_2", 8), ("l1_k_k_2", 8), ("l1_k_a_2", 8),
            ("l1_r_k_2", 8), ("l1_lnx_g_2", 8), ("l1_lnx_b_2", 8),
            ("l0_conv_w_2", 4 * CONV2_TAPS), ("l0_conv_b_2", 4)]
COLUMN_AT = {}
for _n, _c in COLUMNS:
    COLUMN_AT[_n] = (sum(c for _, c in COLUMNS[:len(COLUMN_AT)]), _c)
N_COLUMNS = sum(c for _, c in COLUMNS)

STREAM = [("w_in", 44), ("w_up_pair", 8), ("w_mix_out", 8), ("w_cq", 8), ("w_ckv", 16),
          ("w_co", 8), ("w_pq", 16), ("l0_ffn1", 3 * FT), ("l0_in", 22),
          ("l0_out", 8), ("l0_ffn2", 3 * FT), ("l1_ffn1", 3 * FT), ("l1_rkv", 24),
          ("l1_o", 8), ("l1_ffn2", 3 * FT)]


def const_tiles():
    s, t = np.arange(P)[:, None], np.arange(P)[None, :]
    tiles = {
        "ones": np.ones((P, P)), "identity": s == t, "head_ones": s // 64 == t // 64,
        "upto": s <= t, "neg_suffix": -1.0 * (s >= t), "neg_ones": -np.ones((P, P)),
        "strict": s < t, "negated_strict": -1.0 * (s < t),
        "causal0": np.where(t <= s, t - s, NEG),
        "causal1a": t - (P + s) + 0.0,
        "causal1b": np.where(t <= s, t - s, NEG),
    }
    tiles["level0"] = (s // 2 == t // 2) & (s < t)
    for i in range(1, LEVELS):
        b = 1 << i
        tiles[f"level{i}"] = (s // (2 * b) == t // (2 * b)) & ((s // b) % 2 == 1) & ((t // b) % 2 == 0)
    misc = np.zeros((P, P))
    for tb in range(TB):
        ends = np.arange(N_CMP) * CMP_STRIDE + CMP_BLOCK - 1
        far = tb * P + np.arange(P)[:, None] - ends[None, :]
        misc[:, N_CMP * tb:N_CMP * (tb + 1)] = np.where(far >= 0, -far, NEG)
    misc[:, 32:48] = np.arange(16)[None, :]
    tiles["misc"] = misc
    return np.stack([np.asarray(tiles[n], np.float32) for n in CONST_ROWS], axis=1)


class Signals:

    def __init__(self, bank):
        self.bank, self.names = bank, {}

    def __getitem__(self, name):
        if name not in self.names:
            self.names[name] = self.bank[len(self.names)]
        return self.names[name]


class Steps:

    def __init__(self, engine, semaphore):
        self.engine, self.semaphore, self.count = engine, semaphore, 0

    def did(self, instruction):
        instruction.then_inc(self.semaphore, 1)
        self.count += 1

    def settle(self):
        self.engine.wait_ge(self.semaphore, self.count)


class Weights:

    def __init__(self, nc, ctx, dram):
        sb = lambda name, slots, dtype: ctx.enter_context(nc.sbuf_tensor(name, [P, slots, CHUNK], dtype))
        self.raw, self.high, self.low = sb("weights", RING, F32), sb("weights_high", SPLIT, F32R), sb("weights_low", SPLIT, F32R)
        self.filled = [ctx.enter_context(nc.semaphore(f"weights_filled{i}")) for i in range(RING)]
        self.rounded, self.split, self.used = (ctx.enter_context(nc.semaphore(f"weights_{n}"))
                                               for n in ("rounded", "split", "used"))
        self.plan = [dram[name][c] for name, n in STREAM for c in range(n)]
        self.loaded = self.n_rounded = self.n_split = self.taken = 0

    def load_ahead(self, sp, first, count):
        for c in range(self.loaded, min(first + count + SPLIT + RING, len(self.plan))):
            if c >= RING:
                sp.wait_ge(self.split, c - RING + 1)
            sp.dma_start(self.raw[:, c % RING, :], self.plan[c]).then_inc(self.filled[c % RING], 16)
            self.loaded = c + 1

    def round_high(self, act, used):
        for c in range(self.n_rounded, min(used + SPLIT, len(self.plan))):
            act.wait_ge(self.filled[c % RING], 16 * (c // RING + 1))
            if c >= SPLIT:
                act.wait_ge(self.used, c - SPLIT + 1)
            act.activation(self.high[:, c % SPLIT, :], self.raw[:, c % RING, :], ACT.Copy)\
               .then_inc(self.rounded, 1)
            self.n_rounded = c + 1

    def split_low(self, v, used):
        for c in range(self.n_split, min(used + SPLIT, len(self.plan))):
            v.wait_ge(self.rounded, c + 1)
            v.tensor_tensor(self.low[:, c % SPLIT, :], self.raw[:, c % RING, :],
                            self.high[:, c % SPLIT, :].bitcast(F32), ALU.subtract).then_inc(self.split, 1)
            self.n_split = c + 1

    def arrived(self, pe):
        c = self.taken
        self.taken += 1
        pe.wait_ge(self.split, c + 1)
        return Pair(*(part[:, c % SPLIT, :].rearrange("p (k n) -> p k n", n=P) for part in (self.high, self.low)))


class Pair:

    def __init__(self, high, low):
        self.high, self.low = high, low

    def __getitem__(self, at):
        return Pair(self.high[at], self.low[at])


def product(pe, out, lhs, rhs, start, stop):
    pe.matmul(out, lhs.high, rhs.high, start=start, stop=False)
    pe.matmul(out, lhs.high, rhs.low, start=False, stop=False)
    return pe.matmul(out, lhs.low, rhs.high, start=False, stop=stop)


class Kernel:

    def __init__(self, nc, ctx, dram):
        self.nc, self.ctx, self.dram = nc, ctx, dram
        self.banks = [[ctx.enter_context(nc.semaphore(f"stage{b}_{i}")) for i in range(56)]
                      for b in range(2)]
        self.stage_number, self.previous, self.tensors = 0, None, 0
        self.output_stored = ctx.enter_context(nc.semaphore("output_stored"))
        self.rows_ready = [ctx.enter_context(nc.semaphore(f"rows_ready{i}")) for i in range(GATHER_RING)]
        self.w = Weights(nc, ctx, dram)
        self.ps = ctx.enter_context(nc.psum_tensor("ps", [P, 8, 512], F32))
        self.consts = self.sbuf(ctx, "consts", len(CONST_ROWS), P)
        self.columns = self.sbuf(ctx, "columns", N_COLUMNS)
        self.x = self.sbuf(ctx, "x_residual", KT, T)
        self.xn = self.sbuf(ctx, "x_normed", KT, T)

    def sbuf(self, ctx, name, *shape, dtype=F32):
        self.tensors += 1
        return ctx.enter_context(self.nc.sbuf_tensor(f"{name}_{self.tensors}", [P, *shape], dtype))

    def pair(self, ctx, name, *shape):
        return Pair(self.sbuf(ctx, f"{name}_high", *shape, dtype=F32R), self.sbuf(ctx, f"{name}_low", *shape, dtype=F32R))

    def const(self, name):
        return self.consts[:, CONST_ROWS.index(name), :]

    def column(self, name, tile):
        at, _ = COLUMN_AT[name]
        return self.columns[:, at + tile:at + tile + 1]

    def stage(self):
        signals = Signals(self.banks[self.stage_number % 2])
        stale, self.previous = self.previous, signals
        self.stage_number += 1
        return signals, (stale.names.values() if stale else [])


def clear(sp, stale):
    for s in stale:
        sp.sem_clear(s)


def over(ap, n):
    return ap.unsqueeze(1).broadcast_to([ap.shape[0], n, ap.shape[1]])


def load_constants(k):
    S, stale = k.stage()
    with k.nc.Block() as block:
        @block.sync
        def _(sp):
            sp.dma_start(k.x[:, :, :], k.dram["x"]).then_inc(S["loads"], 16)
            sp.dma_start(k.consts[:, :, :], k.dram["consts"]).then_inc(S["loads"], 16)
            sp.dma_start(k.columns[:, :], k.dram["columns"]).then_inc(S["loads"], 16)
            k.w.load_ahead(sp, 0, 0)
            sp.wait_ge(S["loads"], 48)

        @block.scalar
        def _(act):
            k.w.round_high(act, 0)

        @block.vector
        def _(v):
            k.w.split_low(v, 0)


def rmsnorm(k, src, gain, dst, residual=False, parts=None):
    S, stale = k.stage()
    with ExitStack() as ctx:
        squares = k.sbuf(ctx, "squares", KT, T)
        scale = k.sbuf(ctx, "scale", 2, T)
        with k.nc.Block() as block:
            @block.sync
            def _(sp):
                clear(sp, stale)

            @block.scalar
            def _(act):
                for half in range(2):
                    part = slice(4 * half, 4 * half + 4)
                    act.activation(squares[:, part, :], src[:, part, :], ACT.Square)\
                       .then_inc(S["squares_ready"], 1)
                act.wait_ge(S["mean_ready"], 1)
                act.activation(scale[:, 1, :], scale[:, 0, :], ACT.Sqrt).then_inc(S["root_ready"], 1)
                if parts:
                    for half in range(2):
                        part = slice(4 * half, 4 * half + 4)
                        act.wait_ge(S["normed"], 4 * half + 4)
                        act.activation(parts.high[:, part, :], dst[:, part, :], ACT.Copy).then_inc(S["high_ready"], 1)

            @block.tensor
            def _(pe):
                for t in range(KT):
                    if t % 4 == 0:
                        pe.wait_ge(S["squares_ready"], t // 4 + 1)
                    last = pe.matmul(k.ps[:, 7, 0:T], k.const("ones"), squares[:, t, :],
                                     start=t == 0, stop=t == KT - 1)
                last.then_inc(S["sum_ready"], 1)

            @block.vector
            def _(v):
                own = Steps(v, S["vector_steps"])
                v.wait_ge(S["sum_ready"], 1)
                v.tensor_scalar(scale[:, 0, :], k.ps[:, 7, 0:T], 1.0 / D, EPS, ALU.mult, ALU.add)\
                 .then_inc(S["mean_ready"], 1)
                v.wait_ge(S["root_ready"], 1)
                own.did(v.reciprocal(scale[:, 0, :], scale[:, 1, :]))
                own.settle()
                if residual:
                    if residual != 1:
                        own.did(v.tensor_scalar(scale[:, 0, :], scale[:, 0, :], residual, None, ALU.mult))
                        own.settle()
                    own.did(v.tensor_tensor(squares[:, :, :], src[:, :, :], over(scale[:, 0, :], KT),
                                            ALU.mult))
                    own.settle()
                    for t in range(KT):
                        v.scalar_tensor_tensor(dst[:, t, :], squares[:, t, :], k.column(gain, t),
                                               dst[:, t, :], ALU.mult, ALU.add)
                else:
                    for t in range(KT):
                        v.scalar_tensor_tensor(dst[:, t, :], src[:, t, :], k.column(gain, t),
                                               scale[:, 0, :], ALU.mult, ALU.mult).then_inc(S["normed"], 1)
                    if parts:
                        v.wait_ge(S["normed"], KT)
                        for half in range(2):
                            part = slice(4 * half, 4 * half + 4)
                            v.wait_ge(S["high_ready"], half + 1)
                            v.tensor_tensor(parts.low[:, part, :], dst[:, part, :],
                                            parts.high[:, part, :].bitcast(F32), ALU.subtract)


def token_tiles(k, pe, bank, moving, tiles):
    for tb in range(TB):
        for t in range(KT):
            last = product(pe, k.ps[:, bank, P * tb:P * tb + P], moving[:, t, P * tb:P * tb + P],
                           tiles[:, t, :], start=t == 0, stop=t == KT - 1)
    last.then_inc(k.w.used, 1)


def feature_tiles(k, pe, bank, moving, tiles):
    for t in range(KT):
        last = product(pe, k.ps[:, bank, 0:T], tiles[:, t, :], moving[:, t, :], start=t == 0, stop=t == KT - 1)
    last.then_inc(k.w.used, 1)


def project_from(k, src, dst, parts, add):
    S, stale = k.stage()
    first = k.w.taken
    with k.nc.Block() as block:
        @block.sync
        def _(sp):
            clear(sp, stale)
            k.w.load_ahead(sp, first, KT)

        @block.scalar
        def _(act):
            for part in (slice(0, 4), slice(4, 8)):
                act.activation(parts.high[:, part, :], src[:, part, :], ACT.Copy).then_inc(S["high_ready"], 1)
            for i in range(KT):
                k.w.round_high(act, first + i + 1)

        @block.tensor
        def _(pe):
            for i in range(KT):
                if i >= 4:
                    pe.wait_ge(S["tile_out"], i - 3)
                tiles = k.w.arrived(pe)
                for t in range(KT):
                    if i == 0 and t % 4 == 0:
                        pe.wait_ge(S["low_ready"], t // 4 + 1)
                    last = product(pe, k.ps[:, i % 4, 0:T], tiles[:, t, :], parts[:, t, :],
                                   start=t == 0, stop=t == KT - 1)
                last.then_inc(k.w.used, 1)

        @block.vector
        def _(v):
            for half, part in enumerate((slice(0, 4), slice(4, 8))):
                v.wait_ge(S["high_ready"], half + 1)
                v.tensor_tensor(parts.low[:, part, :], src[:, part, :], parts.high[:, part, :].bitcast(F32),
                                ALU.subtract).then_inc(S["low_ready"], 1)
            for i in range(KT):
                v.wait_ge(k.w.used, first + i + 1)
                if add:
                    ins = v.tensor_tensor(dst[:, i, :], dst[:, i, :], k.ps[:, i % 4, 0:T], ALU.add)
                else:
                    ins = v.tensor_copy(dst[:, i, :], k.ps[:, i % 4, 0:T])
                ins.then_inc(S["tile_out"], 1)
                k.w.split_low(v, first + i + 1)


def project_in(k, m):
    S, stale = k.stage()
    first = k.w.taken
    n_copy, n_tok, n_silu, n_gate = 20, 4, 4, 16
    with k.nc.Block() as block:
        @block.sync
        def _(sp):
            clear(sp, stale)
            sp.dma_start(m["w_ba"][:, :, :], k.dram["w_ba"]).then_inc(S["small_loaded"], 16)
            sp.dma_start(m["rows"][:, :], k.dram["gdn_rows"]).then_inc(S["small_loaded"], 16)
            k.w.load_ahead(sp, first, 44)

        @block.tensor
        def _(pe):
            pe.wait_ge(S["small_loaded"], 32)
            for tb in range(TB):
                for t in range(KT):
                    last = pe.matmul(k.ps[:, 6, 8 * tb:8 * tb + 8], k.xn[:, t, P * tb:P * tb + P],
                                     m["w_ba"][:, t, :], start=t == 0, stop=t == KT - 1)
            last.then_inc(S["ba_ready"], 1)
            for i in range(44):
                if i >= 4:
                    if i - 4 < n_copy + n_tok:
                        pe.wait_ge(S["copied"], i - 3)
                    else:
                        pe.wait_ge(S["activated"], i - 3 - n_copy - n_tok)
                tiles = k.w.arrived(pe)
                put = token_tiles if n_copy <= i < n_copy + n_tok else feature_tiles
                put(k, pe, i % 4, m["parts"], tiles)

        @block.vector
        def _(v):
            own = Steps(v, S["vector_steps"])
            pad = CONV_TAPS - 1
            v.memset(m["conv_in"][:, :, 0:pad], 0.0)
            b, a = m["beta"], m["decay"]
            v.wait_ge(S["ba_ready"], 1)
            ba = k.ps[:, 6, 0:16].rearrange("p (b c) -> p b c", b=TB)
            v.tensor_copy(b[:, :, :], ba[:, :, 0:4]).then_inc(S["beta_in"], 1)
            own.did(v.tensor_tensor(a[:, 0], ba[:, :, 4:8], over(m["rows"][:, 4:8], TB), ALU.add))
            own.settle()
            own.did(v.tensor_scalar(a[:, 1], a[:, 0], -1.0, None, ALU.mult))
            own.settle()
            v.tensor_tensor(a[:, 2], a[:, 0], a[:, 1], ALU.min).then_inc(S["minus_abs"], 1)
            for i in range(n_copy + n_tok):
                v.wait_ge(k.w.used, first + i + 1)
                if i < 12:
                    out = m["conv_in"][:, i, pad:pad + T]
                elif i < n_copy:
                    out = m["sb_qk"][:, i - 12, :]
                else:
                    c = i - n_copy
                    out = m["sb_v"][:, :, P * c:P * c + P]
                src = k.ps[:, i % 4, 0:T]
                if i >= n_copy:
                    src = src.rearrange("p (b n) -> p b n", b=TB)
                v.tensor_copy(out, src).then_inc(S["copied"], 1)
                k.w.split_low(v, first + i + 1)
            v.wait_ge(S["softplus_log"], 1)
            own.did(v.scalar_tensor_tensor(a[:, 0], a[:, 0], 0.0, a[:, 2], ALU.max, ALU.add))
            own.settle()
            own.did(v.scalar_tensor_tensor(a[:, 1], a[:, 0], -1.0, over(m["rows"][:, 0:4], TB),
                                           ALU.mult, ALU.mult))
            for i in range(n_copy + n_tok, 44):
                k.w.split_low(v, first + i + 1)

        @block.scalar
        def _(act):
            a = m["decay"]
            act.wait_ge(S["small_loaded"], 32)
            act.activation(m["rows"][:, 0:4], m["rows"][:, 0:4], ACT.Exp)
            act.wait_ge(S["minus_abs"], 1)
            act.activation(a[:, 2], a[:, 2], ACT.Exp).then_inc(S["softplus_exp"], 1)
            act.wait_ge(S["softplus_exp"], 1)
            act.activation(a[:, 2], a[:, 2], ACT.Ln, bias=1.0).then_inc(S["softplus_log"], 1)
            for i in range(n_copy + n_tok):
                k.w.round_high(act, first + i + 1)
            for i in range(n_copy + n_tok, n_copy + n_tok + n_silu):
                act.wait_ge(k.w.used, first + i + 1)
                act.activation(m["z"][:, i - n_copy - n_tok, :], k.ps[:, i % 4, 0:T], ACT.Silu)\
                   .then_inc(S["activated"], 1)
                k.w.round_high(act, first + i + 1)
            act.wait_ge(S["beta_in"], 1)
            act.activation(m["beta"][:, :, :], m["beta"][:, :, :], ACT.Sigmoid)
            for i in range(28, 28 + n_gate):
                act.wait_ge(k.w.used, first + i + 1)
                act.activation(m["gates"][:, i - 28, :], k.ps[:, i % 4, 0:T], ACT.Sigmoid)\
                   .then_inc(S["activated"], 1)
                k.w.round_high(act, first + i + 1)


def stick_breaking(k, m):
    S, stale = k.stage()
    H, SEG = SB_HEADS, 3 * P
    with ExitStack() as ctx:
        z = k.sbuf(ctx, "z_scaled", H, SEG)
        w = k.sbuf(ctx, "softplus", H, SEG)
        a = k.sbuf(ctx, "weights", H, SEG)
        mask = k.sbuf(ctx, "segment_mask", SEG)

        def half(h):
            return slice(64 * (h % 2), 64 * (h % 2) + 64)

        with k.nc.Block() as block:
            @block.sync
            def _(sp):
                clear(sp, stale)

            @block.tensor
            def _(pe):
                for h in range(H):
                    if h >= 2:
                        pe.wait_ge(S["z_out"], h - 1)
                    q, kk = m["sb_qk"][half(h), h // 2, :], m["sb_qk"][half(h), 4 + h // 2, :]
                    pe.matmul(k.ps[:, h % 2, 0:T], kk[:, 0:P], q, start=True, stop=True)
                    pe.matmul(k.ps[:, h % 2, T:SEG], kk[:, P:T], q[:, P:T], start=True, stop=True)\
                      .then_inc(S["z_ready"], 1)
                for h in range(H):
                    pe.wait_ge(S["softplus_ready"], h + 1)
                    if h >= 2:
                        pe.wait_ge(S["logs_ready"], h - 1)
                    r = k.ps[:, 2 + h % 2, :]
                    pe.matmul(r[:, 0:P], k.const("neg_suffix"), w[:, h, 0:P], start=True, stop=True)
                    pe.matmul(r[:, P:T], k.const("neg_suffix"), w[:, h, P:T], start=True, stop=False)
                    pe.matmul(r[:, P:T], k.const("neg_ones"), w[:, h, T:SEG], start=False, stop=True)
                    pe.matmul(r[:, T:SEG], k.const("neg_suffix"), w[:, h, T:SEG], start=True, stop=True)\
                      .then_inc(S["sums_ready"], 1)
                for h in range(H):
                    pe.wait_ge(S["weights_ready"], h + 1)
                    if h >= 2:
                        pe.wait_ge(S["head_out"], h - 1)
                    o = k.ps[half(h), 4 + h % 2, :]
                    v0, v1 = (m["sb_v"][:, b, 64 * h:64 * h + 64] for b in range(TB))
                    pe.matmul(o[:, 0:P], v0, a[:, h, 0:P], start=True, stop=True)
                    pe.matmul(o[:, P:T], v0, a[:, h, P:T], start=True, stop=False)
                    pe.matmul(o[:, P:T], v1, a[:, h, T:SEG], start=False, stop=True)\
                      .then_inc(S["output_ready"], 1)

            @block.scalar
            def _(act):
                for h in range(H):
                    act.wait_ge(S["z_ready"], h + 1)
                    act.activation(z[:, h, :], k.ps[:, h % 2, 0:SEG], ACT.Copy, scale=SB_DIM ** -0.5)\
                       .then_inc(S["z_out"], 1)
                for h in range(H):
                    act.wait_ge(S["minus_abs"], h + 1)
                    act.activation(w[:, h, :], w[:, h, :], ACT.Exp).then_inc(S["exps"], 1)
                for h in range(H):
                    act.wait_ge(S["exps"], h + 1)
                    act.activation(w[:, h, :], w[:, h, :], ACT.Ln, bias=1.0).then_inc(S["log_ready"], 1)
                for h in range(H):
                    act.wait_ge(S["logs_ready"], h + 1)
                    act.activation(a[:, h, :], a[:, h, :], ACT.Exp).then_inc(S["exp_ready"], 1)
                for h in range(H):
                    act.wait_ge(S["output_ready"], h + 1)
                    act.activation(m["o_sb"][half(h), h // 2, :], k.ps[half(h), 4 + h % 2, 0:T], ACT.Copy)\
                       .then_inc(S["head_out"], 1)

            @block.vector
            def _(v):
                own = Steps(v, S["vector_steps"])
                own.did(v.tensor_copy(mask[:, 0:P], k.const("strict")))
                own.did(v.tensor_copy(mask[:, P:T], k.const("ones")))
                own.did(v.tensor_copy(mask[:, T:SEG], k.const("strict")))
                for h in range(H):
                    v.wait_ge(S["z_out"], h + 1)
                    own.did(v.tensor_scalar(w[:, h, :], z[:, h, :], -1.0, None, ALU.mult))
                    own.settle()
                    v.tensor_tensor(w[:, h, :], w[:, h, :], z[:, h, :], ALU.min)\
                     .then_inc(S["minus_abs"], 1)
                for h in range(H):
                    v.wait_ge(S["log_ready"], h + 1)
                    own.did(v.scalar_tensor_tensor(w[:, h, :], z[:, h, :], 0.0, w[:, h, :],
                                                   ALU.max, ALU.add))
                    own.settle()
                    v.tensor_tensor(w[:, h, :], w[:, h, :], mask[:, :], ALU.mult)\
                     .then_inc(S["softplus_ready"], 1)
                for h in range(H):
                    v.wait_ge(S["sums_ready"], h + 1)
                    v.tensor_tensor(a[:, h, :], z[:, h, :], k.ps[:, 2 + h % 2, 0:SEG], ALU.add)\
                     .then_inc(S["logs_ready"], 1)
                for h in range(H):
                    v.wait_ge(S["exp_ready"], h + 1)
                    v.scalar_tensor_tensor(a[:, h, :], a[:, h, :], 1.0, mask[:, :], ALU.min, ALU.mult)\
                     .then_inc(S["weights_ready"], 1)


def gdn_conv(k, m):
    S, stale = k.stage()
    y = m["qkv"]
    with ExitStack() as ctx:
        sq = k.sbuf(ctx, "squares", KT, T)
        with k.nc.Block() as block:
            @block.sync
            def _(sp):
                clear(sp, stale)

            @block.vector
            def _(v):
                own = Steps(v, S["vector_steps"])
                for group in range(3):
                    for tap in range(CONV_TAPS):
                        own.settle()
                        for i in range(4 * group, 4 * group + 4):
                            x = m["conv_in"][:, i, tap:tap + T]
                            g = k.column("gdn_conv", CONV_TAPS * i + tap)
                            if tap == 0:
                                ins = v.tensor_scalar(y[:, i, :], x, g, None, ALU.mult)
                            else:
                                ins = v.scalar_tensor_tensor(y[:, i, :], x, g, y[:, i, :], ALU.mult, ALU.add)
                            own.did(ins)
                for i in range(KT):
                    v.wait_ge(S["sums"], i + 1)
                    v.tensor_scalar(sq[:, i, :], k.ps[:, i % 8, 0:T], 1.0, EPS, ALU.mult, ALU.add)\
                     .then_inc(S["eps_added"], 1)
                v.wait_ge(S["roots"], 1)
                own.did(v.reciprocal(sq[:, :, :], sq[:, :, :]))
                own.settle()
                own.did(v.scalar_tensor_tensor(y[:, 0:4, :], y[:, 0:4, :], GDN_DIM ** -0.5, sq[:, 0:4, :],
                                               ALU.mult, ALU.mult))
                own.did(v.tensor_tensor(y[:, 4:8, :], y[:, 4:8, :], sq[:, 4:8, :], ALU.mult))

            @block.scalar
            def _(act):
                for group in range(3):
                    act.wait_ge(S["vector_steps"], 4 * CONV_TAPS * (group + 1))
                    act.activation(y[:, 4 * group:4 * group + 4, :], y[:, 4 * group:4 * group + 4, :],
                                   ACT.Silu).then_inc(S["silu"], 1)
                for group in range(2):
                    act.wait_ge(S["silu"], group + 1)
                    act.activation(sq[:, 4 * group:4 * group + 4, :], y[:, 4 * group:4 * group + 4, :],
                                   ACT.Square).then_inc(S["squares"], 1)
                act.wait_ge(S["eps_added"], KT)
                act.activation(sq[:, :, :], sq[:, :, :], ACT.Sqrt).then_inc(S["roots"], 1)

            @block.tensor
            def _(pe):
                for i in range(KT):
                    pe.wait_ge(S["squares"], i // 4 + 1)
                    pe.matmul(k.ps[:, i % 8, 0:T], k.const("ones"), sq[:, i, :], start=True, stop=True)\
                      .then_inc(S["sums"], 1)


def level_columns(ap, level, odd):
    return ap.rearrange("p h (n two b) -> p h n two b", two=2, b=1 << level)[:, :, :, int(odd), :]


def block_columns(ap, level, odd):
    return ap.rearrange("p (n two b) -> p n two b", two=2, b=1 << level)[:, :, int(odd), :]


START_BANKS = (1, 2, 4, 5)


def invert_tensor(k, pe, S, lt, x, u, pc, groups):
    n, size = (LEVELS - 1) * groups, u.shape[2]
    for g in range(groups):
        pe.wait_ge(S["level0"], g + 1)
        for h in range(size):
            last = pe.transpose(k.ps[:, START_BANKS[g], P * h:P * h + P], u[:, g, h, :], k.const("identity"))
        last.then_inc(S["level0_transposed"], 1)

    def product_step(i):
        g = i % groups
        if i < groups:
            pe.wait_ge(S["inverse_started"], i + 1)
        else:
            pe.wait_ge(S["inverse_updated"], i - groups + 1)
        if i >= 2:
            pe.wait_ge(S["product_masked"], i - 1)
        for h in range(size):
            last = pe.matmul(k.ps[:, 3 * (i % 2), P * h:P * h + P], lt[:, g, h, :], x[:, g, h, :],
                             start=True, stop=True)
        last.then_inc(S["product_ready"], 1)

    product_step(0)
    for i in range(n):
        g, level = i % groups, 1 + i // groups
        if i + 1 < n:
            product_step(i + 1)
        pe.wait_ge(S["product_masked"], i + 1)
        if i == 0:
            pe.wait_ge(S["inverse_started"], groups)
        if i >= 2:
            pe.wait_ge(S["inverse_updated"], i - 1)
        for h in range(size):
            half = slice(64 * h, 64 * h + 64)
            if level < LEVELS - 1:
                pe.matmul(k.ps[:, 3 * (i % 2) + 1, half], u[:, g, h, :], block_columns(pc[:, i % 2, h, :], level, 0),
                          start=True, stop=True)
            last = pe.matmul(k.ps[:, 3 * (i % 2) + 2, half], pc[:, i % 2, h, :],
                             block_columns(u[:, g, h, :], level, 1), start=True, stop=True)
        last.then_inc(S["updates_ready"], 1)


def invert_scalar(k, act, S, x, groups):
    size = x.shape[2]
    for g in range(groups):
        act.wait_ge(S["level0_transposed"], g + 1)
        act.activation(x[:, g, :, :], k.ps[:, START_BANKS[g], 0:P * size].rearrange("p (h n) -> p h n", n=P),
                       ACT.Copy).then_inc(S["inverse_started"], 1)


def level0(k, v, own, S, lt, u, g):
    size = u.shape[2]
    own.did(v.scalar_tensor_tensor(u[:, g, :, :], lt[:, g, :, :], -1.0, over(k.const("level0"), size),
                                   ALU.mult, ALU.mult))
    own.settle()
    v.tensor_tensor(u[:, g, :, :], u[:, g, :, :], over(k.const("identity"), size), ALU.add).then_inc(S["level0"], 1)


def invert_vector(k, v, S, x, u, pc, groups):
    n, size = (LEVELS - 1) * groups, u.shape[2]

    def mask_product(i):
        v.wait_ge(S["product_ready"], i + 1)
        if i >= 2:
            v.wait_ge(S["updates_ready"], i - 1)
        v.tensor_tensor(pc[:, i % 2, :, :], k.ps[:, 3 * (i % 2), 0:P * size].rearrange("p (h n) -> p h n", n=P),
                        over(k.const(f"level{1 + i // groups}"), size), ALU.mult).then_inc(S["product_masked"], 1)

    mask_product(0)
    for i in range(n):
        g, level = i % groups, 1 + i // groups
        if i + 1 < n:
            mask_product(i + 1)
        v.wait_ge(S["updates_ready"], i + 1)
        for odd, (dst, bank) in enumerate(((x, 1), (u, 2))):
            if odd or level < LEVELS - 1:
                part = level_columns(dst[:, g, :, :], level, odd)
                src = k.ps[:, 3 * (i % 2) + bank, 0:64 * size].rearrange("p (h n b) -> p h n b", h=size, b=1 << level)
                last = v.tensor_tensor(part, part, src, ALU.subtract)
        last.then_inc(S["inverse_updated"], 1)


def four(ap):
    return ap.rearrange("p (h n) -> p h n", h=4)


def gdn_chunks(k, m):
    S, stale = k.stage()
    H = GDN_HEADS
    q, kk, vv = (lambda h: m["qkv"][:, h, :]), (lambda h: m["qkv"][:, 4 + h, :]), (lambda h: m["qkv"][:, 8 + h, :])
    with ExitStack() as ctx:
        sb = lambda name, *shape: k.sbuf(ctx, name, *shape)
        wide_g, wide_b = sb("wide_g", 2, H, P), sb("wide_beta", 2, H, P)
        sums = sb("gc_columns", 2, H)
        edge = sb("exp_gc_columns", 2, H)
        decay = sb("decay_t", 2, H, P)
        grown = sb("exp_gc_rows", 2, H, P)
        lt, qk_t = sb("lt", 2, H, P), sb("qk_t", 2, H, P)
        x, pc = sb("inverse", 4, 2, P), sb("product", 2, 2, P)
        inverse_t = sb("inverse_t", 2, H, P)
        groups_of_two = lambda tile: tile[:, :, :, :].rearrange("p t (a b) n -> p (t a) b n", b=2)
        u, lt_groups = groups_of_two(inverse_t), groups_of_two(lt)
        k_beta, v_beta, k_dec = sb("k_beta", 2, H, P), sb("v_beta", 2, H, P), sb("k_dec", 2, H, P)
        w_t, uu = sb("w_t", H, P), sb("u", 2, H, P)
        q_dec, state = sb("q_dec", H, P), sb("state", H, P)

        with k.nc.Block() as block:
            @block.sync
            def _(sp):
                clear(sp, stale)

            @block.tensor
            def _(pe):
                for tb in range(TB):
                    tok = slice(P * tb, P * tb + P)
                    if tb:
                        pe.wait_ge(S["scores_read"], tb)
                    pe.wait_ge(S["wide"], tb + 1)
                    for h in range(H):
                        cols = slice(P * h, P * h + P)
                        pe.matmul(k.ps[:, 0, cols], wide_g[:, tb, h, :], k.const("upto"), start=True, stop=True)
                        pe.matmul(k.ps[:, 1, cols], wide_b[:, tb, h, :], k.const("identity"), start=True, stop=True)
                        pe.matmul(k.ps[:, 2, cols], kk(h)[:, tok], kk(h)[:, tok], start=True, stop=True)
                        pe.matmul(k.ps[:, 3, cols], kk(h)[:, tok], q(h)[:, tok], start=True, stop=True)
                    pe.matmul(k.ps[:, 4, 0:H], k.const("upto"), m["decay"][:, 1, tb, :],
                              start=True, stop=True).then_inc(S["scores_ready"], 1)
                for tb in range(TB):
                    tok = slice(P * tb, P * tb + P)
                    if tb:
                        pe.wait_ge(S["tokens_out"], tb)
                    for h in range(H):
                        cols = slice(P * h, P * h + P)
                        pe.transpose(k.ps[:, 6, cols], kk(h)[:, tok], k.const("identity"))
                        last = pe.transpose(k.ps[:, 7, cols], vv(h)[:, tok], k.const("identity"))
                    last.then_inc(S["tokens_ready"], 1)
                pe.wait_ge(S["scores_read"], TB)
                invert_tensor(k, pe, S, lt_groups, x, u, pc, 4)
                pe.wait_ge(S["tokens_out"], TB)
                pe.wait_ge(S["inverse_updated"], 4 * (LEVELS - 1))
                for h in range(H):
                    cols = slice(P * h, P * h + P)
                    pe.matmul(k.ps[:, 0, cols], inverse_t[:, 0, h, :], v_beta[:, 0, h, :], start=True, stop=True)
                    pe.matmul(k.ps[:, 1, cols], inverse_t[:, 1, h, :], v_beta[:, 1, h, :], start=True, stop=True)
                    last = pe.matmul(k.ps[:, 2, cols], k_beta[:, 1, h, :], inverse_t[:, 1, h, :], start=True, stop=True)
                last.then_inc(S["solved"], 1)
                pe.wait_ge(S["solution_out"], 1)
                for h in range(H):
                    cols = slice(P * h, P * h + P)
                    pe.matmul(k.ps[:, 3, cols], uu[:, 0, h, :], qk_t[:, 0, h, :], start=True, stop=True)
                    last = pe.matmul(k.ps[:, 4, cols], k_dec[:, 0, h, :], uu[:, 0, h, :], start=True, stop=True)
                last.then_inc(S["state_ready"], 1)
                pe.wait_ge(S["state_out"], 1)
                for h in range(H):
                    last = pe.matmul(k.ps[:, 5, P * h:P * h + P], w_t[:, h, :], state[:, h, :], start=True, stop=True)
                last.then_inc(S["recalled"], 1)
                pe.wait_ge(S["corrected"], 1)
                for h in range(H):
                    cols = slice(P * h, P * h + P)
                    pe.matmul(k.ps[:, 6, cols], state[:, h, :], q_dec[:, h, :], start=True, stop=False)
                    last = pe.matmul(k.ps[:, 6, cols], uu[:, 1, h, :], qk_t[:, 1, h, :], start=False, stop=True)
                last.then_inc(S["outputs_ready"], 1)

            @block.scalar
            def _(act):
                for tb in range(TB):
                    act.wait_ge(S["scores_ready"], tb + 1)
                    act.activation(grown[:, tb, :, :], four(k.ps[:, 0, :]), ACT.Exp)\
                       .then_inc(S["grown"], 1)
                    act.wait_ge(S["log_decay"], tb + 1)
                    act.activation(decay[:, tb, :, :], decay[:, tb, :, :], ACT.Exp).then_inc(S["decays"], 1)
                    act.activation(edge[:, tb, :], sums[:, tb, :], ACT.Exp).then_inc(S["decays"], 1)
                invert_scalar(k, act, S, x, 4)
                act.wait_ge(S["solved"], 1)
                act.activation(uu[:, 0, :, :], four(k.ps[:, 0, :]), ACT.Copy)
                act.activation(uu[:, 1, :, :], four(k.ps[:, 1, :]), ACT.Copy)
                act.activation(w_t[:, :, :], four(k.ps[:, 2, :]), ACT.Copy).then_inc(S["solution_out"], 1)
                act.wait_ge(S["state_ready"], 1)
                act.activation(state[:, :, :], four(k.ps[:, 4, :]), ACT.Copy).then_inc(S["state_out"], 1)
                act.activation(m["o_gdn"][:, :, 0:P], four(k.ps[:, 3, :]), ACT.Copy)
                act.wait_ge(S["outputs_ready"], 1)
                act.activation(m["o_gdn"][:, :, P:T], four(k.ps[:, 6, :]), ACT.Copy)

            @block.vector
            def _(v):
                own = Steps(v, S["vector_steps"])
                for tb in range(TB):
                    for h in range(H):
                        v.tensor_scalar(wide_g[:, tb, h, :], k.const("ones"), m["decay"][:, 1, tb, h:h + 1],
                                        None, ALU.mult)
                        last = v.tensor_scalar(wide_b[:, tb, h, :], k.const("ones"),
                                               m["beta"][:, tb, h:h + 1], None, ALU.mult)
                    last.then_inc(S["wide"], 1)
                for tb in range(TB):
                    v.wait_ge(S["scores_ready"], tb + 1)
                    own.did(v.tensor_copy(sums[:, tb, :], k.ps[:, 4, 0:H]))
                    own.settle()
                    v.wait_ge(S["grown"], tb + 1)
                    for h in range(H):
                        last = v.tensor_scalar(decay[:, tb, h, :], k.ps[:, 0, P * h:P * h + P],
                                               sums[:, tb, h:h + 1], 0.0, ALU.subtract, ALU.min)
                    last.then_inc(S["log_decay"], 1)
                    v.wait_ge(S["decays"], 2 * tb + 1)
                    own.did(v.tensor_tensor(lt[:, tb, :, :], four(k.ps[:, 2, :]), decay[:, tb, :, :], ALU.mult))
                    own.did(v.tensor_tensor(qk_t[:, tb, :, :], four(k.ps[:, 3, :]), decay[:, tb, :, :], ALU.mult))
                    own.settle()
                    own.did(v.tensor_tensor(lt[:, tb, :, :], lt[:, tb, :, :], four(k.ps[:, 1, :]), ALU.mult))
                    own.did(v.tensor_tensor(qk_t[:, tb, :, :], qk_t[:, tb, :, :], over(k.const("upto"), H), ALU.mult))
                    own.settle()
                    v.tensor_tensor(lt[:, tb, :, :], lt[:, tb, :, :], over(k.const("strict"), H), ALU.mult)\
                     .then_inc(S["scores_read"], 1)
                    v.wait_ge(S["scores_read"], tb + 1)
                    level0(k, v, own, S, lt_groups, u, 2 * tb)
                    level0(k, v, own, S, lt_groups, u, 2 * tb + 1)
                for tb in range(TB):
                    v.wait_ge(S["tokens_ready"], tb + 1)
                    v.wait_ge(S["decays"], 2 * tb + 2)
                    own.did(v.tensor_tensor(edge[:, tb, :], edge[:, tb, :], m["beta"][:, tb, :], ALU.mult))
                    own.settle()
                    for h in range(H):
                        cols = slice(P * h, P * h + P)
                        v.tensor_scalar(k_beta[:, tb, h, :], k.ps[:, 6, cols], edge[:, tb, h:h + 1], None, ALU.mult)
                        v.tensor_scalar(k_dec[:, tb, h, :], k.ps[:, 6, cols], decay[:, tb, h, P - 1:P], None, ALU.mult)
                        last = v.tensor_scalar(v_beta[:, tb, h, :], k.ps[:, 7, cols], m["beta"][:, tb, h:h + 1],
                                               None, ALU.mult)
                    last.then_inc(S["tokens_out"], 1)
                v.tensor_tensor(q_dec[:, :, :], m["qkv"][:, 0:4, P:T], grown[:, 1, :, :], ALU.mult)
                invert_vector(k, v, S, x, u, pc, 4)
                v.wait_ge(S["recalled"], 1)
                v.tensor_tensor(uu[:, 1, :, :], uu[:, 1, :, :], four(k.ps[:, 5, :]), ALU.subtract)\
                 .then_inc(S["corrected"], 1)


def gdn_gate(k, m):
    S, stale = k.stage()
    o = m["o_gdn"]
    with ExitStack() as ctx:
        sq = k.sbuf(ctx, "squares", 4, T)
        with k.nc.Block() as block:
            @block.sync
            def _(sp):
                clear(sp, stale)

            @block.scalar
            def _(act):
                act.activation(sq[:, :, :], o[:, :, :], ACT.Square).then_inc(S["squares"], 1)
                act.wait_ge(S["means"], 4)
                act.activation(sq[:, :, :], sq[:, :, :], ACT.Sqrt).then_inc(S["roots"], 1)

            @block.tensor
            def _(pe):
                pe.wait_ge(S["squares"], 1)
                for i in range(4):
                    pe.matmul(k.ps[:, i, 0:T], k.const("ones"), sq[:, i, :], start=True, stop=True)\
                      .then_inc(S["sums"], 1)

            @block.vector
            def _(v):
                own = Steps(v, S["vector_steps"])
                for i in range(4):
                    v.wait_ge(S["sums"], i + 1)
                    v.tensor_scalar(sq[:, i, :], k.ps[:, i, 0:T], 1.0 / GDN_DIM, EPS, ALU.mult, ALU.add)\
                     .then_inc(S["means"], 1)
                v.wait_ge(S["roots"], 1)
                own.did(v.reciprocal(sq[:, :, :], sq[:, :, :]))
                own.settle()
                own.did(v.scalar_tensor_tensor(o[:, :, :], o[:, :, :], k.column("gdn_norm_g", 0), sq[:, :, :],
                                               ALU.mult, ALU.mult))
                own.settle()
                v.tensor_tensor(o[:, :, :], o[:, :, :], m["z"][:, :, :], ALU.mult)


def merge_branches(k, m):
    S, stale = k.stage()
    first = k.w.taken
    with ExitStack() as ctx:
        part = k.sbuf(ctx, "gated", 2, T)
        with k.nc.Block() as block:
            @block.sync
            def _(sp):
                clear(sp, stale)
                k.w.load_ahead(sp, first, KT)

            @block.tensor
            def _(pe):
                for i in range(KT):
                    if i >= 4:
                        pe.wait_ge(S["tile_merged"], i - 3)
                    tiles = k.w.arrived(pe)
                    for b, src in enumerate((m["parts"][:, 0:4, :], m["parts"][:, 4:8, :])):
                        if i == 0:
                            pe.wait_ge(S["low_ready"], b + 1)
                        for t in range(4):
                            last = product(pe, k.ps[:, i % 4, T * b:T * b + T], tiles[:, 4 * b + t, :],
                                           src[:, t, :], start=t == 0, stop=t == 3)
                    last.then_inc(k.w.used, 1)

            @block.vector
            def _(v):
                own = Steps(v, S["vector_steps"])
                for b, src in enumerate((m["o_sb"], m["o_gdn"])):
                    v.wait_ge(S["high_ready"], b + 1)
                    part_b = slice(4 * b, 4 * b + 4)
                    v.tensor_tensor(m["parts"].low[:, part_b, :], src[:, :, :],
                                    m["parts"].high[:, part_b, :].bitcast(F32), ALU.subtract)\
                     .then_inc(S["low_ready"], 1)
                for i in range(KT):
                    v.wait_ge(k.w.used, first + i + 1)
                    if i:
                        v.wait_ge(S["tile_merged"], i)
                    for b in range(2):
                        own.did(v.tensor_tensor(part[:, b, :], m["gates"][:, KT * b + i, :],
                                                k.ps[:, i % 4, T * b:T * b + T], ALU.mult))
                    own.settle()
                    v.tensor_tensor(k.xn[:, i, :], part[:, 0, :], part[:, 1, :], ALU.add)\
                     .then_inc(S["tile_merged"], 1)
                    k.w.split_low(v, first + i + 1)

            @block.scalar
            def _(act):
                for b, src in enumerate((m["o_sb"], m["o_gdn"])):
                    act.activation(m["parts"].high[:, 4 * b:4 * b + 4, :], src[:, :, :], ACT.Copy)\
                       .then_inc(S["high_ready"], 1)
                for i in range(KT):
                    k.w.round_high(act, first + i + 1)


def token_mixer(k):
    with ExitStack() as ctx:
        sb = lambda name, *shape: k.sbuf(ctx, name, *shape)
        m = {"parts": k.pair(ctx, "moving", KT, T), "w_ba": sb("w_ba", KT, 8), "rows": sb("gdn_rows", 8),
             "beta": sb("beta", TB, 4), "decay": sb("decay", 3, TB, 4),
             "z": sb("z_silu", 4, T), "o_sb": sb("o_sb", 4, T), "o_gdn": sb("o_gdn", 4, T),
             "gates": sb("gates", 16, T), "qkv": sb("qkv", 12, T)}
        with ExitStack() as early:
            eb = lambda name, *shape: k.sbuf(early, name, *shape)
            m |= {"sb_qk": eb("sb_qk", 8, T), "sb_v": eb("sb_v", TB, 512),
                  "conv_in": eb("conv_in", 12, T + CONV_TAPS - 1)}
            rmsnorm(k, k.x, "g_mix", k.xn, parts=m["parts"])
            project_in(k, m)
            stick_breaking(k, m)
            gdn_conv(k, m)
        gdn_chunks(k, m)
        gdn_gate(k, m)
        merge_branches(k, m)
        project_from(k, k.xn, k.x, m["parts"], add=True)


def cross_attention(k):
    with ExitStack() as ctx:
        q, kk = k.sbuf(ctx, "xq", KT, T), k.sbuf(ctx, "xk", KT, T)
        v_tok, o = k.sbuf(ctx, "xv", TB, D), k.sbuf(ctx, "xo", KT, T)
        mem = k.sbuf(ctx, "mem", KT, T)
        parts, mem_parts = k.pair(ctx, "moving", KT, T), k.pair(ctx, "moving_mem", KT, T)
        load_memory(k, mem)
        rmsnorm(k, mem, "g_mem", mem, parts=mem_parts)
        rmsnorm(k, k.x, "g_cross", k.xn, parts=parts)
        cross_project(k, q, kk, v_tok, parts, mem_parts)
        cross_heads(k, q, kk, v_tok, o)
        project_from(k, o, k.x, parts, add=True)


def load_memory(k, mem):
    S, stale = k.stage()
    with k.nc.Block() as block:
        @block.sync
        def _(sp):
            clear(sp, stale)
            sp.dma_start(mem[:, :, :], k.dram["mem"]).then_inc(S["loaded"], 16)
            sp.wait_ge(S["loaded"], 16)


def cross_project(k, q, kk, v_tok, parts, mem_parts):
    S, stale = k.stage()
    first = k.w.taken
    with k.nc.Block() as block:
        @block.sync
        def _(sp):
            clear(sp, stale)
            k.w.load_ahead(sp, first, 3 * KT)

        @block.tensor
        def _(pe):
            for i in range(3 * KT):
                if i >= 4:
                    pe.wait_ge(S["copied"], i - 3)
                tiles = k.w.arrived(pe)
                if i < 2 * KT:
                    feature_tiles(k, pe, i % 4, parts if i < KT else mem_parts, tiles)
                else:
                    token_tiles(k, pe, i % 4, mem_parts, tiles)

        @block.scalar
        def _(act):
            for i in range(3 * KT):
                k.w.round_high(act, first + i + 1)

        @block.vector
        def _(v):
            for i in range(3 * KT):
                v.wait_ge(k.w.used, first + i + 1)
                src = k.ps[:, i % 4, 0:T]
                if i < KT:
                    out = q[:, i, :]
                elif i < 2 * KT:
                    out = kk[:, i - KT, :]
                else:
                    c = i - 2 * KT
                    out, src = v_tok[:, :, P * c:P * c + P], src.rearrange("p (b n) -> p b n", b=TB)
                v.tensor_copy(out, src).then_inc(S["copied"], 1)
                k.w.split_low(v, first + i + 1)


def cross_heads(k, q, kk, v_tok, o):
    S, stale = k.stage()
    N = X_HEADS * TB
    with ExitStack() as ctx:
        p = k.sbuf(ctx, "probs", N, T)
        p_t = k.sbuf(ctx, "probs_t", X_HEADS, TB, T)
        top, total = k.sbuf(ctx, "row_max", N), k.sbuf(ctx, "row_sum", N)
        with k.nc.Block() as block:
            @block.sync
            def _(sp):
                clear(sp, stale)

            @block.tensor
            def _(pe):
                for i in range(N):
                    h, tb = i // TB, i % TB
                    if i >= 4:
                        pe.wait_ge(S["scores_out"], i - 3)
                    for c in range(2):
                        last = pe.matmul(k.ps[:, i % 4, 0:T], q[:, 2 * h + c, P * tb:P * tb + P],
                                         kk[:, 2 * h + c, :], start=c == 0, stop=c == 1)
                    last.then_inc(S["scores_ready"], 1)
                for i in range(N):
                    h, tb = i // TB, i % TB
                    pe.wait_ge(S["probs_ready"], i + 1)
                    if i >= 2:
                        pe.wait_ge(S["transposed_out"], i - 1)
                    for mb in range(TB):
                        last = pe.transpose(k.ps[:, 4 + i % 2, P * mb:P * mb + P],
                                            p[:, i, P * mb:P * mb + P], k.const("identity"))
                    last.then_inc(S["transposed"], 1)
                for h in range(X_HEADS):
                    pe.wait_ge(S["transposed_out"], TB * (h + 1))
                    for c in range(2):
                        n = 2 * h + c
                        if n >= 2:
                            pe.wait_ge(S["outputs_out"], n - 1)
                        for mb in range(TB):
                            last = pe.matmul(k.ps[:, 6 + n % 2, 0:T], v_tok[:, mb, P * n:P * n + P],
                                             p_t[:, h, mb, :], start=mb == 0, stop=mb == 1)
                        last.then_inc(S["outputs_ready"], 1)

            @block.vector
            def _(v):
                own = Steps(v, S["vector_steps"])
                for i in range(N):
                    v.wait_ge(S["scores_ready"], i + 1)
                    own.did(v.reduce_max(top[:, i:i + 1], k.ps[:, i % 4, 0:T], AX.X))
                    own.settle()
                    v.tensor_scalar(top[:, i:i + 1], top[:, i:i + 1], -X_DIM ** -0.5, None, ALU.mult)\
                     .then_inc(S["max_ready"], 1)
                for i in range(N):
                    v.wait_ge(S["scores_out"], i + 1)
                    own.did(v.reciprocal(total[:, i:i + 1], total[:, i:i + 1]))
                    own.settle()
                    v.tensor_scalar(p[:, i, :], p[:, i, :], total[:, i:i + 1], None, ALU.mult)\
                     .then_inc(S["probs_ready"], 1)
                for i in range(N):
                    h, tb = i // TB, i % TB
                    v.wait_ge(S["transposed"], i + 1)
                    v.tensor_copy(p_t[:, h, :, P * tb:P * tb + P],
                                  k.ps[:, 4 + i % 2, 0:T].rearrange("p (b n) -> p b n", b=TB))\
                     .then_inc(S["transposed_out"], 1)

            @block.scalar
            def _(act):
                for i in range(N):
                    act.wait_ge(S["max_ready"], i + 1)
                    act.activation(p[:, i, :], k.ps[:, i % 4, 0:T], ACT.Exp, bias=top[:, i:i + 1],
                                   scale=X_DIM ** -0.5, accum_out=total[:, i:i + 1])\
                       .then_inc(S["scores_out"], 1)
                for n in range(KT):
                    act.wait_ge(S["outputs_ready"], n + 1)
                    act.activation(o[:, n, :], k.ps[:, 6 + n % 2, 0:T], ACT.Copy)\
                       .then_inc(S["outputs_out"], 1)


def peer(k):
    with ExitStack() as ctx:
        tokens = k.sbuf(ctx, "x_tokens", TB, D)
        experts = k.sbuf(ctx, "experts", TB, SLOTS, dtype=U32)
        gates = k.sbuf(ctx, "expert_gates", TB, SLOTS)
        with ExitStack() as early:
            eb = lambda name, *shape, dtype=F32: k.sbuf(early, name, *shape, dtype=dtype)
            parts = k.pair(early, "moving", KT, T)
            top = eb("top", TB, 2 * PEER_HEADS, TOPK)
            top_at = eb("top_at", TB, 2 * PEER_HEADS, TOPK, dtype=U32)
            rmsnorm(k, k.x, "g_peer", k.xn, parts=parts)
            peer_keys(k, parts, tokens, top, top_at)
            peer_route(k, top, top_at, experts, gates)
        peer_experts(k, tokens, experts, gates)


def peer_keys(k, parts, tokens, top, top_at):
    S, stale = k.stage()
    first = k.w.taken
    N = 2 * PEER_HEADS
    with ExitStack() as ctx:
        q = k.sbuf(ctx, "peer_q", 2, T)
        keys = k.sbuf(ctx, "subkeys", N, PEER_KEYS)
        scores, spare = (k.sbuf(ctx, n, 2, TB, PEER_KEYS) for n in ("key_scores", "key_scores_spare"))
        with k.nc.Block() as block:
            @block.sync
            def _(sp):
                clear(sp, stale)
                sp.dma_start(keys[:, :, :], k.dram["subkeys"]).then_inc(S["keys_loaded"], 16)
                k.w.load_ahead(sp, first, N)

            @block.tensor
            def _(pe):
                for i in range(N + 1):
                    if i < N:
                        if i >= 2:
                            pe.wait_ge(S["queries_out"], i - 1)
                        feature_tiles(k, pe, i % 2, parts, k.w.arrived(pe))
                    if i == 0:
                        pe.wait_ge(S["keys_loaded"], 16)
                    else:
                        n = i - 1
                        pe.wait_ge(S["queries_out"], n + 1)
                        if n >= 2:
                            pe.wait_ge(S["scores_out"], n - 1)
                        for tb in range(TB):
                            last = pe.matmul(k.ps[:, 2 + n % 2, P * tb:P * tb + P], q[:, n % 2, P * tb:P * tb + P],
                                             keys[:, n, :], start=True, stop=True)
                        last.then_inc(S["scores_ready"], 1)
                for i in range(4):
                    for t in range(4):
                        last = pe.transpose(k.ps[:, 4 + i, P * t:P * t + P],
                                            k.xn[:, 4 * (i % 2) + t, P * (i // 2):P * (i // 2) + P],
                                            k.const("identity"))
                    last.then_inc(S["transposed"], 1)

            @block.scalar
            def _(act):
                for i in range(N + 1):
                    if i < N:
                        act.wait_ge(k.w.used, first + i + 1)
                        if i >= 2:
                            act.wait_ge(S["scores_ready"], i - 1)
                        act.activation(q[:, i % 2, :], k.ps[:, i % 2, 0:T], ACT.Copy).then_inc(S["queries_out"], 1)
                        k.w.round_high(act, first + i + 1)
                    if i:
                        act.wait_ge(S["scores_ready"], i)
                        if i >= 3:
                            act.wait_ge(S["tops_found"], i - 2)
                        act.activation(scores[:, (i - 1) % 2, :, :], k.ps[:, 2 + (i - 1) % 2, 0:T]
                                       .rearrange("p (b n) -> p b n", b=TB), ACT.Copy).then_inc(S["scores_out"], 1)
                for i in range(4):
                    act.wait_ge(S["transposed"], i + 1)
                    act.activation(tokens[:, i // 2, 512 * (i % 2):512 * (i % 2) + 512], k.ps[:, 4 + i, :],
                                   ACT.Copy)

            @block.vector
            def _(v):
                own = Steps(v, S["vector_steps"])
                k.w.split_low(v, first + 1)
                for i in range(N):
                    k.w.split_low(v, first + min(i + 2, N))
                    v.wait_ge(S["scores_out"], i + 1)
                    top16(v, own, lambda tb: scores[:, i % 2, tb, :], lambda tb: spare[:, i % 2, tb, :],
                          lambda tb: top[:, tb, i, :], lambda tb: top_at[:, tb, i, :], TB, S["tops_found"])


def top16(v, own, values, spare, top, index, count, found=None):
    for i in range(count):
        own.did(v.max(top(i)[:, 0:8], values(i)))
    own.settle()
    for i in range(count):
        own.did(v.max_index(index(i)[:, 0:8], top(i)[:, 0:8], values(i)))
        own.did(v.match_replace(spare(i), top(i)[:, 0:8], values(i), -3e38))
    own.settle()
    for i in range(count):
        own.did(v.max(top(i)[:, 8:16], spare(i)))
    own.settle()
    for i in range(count):
        last = v.max_index(index(i)[:, 8:16], top(i)[:, 8:16], spare(i))
        if found is not None and i == count - 1:
            last.then_inc(found, 1)
        else:
            own.did(last)
    if found is None:
        own.settle()


def peer_route(k, tops, tops_at, experts, gates):
    S, stale = k.stage()
    H, K = PEER_HEADS, TOPK
    with ExitStack() as ctx:
        sb = lambda name, *shape, dtype=F32: k.sbuf(ctx, name, *shape, dtype=dtype)
        top_n = sb("top_numbers", 2 * H, K)
        sums, sums_spare = sb("pair_sums", H, K * K), sb("pair_sums_spare", H, K * K)
        best, best_at = sb("best", H, K), sb("best_at", H, K, dtype=U32)
        place = sb("best_place", 2, H * K, dtype=U32)
        place_f = sb("best_place_f", 2, H * K)
        hot = sb("one_hot", H * K, K)
        key = sb("key_numbers", 2, H * K)
        total = sb("gate_sum", H)
        iota = k.const("misc")[:, 32:48]
        with k.nc.Block() as block:
            @block.sync
            def _(sp):
                clear(sp, stale)

            @block.scalar
            def _(act):
                for tb in range(TB):
                    act.wait_ge(S["shifted"], tb + 1)
                    act.activation(gates[:, tb, :], gates[:, tb, :], ACT.Exp).then_inc(S["gate_exps"], 1)

            @block.vector
            def _(v):
                own = Steps(v, S["vector_steps"])
                for tb in range(TB):
                    own.did(v.tensor_copy(top_n[:, :, :], tops_at[:, tb, :, :]))
                    halves = tops[:, tb, :, :].rearrange("p (h two) i -> p h two i", two=2)
                    a = halves[:, :, 0, :].unsqueeze(3).broadcast_to([P, H, K, K])
                    b = halves[:, :, 1, :].unsqueeze(2).broadcast_to([P, H, K, K])
                    own.did(v.tensor_tensor(sums[:, :, :].rearrange("p h (i j) -> p h i j", i=K), a, b, ALU.add))
                    own.settle()
                    top16(v, own, lambda i: sums[:, i, :], lambda i: sums_spare[:, i, :],
                          lambda i: best[:, i, :], lambda i: best_at[:, i, :], H)
                    shifted = gates[:, tb, :].rearrange("p (h i) -> p h i", h=H)
                    v.tensor_tensor(shifted, best[:, :, :], best[:, :, 0:1].broadcast_to([P, H, K]), ALU.subtract)\
                     .then_inc(S["shifted"], 1)
                    flat_at = best_at[:, :, :].rearrange("p h i -> p (h i)")
                    own.did(v.tensor_scalar(place[:, 0, :], flat_at, 4, None, ALU.logical_shift_right))
                    own.did(v.tensor_scalar(place[:, 1, :], flat_at, K - 1, None, ALU.bitwise_and))
                    own.settle()
                    own.did(v.tensor_copy(place_f[:, :, :], place[:, :, :]))
                    own.settle()
                    numbers = top_n[:, :, :].rearrange("p (h two) i -> p h two i", two=2)
                    hot4 = hot[:, :, :].rearrange("p (h n) j -> p h n j", h=H)
                    for part in range(2):
                        own.did(v.tensor_tensor(hot[:, :, :], place_f[:, part, :].unsqueeze(2).broadcast_to([P, H * K, K]),
                                                over(iota, H * K), ALU.is_equal))
                        own.settle()
                        own.did(v.tensor_tensor(hot4, hot4, numbers[:, :, part, :].unsqueeze(2).broadcast_to([P, H, K, K]),
                                                ALU.mult))
                        own.settle()
                        own.did(v.tensor_reduce(key[:, part, :], hot[:, :, :], AX.X, ALU.add))
                        own.settle()
                    own.did(v.scalar_tensor_tensor(key[:, 0, :], key[:, 0, :], float(PEER_KEYS), key[:, 1, :],
                                                   ALU.mult, ALU.add))
                    own.settle()
                    own.did(v.tensor_copy(experts[:, tb, :], key[:, 0, :]))
                    v.wait_ge(S["gate_exps"], tb + 1)
                    own.did(v.tensor_reduce(total[:, :], shifted, AX.X, ALU.add))
                    own.settle()
                    own.did(v.reciprocal(total[:, :], total[:, :]))
                    own.settle()
                    own.did(v.tensor_tensor(shifted, shifted, total[:, :].unsqueeze(2).broadcast_to([P, H, K]),
                                            ALU.mult))


def peer_experts(k, tokens, experts, gates):
    S, stale = k.stage()
    R = GATHER_RING
    with ExitStack() as ctx:
        rows = k.sbuf(ctx, "expert_rows", R, D)
        dots = k.sbuf(ctx, "expert_dots", TB, SLOTS)
        waste = k.sbuf(ctx, "products", 2, D)
        out = k.sbuf(ctx, "expert_sums", TB, 2, D)
        gathers = [(table, tb, s) for table in ("peer_u", "peer_v") for tb in range(TB) for s in range(SLOTS)]
        rows_ready = k.rows_ready
        with k.nc.Block() as block:
            @block.sync
            def _(sp):
                clear(sp, stale)

            @block.gpsimd
            def _(pool):
                for i, (table, tb, s) in enumerate(gathers):
                    if i >= R:
                        pool.wait_ge(S["rows_used"], i - R + 1)
                    pool.indirect_dma_start(
                        out=rows[:, i % R, :], out_offset=None, in_=k.dram[table],
                        in_offset=bass.IndirectOffsetOnAxis(ap=experts[:, tb, s:s + 1], axis=0),
                    ).then_inc(rows_ready[i % R], 16)

            @block.scalar
            def _(act):
                for tb in range(TB):
                    act.wait_ge(S["rows_used"], SLOTS * (tb + 1))
                    act.activation(dots[:, tb, :], dots[:, tb, :], ACT.Gelu).then_inc(S["gelus"], 1)

            @block.vector
            def _(v):
                for i, (table, tb, s) in enumerate(gathers):
                    v.wait_ge(rows_ready[i % R], 16 * (i // R + 1))
                    row = rows[:, i % R, :]
                    if table == "peer_u":
                        if i >= 2:
                            v.wait_ge(S["rows_used"], i - 1)
                        v.tensor_tensor_reduce(out=waste[:, i % 2, :], in0=row, in1=tokens[:, tb, :], scale=1.0,
                                               scalar=0.0, op0=ALU.mult, op1=ALU.add,
                                               accum_out=dots[:, tb, s:s + 1]).then_inc(S["rows_used"], 1)
                        continue
                    if s == 0:
                        v.wait_ge(S["gelus"], tb + 1)
                        v.tensor_tensor(gates[:, tb, :], gates[:, tb, :], dots[:, tb, :], ALU.mult)\
                         .then_inc(S["weighted"], 1)
                        v.wait_ge(S["weighted"], tb + 1)
                    acc = out[:, tb, s % 2, :]
                    if s < 2:
                        ins = v.tensor_scalar(acc, row, gates[:, tb, s:s + 1], None, ALU.mult)
                    else:
                        v.wait_ge(S["rows_used"], i - 1)
                        ins = v.scalar_tensor_tensor(acc, row, gates[:, tb, s:s + 1], acc, ALU.mult, ALU.add)
                    ins.then_inc(S["rows_used"], 1)
                    if s == SLOTS - 1:
                        v.wait_ge(S["rows_used"], i + 1)
                        v.tensor_tensor(out[:, tb, 0, :], out[:, tb, 0, :], out[:, tb, 1, :], ALU.add)\
                         .then_inc(S["sums_ready"], 1)
                for tb in range(TB):
                    for half in range(2):
                        v.wait_ge(S["transposed"], 2 * tb + half + 1)
                        part = k.x[:, 4 * half:4 * half + 4, P * tb:P * tb + P]
                        v.tensor_tensor(part, part, four(k.ps[:, 2 * tb + half, :]), ALU.add)

            @block.tensor
            def _(pe):
                for tb in range(TB):
                    pe.wait_ge(S["sums_ready"], tb + 1)
                    for half in range(2):
                        for t in range(4):
                            at = P * (4 * half + t)
                            last = pe.transpose(k.ps[:, 2 * tb + half, P * t:P * t + P],
                                                out[:, tb, 0, at:at + P], k.const("identity"))
                        last.then_inc(S["transposed"], 1)


def ffn(k, name):
    S, stale = k.stage()
    first = k.w.taken

    def up_done(f):
        return first + 2 * (f + 1) + max(f - 1, 0)

    with ExitStack() as ctx:
        sb = lambda name, *shape: k.sbuf(ctx, name, *shape)
        x_parts, h_parts = k.pair(ctx, "moving", KT, T), k.pair(ctx, "hidden", 2, T)
        gate, up, hidden = sb("gate", 2, T), sb("up", 2, T), sb("hidden_full", 2, T)
        squares, y, scale = sb("squares", KT, T), sb("ffn_out", KT, T), sb("inverse_rms", 3, T)
        acc = k.ps[:, 4:8, :].rearrange("p b (two n) -> p (b two) n", two=2)
        with k.nc.Block() as block:
            @block.sync
            def _(sp):
                clear(sp, stale)
                k.w.load_ahead(sp, first, 3 * FT)

            @block.tensor
            def _(pe):
                def down(f):
                    tiles = k.w.arrived(pe)
                    pe.wait_ge(S["hidden_ready"], f + 1)
                    moving = h_parts[:, f % 2, :]
                    for o in range(KT):
                        for n, (w, m) in enumerate(((tiles.high, moving.high), (tiles.high, moving.low),
                                                    (tiles.low, moving.high))):
                            last = pe.matmul(acc[:, o, :], w[:, o, :], m, start=f == n == 0 and o % 2 == 0,
                                             stop=f == FT - 1 and n == 2, skip_group_check=True)
                    last.then_inc(k.w.used, 1)

                for f in range(FT):
                    if f >= 2:
                        pe.wait_ge(S["hidden_ready"], f - 1)
                    for b in range(2):
                        tiles = k.w.arrived(pe)
                        for t in range(KT):
                            if f == b == 0:
                                pe.wait_ge(S["parts_ready"], t + 1)
                            last = product(pe, k.ps[:, 2 * (f % 2) + b, 0:T], tiles[:, t, :], x_parts[:, t, :],
                                           start=t == 0, stop=t == KT - 1)
                        last.then_inc(k.w.used, 1)
                        if f == b == 0:
                            for t in range(KT):
                                if t % 4 == 0:
                                    pe.wait_ge(S["squares_ready"], t // 4 + 1)
                                last = pe.matmul(k.ps[:, 4, 0:T], k.const("ones"), squares[:, t, :],
                                                 start=t == 0, stop=t == KT - 1)
                            last.then_inc(S["sum_ready"], 1)
                    if f:
                        down(f - 1)
                down(FT - 1)
                for t in range(KT):
                    if t % 2 == 0:
                        pe.wait_ge(S["squares_ready"], 2 + t // 2 + 1)
                    last = pe.matmul(k.ps[:, 0, 0:T], k.const("ones"), squares[:, t, :],
                                     start=t == 0, stop=t == KT - 1)
                last.then_inc(S["sum_ready"], 1)

            @block.scalar
            def _(act):
                for half in range(2):
                    part = slice(4 * half, 4 * half + 4)
                    act.activation(squares[:, part, :], k.x[:, part, :], ACT.Square)\
                       .then_inc(S["squares_ready"], 1)
                k.w.round_high(act, first + 1)
                act.wait_ge(S["mean_ready"], 1)
                act.activation(scale[:, 1, :], scale[:, 0, :], ACT.Sqrt).then_inc(S["root_ready"], 1)
                for f in range(FT):
                    act.wait_ge(S["gate_scaled"], f + 1)
                    act.activation(gate[:, f % 2, :], gate[:, f % 2, :], ACT.Silu).then_inc(S["gate_ready"], 1)
                    k.w.round_high(act, up_done(f + 1) if f + 1 < FT else first + 3 * FT)
                for b in range(4):
                    act.wait_ge(k.w.used, first + 3 * FT)
                    act.activation(squares[:, 2 * b:2 * b + 2, :], acc[:, 2 * b:2 * b + 2, :], ACT.Square)\
                       .then_inc(S["squares_ready"], 1)
                act.wait_ge(S["mean_ready"], 2)
                act.activation(scale[:, 1, :], scale[:, 0, :], ACT.Sqrt).then_inc(S["root_ready"], 1)

            @block.vector
            def _(v):
                own = Steps(v, S["vector_steps"])
                for t in range(KT):
                    g = k.column(f"{name}_pre_g_2", t)
                    own.did(v.tensor_scalar(x_parts.high[:, t, :], k.x[:, t, :], g, None, ALU.mult))
                    own.settle()
                    v.scalar_tensor_tensor(x_parts.low[:, t, :], k.x[:, t, :], g, x_parts.high[:, t, :].bitcast(F32),
                                           ALU.mult, ALU.subtract).then_inc(S["parts_ready"], 1)
                k.w.split_low(v, first + 1)

                def inverse_rms(n, bank, factor):
                    v.wait_ge(S["sum_ready"], n)
                    v.tensor_scalar(scale[:, 0, :], k.ps[:, bank, 0:T], 1.0 / D, EPS, ALU.mult, ALU.add)\
                     .then_inc(S["mean_ready"], 1)
                    v.wait_ge(S["root_ready"], n)
                    own.did(v.reciprocal(scale[:, 2, :], scale[:, 1, :]))
                    own.settle()
                    if factor != 1:
                        own.did(v.tensor_scalar(scale[:, 2, :], scale[:, 2, :], factor, None, ALU.mult))
                        own.settle()

                inverse_rms(1, 4, 1)
                for f in range(FT):
                    v.wait_ge(k.w.used, up_done(f) - 1)
                    v.tensor_tensor(gate[:, f % 2, :], k.ps[:, 2 * (f % 2), 0:T], scale[:, 2, :], ALU.mult)\
                     .then_inc(S["gate_scaled"], 1)
                    k.w.split_low(v, up_done(f) - 1)
                    v.wait_ge(k.w.used, up_done(f))
                    own.did(v.tensor_tensor(up[:, f % 2, :], k.ps[:, 2 * (f % 2) + 1, 0:T], scale[:, 2, :], ALU.mult))
                    own.settle()
                    v.wait_ge(S["gate_ready"], f + 1)
                    own.did(v.tensor_tensor(hidden[:, f % 2, :], gate[:, f % 2, :], up[:, f % 2, :], ALU.mult))
                    own.settle()
                    if f >= 2:
                        v.wait_ge(k.w.used, first + 3 * (f - 2) + 5)
                    own.did(v.tensor_copy(h_parts.high[:, f % 2, :], hidden[:, f % 2, :]))
                    own.settle()
                    v.tensor_tensor(h_parts.low[:, f % 2, :], hidden[:, f % 2, :],
                                    h_parts.high[:, f % 2, :].bitcast(F32), ALU.subtract)\
                     .then_inc(S["hidden_ready"], 1)
                    k.w.split_low(v, up_done(f))
                    if f + 1 < FT:
                        k.w.split_low(v, up_done(f) + (f > 0))
                k.w.split_low(v, first + 3 * FT)
                for t in range(KT):
                    v.wait_ge(S["squares_ready"], 2 + t // 2 + 1)
                    own.did(v.tensor_scalar(y[:, t, :], acc[:, t, :], k.column(f"{name}_post_g_2", t), None, ALU.mult))
                inverse_rms(2, 0, 0.5)
                for half in range(2):
                    part = slice(4 * half, 4 * half + 4)
                    own.did(v.tensor_tensor(y[:, part, :], y[:, part, :], over(scale[:, 2, :], 4), ALU.mult))
                own.settle()
                v.tensor_tensor(k.x[:, :, :], k.x[:, :, :], y[:, :, :], ALU.add)


def nsa_mixer(k):
    with ExitStack() as ctx:
        sb = lambda name, *shape: k.sbuf(ctx, name, *shape)
        m = {"q": sb("nsa_q", 4, T), "cmp_in": sb("cmp_in", 2, T), "k_sw": sb("nsa_k", 2, T),
             "v_sw": sb("nsa_v", TB, 2, P), "conv": sb("conv_in2", 12, T), "w_g": sb("w_g", KT, 24),
             "gates": sb("nsa_gates", TB, 24), "o": sb("nsa_o", KT, T),
             "kc": sb("kc", N_CMP), "vc": sb("vc", P), "parts": k.pair(ctx, "moving", KT, T)}
        rmsnorm(k, k.x, "l0_mix_pre_g_2", k.xn, parts=m["parts"])
        nsa_project(k, m)
        nsa_compress(k, m)
        nsa_heads(k, m)
        short_conv(k, m)
        project_from(k, m["o"], k.xn, m["parts"], add=False)
        rmsnorm(k, k.xn, "l0_mix_post_g_2", k.x, residual=1)


def nsa_project(k, m):
    S, stale = k.stage()
    first = k.w.taken
    with k.nc.Block() as block:
        @block.sync
        def _(sp):
            clear(sp, stale)
            sp.dma_start(m["w_g"][:, :, :], k.dram["w_g"]).then_inc(S["small_loaded"], 16)
            k.w.load_ahead(sp, first, 22)

        @block.tensor
        def _(pe):
            pe.wait_ge(S["small_loaded"], 16)
            for tb in range(TB):
                for t in range(KT):
                    last = pe.matmul(k.ps[:, 6, 24 * tb:24 * tb + 24], k.xn[:, t, P * tb:P * tb + P],
                                     m["w_g"][:, t, :], start=t == 0, stop=t == KT - 1)
            last.then_inc(S["gates_ready"], 1)
            for i in range(22):
                if i >= 4:
                    pe.wait_ge(S["copied"], i - 3)
                (token_tiles if i in (8, 9) else feature_tiles)(k, pe, i % 4, m["parts"], k.w.arrived(pe))

        @block.scalar
        def _(act):
            act.wait_ge(S["gates_ready"], 1)
            act.activation(m["gates"][:, :, :], k.ps[:, 6, 0:48].rearrange("p (b n) -> p b n", b=TB), ACT.Sigmoid)
            for i in range(22):
                k.w.round_high(act, first + i + 1)

        @block.vector
        def _(v):
            for i in range(22):
                v.wait_ge(k.w.used, first + i + 1)
                src = k.ps[:, i % 4, 0:T]
                if i < 4:
                    ins = v.tensor_scalar(m["q"][:, i, :], src, NSA_DIM ** -0.5, None, ALU.mult)
                elif i < 8:
                    ins = v.tensor_copy(m["cmp_in" if i < 6 else "k_sw"][:, i % 2, :], src)
                elif i < 10:
                    ins = v.tensor_copy(m["v_sw"][:, :, i - 8, :], src.rearrange("p (b n) -> p b n", b=TB))
                else:
                    ins = v.tensor_copy(m["conv"][:, i - 10, :], src)
                ins.then_inc(S["copied"], 1)
                k.w.split_low(v, first + i + 1)


def nsa_compress(k, m):
    S, stale = k.stage()
    L, HALF = CMP_BLOCK, CMP_STRIDE
    with ExitStack() as ctx:
        sb = lambda name, *shape: k.sbuf(ctx, name, *shape)
        w1, w2, pos = sb("cmp_w1", 2, L, P), sb("cmp_w2", 2, NSA_DIM), sb("cmp_pos", 2, L)
        blocks, hidden = sb("cmp_blocks", 2, L, N_CMP), sb("cmp_hidden", 4, N_CMP)
        with k.nc.Block() as block:
            @block.sync
            def _(sp):
                clear(sp, stale)
                sp.dma_start(pos[:, :, :], k.dram["cmp_pos"]).then_inc(S["pos_loaded"], 16)
                sp.dma_start(w1[:, :, :, :], k.dram["cmp_w1"]).then_inc(S["w1_loaded"], 16)
                sp.dma_start(w2[:, :, :], k.dram["cmp_w2"]).then_inc(S["w2_loaded"], 16)

            @block.vector
            def _(v):
                v.wait_ge(S["pos_loaded"], 16)
                for kv in range(2):
                    strided = m["cmp_in"][:, kv, :].rearrange("p (n s) -> p s n", s=HALF)
                    for a in range(2):
                        part = slice(HALF * a, HALF * a + HALF)
                        v.tensor_tensor(blocks[:, kv, part, :], strided[:, :, a:a + N_CMP],
                                        pos[:, kv, part].unsqueeze(2).broadcast_to([P, HALF, N_CMP]), ALU.add)\
                         .then_inc(S["blocks_ready"], 1)
                v.wait_ge(S["keys_ready"], 1)
                for g in range(NSA_GROUPS):
                    half = slice(64 * g, 64 * g + 64)
                    v.tensor_copy(m["kc"][half, :], k.ps[half, 4 + g, 0:N_CMP])
                v.tensor_copy(m["vc"][0:N_CMP, :], k.ps[0:N_CMP, 6, 0:P])

            @block.tensor
            def _(pe):
                pe.wait_ge(S["w1_loaded"], 16)
                for kv in range(2):
                    pe.wait_ge(S["blocks_ready"], 2 * kv + 2)
                    for g in range(NSA_GROUPS):
                        half = slice(64 * g, 64 * g + 64)
                        for i in range(L):
                            last = pe.matmul(k.ps[:, 2 * kv + g, 0:N_CMP], w1[half, kv, i, :], blocks[half, kv, i, :],
                                             start=i == 0, stop=i == L - 1)
                        last.then_inc(S["hidden_ready"], 1)
                pe.wait_ge(S["w2_loaded"], 16)
                pe.wait_ge(S["gelus"], 4)
                for g in range(NSA_GROUPS):
                    pe.matmul(k.ps[64 * g:64 * g + 64, 4 + g, 0:N_CMP], w2[:, 0, :], hidden[:, g, :],
                              start=True, stop=True)
                    last = pe.matmul(k.ps[0:N_CMP, 6, 64 * g:64 * g + 64], hidden[:, 2 + g, :], w2[:, 1, :],
                                     start=True, stop=True)
                last.then_inc(S["keys_ready"], 1)

            @block.scalar
            def _(act):
                for i in range(4):
                    act.wait_ge(S["hidden_ready"], i + 1)
                    act.activation(hidden[:, i, :], k.ps[:, i, 0:N_CMP], ACT.Gelu_apprx_tanh)\
                       .then_inc(S["gelus"], 1)


def nsa_heads(k, m):
    S, stale = k.stage()
    N = NSA_HEADS * TB
    CMP = 2 * T
    with ExitStack() as ctx:
        p = k.sbuf(ctx, "nsa_probs", N, CMP + 16)
        p_t = k.sbuf(ctx, "nsa_probs_t", 4, 4, P)
        c_t = k.sbuf(ctx, "nsa_cmp_t", 4, P)
        top, total = k.sbuf(ctx, "nsa_max", N, 3), k.sbuf(ctx, "nsa_sum", N, 3)

        def at(i):
            h, tb = i // TB, i % TB
            g = h // NSA_REP
            return h, tb, P * (tb + 1), slice(64 * g, 64 * g + 64), h % NSA_REP, slice(P * tb, P * tb + P)

        def wide(i, ap):
            return ap.rearrange("p (two n) -> p two n", two=2)[:, :, 0:at(i)[2]]

        with k.nc.Block() as block:
            @block.sync
            def _(sp):
                clear(sp, stale)

            @block.tensor
            def _(pe):
                for i in range(N):
                    h, tb, keys, half, j, tok = at(i)
                    if i >= 2:
                        pe.wait_ge(S["biased"], i - 1)
                    q = m["q"][half, j, tok]
                    for b in range(2):
                        pe.matmul(k.ps[:, i % 2, T * b:T * b + keys], q, m["k_sw"][half, b, 0:keys],
                                  start=True, stop=True)
                    pe.matmul(k.ps[:, 2 + i % 2, 0:N_CMP], q, m["kc"][half, :], start=True, stop=True)\
                      .then_inc(S["scores_ready"], 1)
                pe.wait_ge(S["biased"], N)
                for i in range(N + 1):
                    if i < N:
                        h, tb, keys, half, j, tok = at(i)
                        pe.wait_ge(S["probs_ready"], i + 1)
                        if i >= 2:
                            pe.wait_ge(S["transposed_out"], i - 1)
                        for b in range(2):
                            for c in range(tb + 1):
                                pe.transpose(k.ps[:, 4 + i % 2, P * (2 * b + c):P * (2 * b + c) + P],
                                             p[:, i, T * b + P * c:T * b + P * c + P], k.const("identity"))
                        pe.transpose(k.ps[0:N_CMP, 2 + i % 2, 0:P], p[:, i, CMP:CMP + N_CMP],
                                     k.const("identity")).then_inc(S["transposed"], 1)
                    if i:
                        n = i - 1
                        h, tb, keys, half, j, tok = at(n)
                        pe.wait_ge(S["transposed_out"], n + 1)
                        if n >= 2:
                            pe.wait_ge(S["outputs_out"], n - 1)
                        out = k.ps[half, 6 + n % 2, 0:P]
                        pe.matmul(out, m["vc"][0:N_CMP, half], c_t[0:N_CMP, n % 4, :], start=True, stop=False)
                        for b in range(2):
                            for c in range(tb + 1):
                                last = pe.matmul(out, m["v_sw"][:, c, b, half], p_t[:, n % 4, 2 * b + c, :],
                                                 start=False, stop=b == 1 and c == tb)
                        last.then_inc(S["outputs_ready"], 1)

            @block.vector
            def _(v):
                own = Steps(v, S["vector_steps"])
                for i in range(N):
                    h, tb, keys, half, j, tok = at(i)
                    slope = 2.0 ** -(h + 1)
                    v.wait_ge(S["scores_ready"], i + 1)
                    delta = k.consts[:, CONST_ROWS.index("causal0"), :] if tb == 0 else \
                        k.consts[:, CONST_ROWS.index("causal1a"):CONST_ROWS.index("causal1b") + 1, :]\
                         .rearrange("p a n -> p (a n)")
                    far = k.const("misc")[:, N_CMP * tb:N_CMP * tb + N_CMP]
                    v.scalar_tensor_tensor(wide(i, p[:, i, 0:CMP]), over(delta, 2), slope,
                                           wide(i, k.ps[:, i % 2, :]), ALU.mult, ALU.add)
                    v.scalar_tensor_tensor(p[:, i, CMP:CMP + N_CMP], far, slope, k.ps[:, 2 + i % 2, 0:N_CMP],
                                           ALU.mult, ALU.add).then_inc(S["biased"], 1)
                    v.wait_ge(S["biased"], i + 1)
                    own.did(v.reduce_max(top[:, i, 1:3], wide(i, p[:, i, 0:CMP]), AX.X))
                    own.did(v.reduce_max(top[:, i, 0:1], p[:, i, CMP:CMP + N_CMP], AX.X))
                    own.settle()
                    v.tensor_scalar(top[:, i, :], top[:, i, :], CLAMP, -1.0, ALU.max, ALU.mult)\
                     .then_inc(S["max_ready"], 1)
                for i in range(N):
                    h, tb, keys, half, j, tok = at(i)
                    v.wait_ge(S["exps_ready"], i + 1)
                    own.did(v.tensor_scalar(total[:, i, :], total[:, i, :], 1e-30, None, ALU.max))
                    own.settle()
                    own.did(v.reciprocal(total[:, i, :], total[:, i, :]))
                    own.settle()
                    own.did(v.tensor_tensor(total[:, i, :], total[:, i, :], m["gates"][:, tb, 3 * h:3 * h + 3], ALU.mult))
                    own.settle()
                    for b in range(2):
                        part = p[:, i, T * b:T * b + keys]
                        v.tensor_scalar(part, part, total[:, i, b + 1:b + 2], None, ALU.mult)
                    part = p[:, i, CMP:CMP + N_CMP]
                    v.tensor_scalar(part, part, total[:, i, 0:1], None, ALU.mult).then_inc(S["probs_ready"], 1)

            @block.scalar
            def _(act):
                for i in range(N):
                    h, tb, keys, half, j, tok = at(i)
                    act.wait_ge(S["max_ready"], i + 1)
                    for b, part in enumerate((p[:, i, CMP:CMP + N_CMP], p[:, i, 0:keys], p[:, i, T:T + keys])):
                        last = act.activation(part, part, ACT.Exp, bias=top[:, i, b:b + 1],
                                              accum_out=total[:, i, b:b + 1])
                    last.then_inc(S["exps_ready"], 1)
                for i in range(N + 1):
                    if i < N:
                        h, tb, keys, half, j, tok = at(i)
                        act.wait_ge(S["transposed"], i + 1)
                        if i >= 4:
                            act.wait_ge(S["outputs_ready"], i - 3)
                        act.activation(p_t[:, i % 4, :, :].rearrange("p (b c) n -> p b c n", b=2)[:, :, 0:tb + 1, :],
                                       k.ps[:, 4 + i % 2, :].rearrange("p (b c n) -> p b c n", b=2, c=2)[:, :, 0:tb + 1, :],
                                       ACT.Copy)
                        act.activation(c_t[0:N_CMP, i % 4, :], k.ps[0:N_CMP, 2 + i % 2, 0:P], ACT.Copy)\
                           .then_inc(S["transposed_out"], 1)
                    if i:
                        h, tb, keys, half, j, tok = at(i - 1)
                        act.wait_ge(S["outputs_ready"], i)
                        act.activation(m["o"][half, j, tok], k.ps[half, 6 + (i - 1) % 2, 0:P], ACT.Copy)\
                           .then_inc(S["outputs_out"], 1)


def short_conv(k, m):
    S, stale = k.stage()
    pad = CONV2_TAPS - 1
    c, o = m["conv"], m["o"]
    with ExitStack() as ctx:
        z = k.sbuf(ctx, "conv_z", 4, T + pad)
        with k.nc.Block() as block:
            @block.sync
            def _(sp):
                clear(sp, stale)

            @block.vector
            def _(v):
                own = Steps(v, S["vector_steps"])
                own.did(v.memset(z[:, :, 0:pad], 0.0))
                own.did(v.tensor_tensor(z[:, :, pad:pad + T], c[:, 4:8, :], c[:, 8:12, :], ALU.mult))
                for tap in range(CONV2_TAPS):
                    own.settle()
                    for i in range(4):
                        w, x, y = k.column("l0_conv_w_2", CONV2_TAPS * i + tap), z[:, i, tap:tap + T], o[:, 4 + i, :]
                        if tap == 0:
                            own.did(v.tensor_scalar(y, x, w, k.column("l0_conv_b_2", i), ALU.mult, ALU.add))
                        else:
                            own.did(v.scalar_tensor_tensor(y, x, w, y, ALU.mult, ALU.add))
                own.settle()
                v.tensor_tensor(o[:, 4:8, :], o[:, 4:8, :], c[:, 0:4, :], ALU.mult)


def rwkv_mixer(k):
    with ExitStack() as ctx:
        sb = lambda name, *shape: k.sbuf(ctx, name, *shape)
        m = {"v_tok": sb("v_tok", TB, D), "g": sb("rwkv_g", KT, T), "bonus": sb("bonus", KT, T),
             "ar": sb("a_and_r", KT, TB, 2, P), "bk": sb("b_and_k", 2, KT, T), "carry": sb("carry", KT)}
        m |= {"a": m["bk"][:, 0, :, :], "k": m["bk"][:, 1, :, :], "r": m["ar"][:, :, :, 1, :]}
        with ExitStack() as early:
            eb = lambda name, *shape: k.sbuf(early, name, *shape)
            m |= {"sig": eb("decay_sigmoid", KT, T), "v": eb("rwkv_v", KT, T)}
            with ExitStack() as shifted:
                m["h"] = k.sbuf(shifted, "h_shifted", KT, T + 1)
                rmsnorm(k, k.x, "l1_mix_pre_g_2", m["h"][:, :, 1:T + 1])
                rwkv_project(k, m)
            rwkv_prepare(k, m)
            m["bk_tok"] = m["sig"][:, :, :].rearrange("p k n -> p (k n)").rearrange("p (i d) -> p i d", i=2)
            rwkv_transpose(k, m)
            rwkv_chunks(k, m)
        rwkv_norm(k, m)
        with ExitStack() as late:
            parts = k.pair(late, "moving", KT, T)
            project_from(k, k.xn, m["g"], parts, add=False)
        rmsnorm(k, m["g"], "l1_mix_post_g_2", k.x, residual=1)


def rwkv_project(k, m):
    S, stale = k.stage()
    first = k.w.taken
    MU = (1, 4, 5, 0, 2, 3)
    with ExitStack() as ctx:
        sb = lambda name, *shape: k.sbuf(ctx, name, *shape)
        down = [sb("w_dec1", KT, LORA), sb("w_a1", KT, LORA), sb("w_g1", KT, GATE_LORA)]
        up = [sb("w_dec2", D), sb("w_a2", D), sb("w_g2", D)]
        hidden = sb("lora_hidden", 3, T)
        full = m["bonus"][:, :, :], m["v_tok"][:, :, :].rearrange("p b n -> p (b n)").rearrange("p (k n) -> p k n", n=T)
        delta, mix = k.xn, [k.pair(ctx, f"mixed{i}", KT, T) for i in range(2)]
        width = (LORA, LORA, GATE_LORA)
        with k.nc.Block() as block:
            @block.sync
            def _(sp):
                clear(sp, stale)
                for n, name in enumerate(("dec", "a", "g")):
                    sp.dma_start(down[n][:, :, :], k.dram[f"w_{name}1"]).then_inc(S["lora_loaded"], 16)
                    sp.dma_start(up[n][0:width[n], :], k.dram[f"w_{name}2"]).then_inc(S["lora_loaded"], 16)
                k.w.load_ahead(sp, first, 3 * KT)

            @block.vector
            def _(v):
                own = Steps(v, S["vector_steps"])
                h = m["h"]

                def make_full(n):
                    for t in range(KT):
                        last = v.scalar_tensor_tensor(full[n % 2][:, t, :], delta[:, t, :],
                                                      k.column("l1_mu_2", KT * MU[n] + t), h[:, t, 1:T + 1],
                                                      ALU.mult, ALU.add)
                    last.then_inc(S["mixed"], 1)

                def make_low(n):
                    v.wait_ge(S["high_ready"], n - 2)
                    v.tensor_tensor(mix[n % 2].low[:, :, :], full[n % 2], mix[n % 2].high[:, :, :].bitcast(F32),
                                    ALU.subtract).then_inc(S["low_ready"], 1)

                own.did(v.memset(h[:, :, 0:1], 0.0))
                own.settle()
                own.did(v.tensor_tensor(delta[:, :, :], h[:, :, 0:T], h[:, :, 1:T + 1], ALU.subtract))
                own.settle()
                for n in range(5):
                    if n >= 2:
                        v.wait_ge(S["mix_used"], n - 1)
                    make_full(n)
                    if n >= 3:
                        make_low(n)
                for c in range(3 * KT):
                    v.wait_ge(k.w.used, first + c + 1)
                    k.w.split_low(v, first + c + 1)
                    if c == KT - 1:
                        make_full(5)
                        make_low(5)

            @block.tensor
            def _(pe):
                pe.wait_ge(S["lora_loaded"], 6 * 16)
                for n in range(3):
                    pe.wait_ge(S["mixed"], n + 1)
                    for t in range(KT):
                        last = pe.matmul(k.ps[0:width[n], 4 + n % 2, 0:T], down[n][:, t, :], full[n % 2][:, t, :],
                                         start=t == 0, stop=t == KT - 1)
                    last.then_inc(S["mix_used"], 1)
                    pe.wait_ge(S["hidden_ready"], n + 1)
                    for t in range(KT):
                        c = KT * n + t
                        if c >= 2:
                            pe.wait_ge(S["lora_out"], c - 1)
                        pe.matmul(k.ps[:, 6 + c % 2, 0:T], up[n][0:width[n], P * t:P * t + P], hidden[0:width[n], n, :],
                                  start=True, stop=True).then_inc(S["lora_ready"], 1)
                for c in range(3 * KT):
                    n = 3 + c // KT
                    pe.wait_ge(S["low_ready"], n - 2)
                    if c >= 4:
                        pe.wait_ge(S["copied"], c - 3)
                    feature_tiles(k, pe, c % 4, mix[n % 2], k.w.arrived(pe))

            @block.scalar
            def _(act):
                def make_high(n):
                    act.wait_ge(S["mixed"], n + 1)
                    if n == 5:
                        act.wait_ge(k.w.used, first + KT)
                    act.activation(mix[n % 2].high[:, :, :], full[n % 2], ACT.Copy).then_inc(S["high_ready"], 1)

                for n in range(3):
                    act.wait_ge(S["mix_used"], n + 1)
                    act.activation(hidden[0:width[n], n, :], k.ps[0:width[n], 4 + n % 2, 0:T],
                                   (ACT.Tanh, ACT.Copy, ACT.Sigmoid)[n]).then_inc(S["hidden_ready"], 1)
                    if n == 2:
                        make_high(3)
                    for t in range(KT):
                        c = KT * n + t
                        act.wait_ge(S["lora_ready"], c + 1)
                        src = k.ps[:, 6 + c % 2, 0:T]
                        if n == 0:
                            ins = act.activation(m["sig"][:, t, :], src, ACT.Sigmoid, bias=k.column("l1_w0_2", t))
                        elif n == 1:
                            ins = act.activation(m["a"][:, t, :], src, ACT.Sigmoid, bias=k.column("l1_a0_2", t))
                        else:
                            ins = act.activation(m["g"][:, t, :], src, ACT.Copy)
                        ins.then_inc(S["lora_out"], 1)
                make_high(4)
                for c in range(3 * KT):
                    act.wait_ge(k.w.used, first + c + 1)
                    src, t = k.ps[:, c % 4, 0:T], c % KT
                    if c < KT:
                        src, out = src.rearrange("p (b n) -> p b n", b=TB), m["r"][:, t, :, :]
                    else:
                        out = m["k" if c < 2 * KT else "v"][:, t, :]
                    act.activation(out, src, ACT.Copy).then_inc(S["copied"], 1)
                    k.w.round_high(act, first + c + 1)
                    if c == KT - 1:
                        make_high(5)


def rwkv_prepare(k, m):
    S, stale = k.stage()
    RATE = -float(np.exp(-0.5))
    with ExitStack() as ctx:
        sb = lambda name, *shape: k.sbuf(ctx, name, *shape)
        kk, tmp, run = sb("kk", KT, T), sb("tmp", KT, T), k.xn
        before = sb("decay_before", KT, T)
        with k.nc.Block() as block:
            @block.sync
            def _(sp):
                clear(sp, stale)

            @block.vector
            def _(v):
                own = Steps(v, S["vector_steps"])
                c3 = lambda ap: ap.rearrange("p (b n) -> p b n", b=TB)
                c4 = lambda ap: ap.rearrange("p k (b n) -> p k b n", b=TB)
                for t in range(KT):
                    v.tensor_scalar(kk[:, t, :], m["k"][:, t, :], k.column("l1_k_k_2", t), None, ALU.mult)\
                     .then_inc(S["kk_raw"], 1)
                for t in range(KT):
                    own.did(v.tensor_scalar(before[:, t, :], m["a"][:, t, :], -1.0, k.column("l1_k_a_2", t),
                                            ALU.add, ALU.mult))
                own.settle()
                own.did(v.scalar_tensor_tensor(m["k"][:, :, :], before[:, :, :], 1.0, m["k"][:, :, :],
                                               ALU.add, ALU.mult))
                own.settle()
                v.wait_ge(S["sums"], 8)
                for t in range(KT):
                    v.wait_ge(S["sums"], t + 1)
                    own.did(v.tensor_scalar(before[:, t, :], k.ps[:, t, 0:T], 1e-12, None, ALU.max))
                    v.scalar_tensor_tensor(c3(tmp[:, t, :]), m["r"][:, t, :, :], k.column("l1_r_k_2", t),
                                           c3(m["k"][:, t, :]), ALU.mult, ALU.mult).then_inc(S["rk_ready"], 1)
                own.settle()
                for c in range(2 * KT):
                    t, b = c // 2, slice(P * (c % 2), P * (c % 2) + P)
                    own.did(v.tensor_tensor_scan(run[:, t, b], k.const("ones"), m["sig"][:, t, b], 0.0,
                                                 ALU.mult, ALU.add))
                own.settle()
                v.wait_ge(S["roots"], 1)
                own.did(v.reciprocal(before[:, :, :], before[:, :, :]))
                own.settle()
                own.did(v.tensor_tensor(kk[:, :, :], kk[:, :, :], before[:, :, :], ALU.mult))
                own.settle()
                own.did(v.tensor_tensor(m["a"][:, :, :], m["a"][:, :, :], kk[:, :, :], ALU.mult))
                own.did(v.tensor_tensor(m["carry"][:, :], run[:, :, P - 1], run[:, :, P + 63], ALU.add))
                own.settle()
                own.did(v.tensor_tensor(m["carry"][:, :], m["carry"][:, :], run[:, :, 63], ALU.subtract))
                own.did(v.tensor_copy(before[:, :, 0:2], run[:, :, :].rearrange("p k (b n) -> p k b n", b=TB)[:, :, :, 63]))
                own.settle()
                middle = before[:, :, 0:2].unsqueeze(3).broadcast_to([P, KT, TB, P])
                run4 = run[:, :, :].rearrange("p k (b n) -> p k b n", b=TB)
                own.did(v.tensor_tensor(run4, run4, middle, ALU.subtract))
                own.settle()
                v.tensor_tensor(before[:, :, :], run[:, :, :], m["sig"][:, :, :], ALU.subtract)\
                 .then_inc(S["exponents_ready"], 1)
                for t in range(KT):
                    v.wait_ge(S["bonus_sums"], t + 1)
                    v.tensor_tensor(m["bonus"][:, t, :], m["v"][:, t, :], k.ps[:, t, 0:T], ALU.mult)
                v.wait_ge(S["exps_ready"], 3)
                ar = m["ar"]
                v.tensor_tensor(ar[:, :, :, 0, :], c4(kk[:, :, :]), c4(before[:, :, :]), ALU.mult)
                v.tensor_tensor(ar[:, :, :, 1, :], m["r"], c4(run[:, :, :]), ALU.mult)
                v.tensor_tensor(m["bk"][:, 0, :, :], m["a"][:, :, :], tmp[:, :, :], ALU.mult)
                v.tensor_tensor(m["bk"][:, 1, :, :], m["k"][:, :, :], tmp[:, :, :], ALU.mult)

            @block.scalar
            def _(act):
                for t in range(KT):
                    act.wait_ge(S["kk_raw"], t + 1)
                    act.activation(tmp[:, t, :], kk[:, t, :], ACT.Square).then_inc(S["squares"], 1)
                act.wait_ge(S["rk_ready"], KT)
                act.activation(before[:, :, :], before[:, :, :], ACT.Sqrt).then_inc(S["roots"], 1)
                act.wait_ge(S["exponents_ready"], 1)
                act.wait_ge(S["bonus_sums"], KT)
                act.activation(tmp[:, :, :], run[:, :, :], ACT.Exp, scale=-RATE).then_inc(S["inverse_exp"], 1)
                act.wait_ge(S["inverse_exp"], 1)
                act.activation(run[:, :, :], run[:, :, :], ACT.Exp, scale=RATE).then_inc(S["exps_ready"], 1)
                act.activation(before[:, :, :], before[:, :, :], ACT.Exp, scale=RATE).then_inc(S["exps_ready"], 1)
                act.activation(m["carry"][:, :], m["carry"][:, :], ACT.Exp, scale=RATE).then_inc(S["exps_ready"], 1)

            @block.tensor
            def _(pe):
                for t in range(KT):
                    pe.wait_ge(S["squares"], t + 1)
                    pe.matmul(k.ps[:, t, 0:T], k.const("head_ones"), tmp[:, t, :], start=True, stop=True)\
                      .then_inc(S["sums"], 1)
                for t in range(KT):
                    pe.wait_ge(S["rk_ready"], t + 1)
                    pe.matmul(k.ps[:, t, 0:T], k.const("head_ones"), tmp[:, t, :], start=True, stop=True)\
                      .then_inc(S["bonus_sums"], 1)


def rwkv_transpose(k, m):
    S, stale = k.stage()
    jobs = [(m["v"], m["v_tok"][:, tb, :], tb) for tb in range(TB)] + \
           [(m["bk"][:, i, :, :], m["bk_tok"][:, i, :], 0) for i in range(2)]
    with k.nc.Block() as block:
        @block.sync
        def _(sp):
            clear(sp, stale)

        @block.tensor
        def _(pe):
            for n, (src, _, tb) in enumerate(jobs):
                for half in range(2):
                    for t in range(4):
                        last = pe.transpose(k.ps[:, 2 * n + half, P * t:P * t + P],
                                            src[:, 4 * half + t, P * tb:P * tb + P], k.const("identity"))
                    last.then_inc(S["transposed"], 1)

        @block.vector
        def _(v):
            for n, (_, dst, _) in enumerate(jobs):
                for half in range(2):
                    v.wait_ge(S["transposed"], 2 * n + half + 1)
                    v.tensor_copy(dst[:, 512 * half:512 * half + 512], k.ps[:, 2 * n + half, :])


def rwkv_chunks(k, m):
    with ExitStack() as ctx:
        sb = lambda name, *shape: k.sbuf(ctx, name, *shape)
        m["scores"] = sb("scores_t", RW_HEADS, 4, P)
        m["quad_mask"] = sb("quad_mask", 4, P)
        m["inverse"], m["inverse_t"] = sb("inverse", 4, 4, P), sb("inverse_t", 4, 4, P)
        m["product"] = sb("product", 2, 4, P)
        free = m["v"][:, :, :].rearrange("p k n -> p (k n)")
        m["rhs"] = free[:, 0:D].rearrange("p (i h n) -> p i h n", i=2, n=RW_DIM)
        m["x"] = free[:, D:2 * D].rearrange("p (h n) -> p h n", n=RW_DIM)
        m["state"] = sb("rwkv_state", KT, RW_DIM)
        for tb in range(TB):
            rwkv_chunk(k, m, tb)


def rwkv_chunk(k, m, tb):
    S, stale = k.stage()
    H, W = RW_HEADS, RW_DIM
    tok = slice(P * tb, P * tb + P)
    sc, x, u = m["scores"], m["inverse"], m["inverse_t"]
    lt = sc[:, :, 0, :].rearrange("p (g h) n -> p g h n", h=4)
    half = lambda h: slice(64 * (h % 2), 64 * (h % 2) + 64)
    with k.nc.Block() as block:
        @block.sync
        def _(sp):
            clear(sp, stale)

        @block.gpsimd
        def _(pool):
            if tb == 0:
                pool.memset(sc[:, :, :, :], 0.0).then_inc(S["scores_cleared"], 1)

        @block.tensor
        def _(pe):
            for h in range(H):
                if h >= 2:
                    pe.wait_ge(S["scores_out"], h - 1)
                ar = m["ar"][half(h), h // 2, tb, :, :].rearrange("p a n -> p (a n)")
                for i in range(2):
                    last = pe.matmul(k.ps[:, 6 + h % 2, T * i:T * i + T], m["bk"][half(h), i, h // 2, tok], ar,
                                     start=True, stop=True)
                last.then_inc(S["scores_ready"], 1)
            invert_tensor(k, pe, S, lt, x, u, m["product"], 4)
            pe.wait_ge(S["inverse_updated"], 4 * (LEVELS - 1))
            for h in range(H):
                out = k.ps[:, h % 2, W * (h // 2):W * (h // 2) + W]
                last = pe.matmul(out, sc[:, h, 2, :], m["v_tok"][:, tb, W * h:W * h + W], start=True, stop=tb == 0)
                if tb:
                    last = pe.matmul(out, m["ar"][half(h), h // 2, tb, 0, :], m["state"][half(h), h // 2, :],
                                     start=False, stop=True)
            last.then_inc(S["rhs_ready"], 1)
            pe.wait_ge(S["rhs_out"], 1)
            for h in range(H):
                last = pe.matmul(k.ps[:, 2 + h // 8, W * (h % 8):W * (h % 8) + W], u[:, h // 4, h % 4, :],
                                 m["rhs"][:, h % 2, h // 2, :], start=True, stop=True)
            last.then_inc(S["x_ready"], 1)
            pe.wait_ge(S["x_out"], 1)
            for h in range(H):
                j = h // 2
                out = k.ps[half(h), 4 + j // 4, P * (j % 4):P * (j % 4) + P]
                pe.matmul(out, m["x"][:, h, :], sc[:, h, 1, :], start=True, stop=False)
                last = pe.matmul(out, m["v_tok"][:, tb, W * h:W * h + W], sc[:, h, 3, :], start=False, stop=tb == 0)
                if tb:
                    last = pe.matmul(out, m["state"][half(h), j, :], m["ar"][half(h), j, tb, 1, :],
                                     start=False, stop=True)
            last.then_inc(S["outputs_ready"], 1)
            if tb == 0:
                for h in range(H):
                    out = k.ps[half(h), 6, W * (h // 2):W * (h // 2) + W]
                    pe.matmul(out, m["bk_tok"][:, 0, W * h:W * h + W], m["x"][:, h, :], start=True, stop=False)
                    last = pe.matmul(out, m["bk_tok"][:, 1, W * h:W * h + W], m["v_tok"][:, 0, W * h:W * h + W],
                                     start=False, stop=True)
                last.then_inc(S["state_ready"], 1)

        @block.scalar
        def _(act):
            invert_scalar(k, act, S, x, 4)
            act.wait_ge(S["x_ready"], 1)
            for i in range(2):
                last = act.activation(m["x"][:, 8 * i:8 * i + 8, :].rearrange("p h n -> p (h n)"), k.ps[:, 2 + i, :],
                                      ACT.Copy, scale=-1.0)
            last.then_inc(S["x_out"], 1)
            act.wait_ge(S["outputs_ready"], 1)
            for i in range(2):
                act.activation(k.xn[:, 4 * i:4 * i + 4, tok], four(k.ps[:, 4 + i, :]), ACT.Copy)

        @block.vector
        def _(v):
            own = Steps(v, S["vector_steps"])
            if tb == 0:
                for i, name in enumerate(("strict", "upto", "strict", "upto")):
                    own.did(v.tensor_copy(m["quad_mask"][:, i, :], k.const(name)))
            own.settle()
            if tb == 0:
                v.wait_ge(S["scores_cleared"], 1)
            for h in range(H):
                v.wait_ge(S["scores_ready"], h + 1)
                v.copy_predicated(sc[:, h, :, :], m["quad_mask"][:, :, :].bitcast(U32), four(k.ps[:, 6 + h % 2, :]))\
                 .then_inc(S["scores_out"], 1)
                if h % 4 == 3:
                    v.wait_ge(S["scores_out"], h + 1)
                    level0(k, v, own, S, lt, u, h // 4)
            invert_vector(k, v, S, x, u, m["product"], 4)
            v.wait_ge(S["rhs_ready"], 1)
            for i in range(2):
                last = v.tensor_copy(m["rhs"][:, i, :, :].rearrange("p h n -> p (h n)"), k.ps[:, i, :])
            last.then_inc(S["rhs_out"], 1)
            if tb == 0:
                v.wait_ge(S["state_ready"], 1)
                v.tensor_tensor(m["state"][:, :, :], k.ps[:, 6, :].rearrange("p (k n) -> p k n", n=W),
                                m["carry"][:, :].unsqueeze(2).broadcast_to([P, KT, W]), ALU.mult)


def rwkv_norm(k, m):
    S, stale = k.stage()
    y = k.xn
    with ExitStack() as ctx:
        tmp = k.sbuf(ctx, "tmp", KT, T)
        with k.nc.Block() as block:
            @block.sync
            def _(sp):
                clear(sp, stale)

            @block.tensor
            def _(pe):
                for t in range(KT):
                    pe.matmul(k.ps[:, t, 0:T], k.const("head_ones"), y[:, t, :], start=True, stop=True)\
                      .then_inc(S["sums"], 1)
                for t in range(KT):
                    pe.wait_ge(S["squares"], t + 1)
                    pe.matmul(k.ps[:, t, 0:T], k.const("head_ones"), tmp[:, t, :], start=True, stop=True)\
                      .then_inc(S["square_sums"], 1)

            @block.scalar
            def _(act):
                for t in range(KT):
                    act.wait_ge(S["centred"], t + 1)
                    act.activation(tmp[:, t, :], y[:, t, :], ACT.Square).then_inc(S["squares"], 1)
                act.wait_ge(S["variances"], KT)
                act.activation(tmp[:, :, :], tmp[:, :, :], ACT.Sqrt).then_inc(S["roots"], 1)

            @block.vector
            def _(v):
                own = Steps(v, S["vector_steps"])
                for t in range(KT):
                    v.wait_ge(S["sums"], t + 1)
                    v.scalar_tensor_tensor(y[:, t, :], k.ps[:, t, 0:T], -1.0 / RW_DIM, y[:, t, :],
                                           ALU.mult, ALU.add).then_inc(S["centred"], 1)
                for t in range(KT):
                    v.wait_ge(S["square_sums"], t + 1)
                    v.tensor_scalar(tmp[:, t, :], k.ps[:, t, 0:T], 1.0 / RW_DIM, LNX_EPS, ALU.mult, ALU.add)\
                     .then_inc(S["variances"], 1)
                v.wait_ge(S["roots"], 1)
                own.did(v.reciprocal(tmp[:, :, :], tmp[:, :, :]))
                own.settle()
                own.did(v.tensor_tensor(y[:, :, :], y[:, :, :], tmp[:, :, :], ALU.mult))
                own.settle()
                for t in range(KT):
                    own.did(v.tensor_scalar(y[:, t, :], y[:, t, :], k.column("l1_lnx_g_2", t),
                                            k.column("l1_lnx_b_2", t), ALU.mult, ALU.add))
                own.settle()
                own.did(v.tensor_tensor(y[:, :, :], y[:, :, :], m["bonus"][:, :, :], ALU.add))
                own.settle()
                v.tensor_tensor(y[:, :, :], y[:, :, :], m["g"][:, :, :], ALU.mult)


def store_output(k):
    S, stale = k.stage()
    with k.nc.Block() as block:
        @block.sync
        def _(sp):
            clear(sp, stale)
            sp.dma_start(k.dram["out"], k.x[:, :, :]).then_inc(k.output_stored, 16)
            sp.wait_ge(k.output_stored, 16)


def build(nc, dram):
    with ExitStack() as ctx:
        k = Kernel(nc, ctx, dram)
        load_constants(k)
        token_mixer(k)
        cross_attention(k)
        peer(k)
        rmsnorm(k, k.x, "g_final", k.x)
        ffn(k, "l0_ffn1")
        nsa_mixer(k)
        ffn(k, "l0_ffn2")
        ffn(k, "l1_ffn1")
        rwkv_mixer(k)
        ffn(k, "l1_ffn2")
        store_output(k)



def features(a):
    return a.reshape(-1, KT, P).transpose(2, 1, 0)


def column_tiles(w):
    return w.reshape(KT, P, -1, P).transpose(2, 1, 0, 3)


def ffn_chunks(gate, up, down):
    g, u, d = column_tiles(gate), column_tiles(up), down.reshape(FT, P, KT, P)
    order = [g[0], u[0]]
    for f in range(1, FT):
        order += [g[f], u[f], d[f - 1]]
    return np.stack(order + [d[FT - 1]])


def layouts(a):
    first = {n: v[0] for n, v in a.items() if v.ndim > 1 and v.shape[0] == 1}
    out = {"x": features(first["x"]), "mem": features(first["mem"]), "consts": const_tiles()}

    columns = []
    for name, tiles in COLUMNS:
        v = first[name] if name in first else a[name]
        if name == "gdn_conv":
            columns.append(v.reshape(CONV_TAPS, 12, P).transpose(2, 1, 0).reshape(P, -1))
        elif name == "l0_conv_w_2":
            columns.append(v.reshape(CONV2_TAPS, 4, P).transpose(2, 1, 0).reshape(P, -1))
        else:
            columns.append(v.reshape(tiles, P).T)
    out["columns"] = np.concatenate(columns, axis=1)

    w = first["w_in"]
    sq, sk, sv, gq, gk, gv, gz = (w[:, 512 * i:512 * i + 512] for i in range(7))
    ba, gates = w[:, 3584:3592], w[:, 3592:]
    out["w_in"] = column_tiles(np.concatenate([gq, gk, gv, sq, sk, sv, gz, gates], axis=1))
    out["w_ba"] = ba.reshape(KT, P, 8).transpose(1, 0, 2)
    rows = np.concatenate([first["gdn_a_log"], first["gdn_dt_bias"]])
    out["gdn_rows"] = np.broadcast_to(rows, (P, 8))
    out["w_up_pair"] = np.concatenate([first[n].reshape(4, P, KT, P).transpose(2, 1, 0, 3)
                                       for n in ("w_sb_up", "w_gdn_up")], axis=2)
    for name in ("w_mix_out", "w_cq", "w_ckv", "w_co", "w_pq"):
        out[name] = column_tiles(first[name])
    out["subkeys"] = first["peer_subkeys"].reshape(2 * PEER_HEADS, P, P).transpose(2, 0, 1)
    out["peer_u"], out["peer_v"] = first["peer_u"], first["peer_v"]

    for f in ("l0_ffn1", "l0_ffn2", "l1_ffn1", "l1_ffn2"):
        out[f] = ffn_chunks(a[f"{f}_w_gate_2"], a[f"{f}_w_up_2"], a[f"{f}_w_down_2"])

    w = a["l0_w_in_2"]
    q = w[:, :512].reshape(D, 2, 4, 64).transpose(0, 2, 1, 3).reshape(D, 512)
    kc, vc, ks, vs, kw, vw = (w[:, 536 + P * i:664 + P * i] for i in range(6))
    out["l0_in"] = column_tiles(np.concatenate([q, kc, vc, ks, kw, vs, vw, w[:, 1304:]], axis=1))
    out["w_g"] = w[:, 512:536].reshape(KT, P, 24).transpose(1, 0, 2)
    w = a["l0_w_out_2"]
    nsa_rows = w[:512].reshape(2, 4, 64, D).transpose(1, 0, 2, 3).reshape(512, D)
    out["l0_out"] = column_tiles(np.concatenate([nsa_rows, w[512:]]))
    twice = lambda v: np.concatenate([v, v], axis=0)
    out["cmp_w1"] = np.stack([twice(a[f"l0_cmp_w1_{n}_2"].reshape(CMP_BLOCK, 64, P).transpose(1, 0, 2))
                              for n in "kv"], axis=1)
    out["cmp_w2"] = np.stack([a[f"l0_cmp_w2_{n}_2"] for n in "kv"], axis=1)
    out["cmp_pos"] = np.stack([twice(a[f"l0_cmp_pe_{n}_2"].T) for n in "kv"], axis=1)

    out["l1_rkv"] = np.concatenate([column_tiles(a[f"l1_w_{n}_2"]) for n in "rkv"])
    out["l1_o"] = column_tiles(a["l1_w_o_2"])
    for n in ("dec", "a", "g"):
        out[f"w_{n}1"] = a[f"l1_w_{n}1_2"].reshape(KT, P, -1).transpose(1, 0, 2)
        out[f"w_{n}2"] = a[f"l1_w_{n}2_2"]
    for name, n in STREAM:
        assert out[name].shape[0] == n, name
        out[name] = out[name].reshape(n, P, CHUNK)
    return {n: np.ascontiguousarray(v) for n, v in out.items()}


def kernel(**inputs):
    from concourse import bacc
    from concourse.bass_utils import run_bass_kernel_spmd

    arrays = layouts({n: np.asarray(v) for n, v in inputs.items()})
    nc = bacc.Bacc("TRN2", target_bir_lowering=False, num_devices=1)
    dram = {n: nc.dram_tensor(f"in_{n}", v.shape, mybir.dt.from_np(v.dtype), kind="ExternalInput").ap()
            for n, v in arrays.items()}
    dram["out"] = nc.dram_tensor("out_x", (P, KT, T), F32, kind="ExternalOutput").ap()
    build(nc, dram)
    result = run_bass_kernel_spmd(nc, [{f"in_{n}": v for n, v in arrays.items()}], core_ids=[0])
    x = np.asarray(result.results[0]["out_x"])
    return np.ascontiguousarray(x.transpose(2, 1, 0).reshape(1, T, D))
```

```python
from contextlib import ExitStack

import numpy as np

import concourse.bass as bass
from concourse import mybir

F32 = mybir.dt.float32
F32R = mybir.dt.float32r
U32 = mybir.dt.uint32
ACT = mybir.ActivationFunctionType
ALU = mybir.AluOpType
AX = mybir.AxisListType

P = 128
D = 1024
T = 256
KT = D // P
TB = T // P
EPS = 1e-6

SB_HEADS, SB_DIM = 8, 64
GDN_HEADS, GDN_DIM = 4, 128
CONV_TAPS = 4
X_HEADS, X_DIM = 4, 256
PEER_HEADS, PEER_KEYS, TOPK = 8, 128, 16
EXPERTS = PEER_KEYS * PEER_KEYS
SLOTS = PEER_HEADS * TOPK

D_FF = 2816
FT = D_FF // P
NSA_HEADS, NSA_GROUPS, NSA_DIM = 8, 2, 64
NSA_REP = NSA_HEADS // NSA_GROUPS
CMP_BLOCK, CMP_STRIDE = 32, 16
N_CMP = (T - CMP_BLOCK) // CMP_STRIDE + 1
CONV2_TAPS = 3
NSA_CHUNKS = 4 + 4 + 2 + 2 + 12
RW_HEADS, RW_DIM = 16, 64
LORA, GATE_LORA = 64, 128
LNX_EPS = 64e-5
NEG = -1e30
CLAMP = -1e20

RING = 5
SPLIT = 3
CHUNK = 8 * P
LEVELS = 7
GATHER_RING = 8

CONST_TILES = ["ones", "identity", "head_ones", "upto", "neg_suffix", "neg_ones", "strict",
               "negated_strict"] + [f"level{i}" for i in range(LEVELS)]
CONST_ROWS = CONST_TILES + ["causal0", "causal1a", "causal1b", "misc"]

HEAD_SELECT = 64

COLUMNS = [("g_mix", 8), ("g_cross", 8), ("g_mem", 8), ("g_peer", 8), ("g_final", 8),
           ("gdn_norm_g", 1), ("gdn_conv", 12 * CONV_TAPS)]
for _l in ("l0", "l1"):
    for _f in ("ffn1", "ffn2", "mix"):
        COLUMNS += [(f"{_l}_{_f}_pre_g_2", 8), (f"{_l}_{_f}_post_g_2", 8)]
COLUMNS += [("l1_mu_2", 48), ("l1_w0_2", 8), ("l1_a0_2", 8), ("l1_k_k_2", 8), ("l1_k_a_2", 8),
            ("l1_r_k_2", 8), ("l1_lnx_g_2", 8), ("l1_lnx_b_2", 8),
            ("l0_conv_w_2", 4 * CONV2_TAPS), ("l0_conv_b_2", 4)]
COLUMN_AT = {}
for _n, _c in COLUMNS:
    COLUMN_AT[_n] = (sum(c for _, c in COLUMNS[:len(COLUMN_AT)]), _c)
N_COLUMNS = sum(c for _, c in COLUMNS)

STREAM = [("w_in", 44), ("w_up_pair", 8), ("w_mix_out", 8), ("w_cq", 8), ("w_ckv", 16),
          ("w_co", 8), ("w_pq", 16), ("l0_ffn1", 3 * FT), ("l0_in", NSA_CHUNKS),
          ("l0_out", 8), ("l0_ffn2", 3 * FT), ("l1_ffn1", 3 * FT), ("l1_rkv", 24),
          ("l1_o", 8), ("l1_ffn2", 3 * FT)]


def const_tiles():
    s, t = np.arange(P)[:, None], np.arange(P)[None, :]
    tiles = {
        "ones": np.ones((P, P)), "identity": s == t, "head_ones": s // 64 == t // 64,
        "upto": s <= t, "neg_suffix": -1.0 * (s >= t), "neg_ones": -np.ones((P, P)),
        "strict": s < t, "negated_strict": -1.0 * (s < t),
        "causal0": np.where(t <= s, t - s, NEG),
        "causal1a": t - (P + s) + 0.0,
        "causal1b": np.where(t <= s, t - s, NEG),
    }
    tiles["level0"] = (s // 2 == t // 2) & (s < t)
    for i in range(1, LEVELS):
        b = 1 << i
        tiles[f"level{i}"] = (s // (2 * b) == t // (2 * b)) & ((s // b) % 2 == 1) & ((t // b) % 2 == 0)
    misc = np.zeros((P, P))
    for tb in range(TB):
        ends = np.arange(N_CMP) * CMP_STRIDE + CMP_BLOCK - 1
        far = tb * P + np.arange(P)[:, None] - ends[None, :]
        misc[:, N_CMP * tb:N_CMP * (tb + 1)] = np.where(far >= 0, -far, NEG)
    misc[:, 32:48] = np.arange(16)[None, :]
    misc[:, HEAD_SELECT + 14:HEAD_SELECT + 16] = s // 64 == np.arange(2)[None, :]
    tiles["misc"] = misc
    return np.stack([np.asarray(tiles[n], np.float32) for n in CONST_ROWS], axis=1)


class Signals:

    def __init__(self, bank):
        self.bank, self.names = bank, {}

    def __getitem__(self, name):
        if name not in self.names:
            self.names[name] = self.bank[len(self.names)]
        return self.names[name]


class Steps:

    def __init__(self, engine, semaphore):
        self.engine, self.semaphore, self.count = engine, semaphore, 0

    def did(self, instruction):
        instruction.then_inc(self.semaphore, 1)
        self.count += 1

    def settle(self):
        self.engine.wait_ge(self.semaphore, self.count)


class Weights:

    def __init__(self, nc, ctx, dram):
        sb = lambda name, slots, dtype: ctx.enter_context(nc.sbuf_tensor(name, [P, slots, CHUNK], dtype))
        self.raw, self.high, self.low = sb("weights", RING, F32), sb("weights_high", SPLIT, F32R), sb("weights_low", SPLIT, F32R)
        self.filled = [ctx.enter_context(nc.semaphore(f"weights_filled{i}")) for i in range(RING)]
        self.rounded, self.split, self.used = (ctx.enter_context(nc.semaphore(f"weights_{n}"))
                                               for n in ("rounded", "split", "used"))
        self.plan = [dram[name][c] for name, n in STREAM for c in range(n)]
        self.loaded = self.n_rounded = self.n_split = self.taken = 0

    def load_ahead(self, sp, first, count):
        for c in range(self.loaded, min(first + count + SPLIT + RING, len(self.plan))):
            if c >= RING:
                sp.wait_ge(self.split, c - RING + 1)
            sp.dma_start(self.raw[:, c % RING, :], self.plan[c]).then_inc(self.filled[c % RING], 16)
            self.loaded = c + 1

    def round_high(self, act, used):
        for c in range(self.n_rounded, min(used + SPLIT, len(self.plan))):
            act.wait_ge(self.filled[c % RING], 16 * (c // RING + 1))
            if c >= SPLIT:
                act.wait_ge(self.used, c - SPLIT + 1)
            act.activation(self.high[:, c % SPLIT, :], self.raw[:, c % RING, :], ACT.Copy)\
               .then_inc(self.rounded, 1)
            self.n_rounded = c + 1

    def split_low(self, v, used):
        for c in range(self.n_split, min(used + SPLIT, len(self.plan))):
            v.wait_ge(self.rounded, c + 1)
            v.tensor_tensor(self.low[:, c % SPLIT, :], self.raw[:, c % RING, :],
                            self.high[:, c % SPLIT, :].bitcast(F32), ALU.subtract).then_inc(self.split, 1)
            self.n_split = c + 1

    def arrived(self, pe, width=P):
        c = self.taken
        self.taken += 1
        pe.wait_ge(self.split, c + 1)
        return Pair(*(part[:, c % SPLIT, :].rearrange("p (k n) -> p k n", n=width)
                      for part in (self.high, self.low)))


class Pair:

    def __init__(self, high, low):
        self.high, self.low = high, low

    def __getitem__(self, at):
        return Pair(self.high[at], self.low[at])


def product(pe, out, lhs, rhs, start, stop):
    pe.matmul(out, lhs.high, rhs.high, start=start, stop=False)
    pe.matmul(out, lhs.high, rhs.low, start=False, stop=False)
    return pe.matmul(out, lhs.low, rhs.high, start=False, stop=stop)


class Kernel:

    def __init__(self, nc, ctx, dram):
        self.nc, self.ctx, self.dram = nc, ctx, dram
        self.banks = [[ctx.enter_context(nc.semaphore(f"stage{b}_{i}")) for i in range(56)]
                      for b in range(2)]
        self.stage_number, self.previous, self.tensors = 0, None, 0
        self.output_stored = ctx.enter_context(nc.semaphore("output_stored"))
        self.consts_loaded = ctx.enter_context(nc.semaphore("consts_loaded"))
        self.rows_ready = [ctx.enter_context(nc.semaphore(f"rows_ready{i}")) for i in range(GATHER_RING)]
        self.w = Weights(nc, ctx, dram)
        self.ps = ctx.enter_context(nc.psum_tensor("ps", [P, 8, 512], F32))
        self.consts = self.sbuf(ctx, "consts", len(CONST_ROWS), P)
        self.columns = self.sbuf(ctx, "columns", N_COLUMNS)
        self.x = self.sbuf(ctx, "x_residual", KT, T)
        self.xn = self.sbuf(ctx, "x_normed", KT, T)

    def sbuf(self, ctx, name, *shape, dtype=F32):
        self.tensors += 1
        return ctx.enter_context(self.nc.sbuf_tensor(f"{name}_{self.tensors}", [P, *shape], dtype))

    def pair(self, ctx, name, *shape):
        return Pair(self.sbuf(ctx, f"{name}_high", *shape, dtype=F32R), self.sbuf(ctx, f"{name}_low", *shape, dtype=F32R))

    def const(self, name):
        return self.consts[:, CONST_ROWS.index(name), :]

    def column(self, name, tile):
        at, _ = COLUMN_AT[name]
        return self.columns[:, at + tile:at + tile + 1]

    def head_select(self, t):
        return self.const("misc")[:, HEAD_SELECT + 14 - 2 * t:HEAD_SELECT + 30 - 2 * t]

    def stage(self):
        signals = Signals(self.banks[self.stage_number % 2])
        stale, self.previous = self.previous, signals
        self.stage_number += 1
        return signals, (stale.names.values() if stale else [])


def clear(sp, stale):
    for s in stale:
        sp.sem_clear(s)


def over(ap, n):
    return ap.unsqueeze(1).broadcast_to([ap.shape[0], n, ap.shape[1]])


def load_constants(k):
    S, stale = k.stage()
    with k.nc.Block() as block:
        @block.sync
        def _(sp):
            sp.dma_start(k.x[:, :, :], k.dram["x"]).then_inc(S["loads"], 16)
            sp.dma_start(k.columns[:, :], k.dram["columns"]).then_inc(S["loads"], 16)
            sp.dma_start(k.consts[:, 0:2, :], k.dram["consts"][:, 0:2, :]).then_inc(S["loads"], 16)
            k.w.load_ahead(sp, 0, -SPLIT)
            sp.dma_start(k.consts[:, 2:, :], k.dram["consts"][:, 2:, :]).then_inc(k.consts_loaded, 16)
            sp.wait_ge(S["loads"], 48)


def keep_warm(k, pe, n, bank):
    for _ in range(n):
        pe.matmul(k.ps[:, bank, 0:T], k.const("identity"), k.consts[:, 0:2, :].rearrange("p a n -> p (a n)"),
                  start=True, stop=True)


def rmsnorm(k, src, gain, dst, residual=False, parts=None):
    S, stale = k.stage()
    with ExitStack() as ctx:
        squares = k.sbuf(ctx, "squares", KT, T)
        scale = k.sbuf(ctx, "scale", 2, T)
        with k.nc.Block() as block:
            @block.sync
            def _(sp):
                clear(sp, stale)
                sp.wait_ge(k.consts_loaded, 16)

            @block.scalar
            def _(act):
                for half in range(2):
                    part = slice(4 * half, 4 * half + 4)
                    act.activation(squares[:, part, :], src[:, part, :], ACT.Square)\
                       .then_inc(S["squares_ready"], 1)
                k.w.round_high(act, k.w.taken)
                act.wait_ge(S["mean_ready"], 1)
                act.activation(scale[:, 1, :], scale[:, 0, :], ACT.Sqrt).then_inc(S["root_ready"], 1)
                if parts:
                    for q in range(4):
                        part = slice(2 * q, 2 * q + 2)
                        act.wait_ge(S["normed"], 2 * q + 2)
                        act.activation(parts.high[:, part, :], dst[:, part, :], ACT.Copy).then_inc(S["high_ready"], 1)

            @block.tensor
            def _(pe):
                for t in range(KT):
                    if t % 4 == 0:
                        pe.wait_ge(S["squares_ready"], t // 4 + 1)
                    last = pe.matmul(k.ps[:, 7, 0:T], k.const("ones"), squares[:, t, :],
                                     start=t == 0, stop=t == KT - 1)
                last.then_inc(S["sum_ready"], 1)

            @block.vector
            def _(v):
                own = Steps(v, S["vector_steps"])
                k.w.split_low(v, k.w.taken)
                v.wait_ge(S["sum_ready"], 1)
                v.tensor_scalar(scale[:, 0, :], k.ps[:, 7, 0:T], 1.0 / D, EPS, ALU.mult, ALU.add)\
                 .then_inc(S["mean_ready"], 1)
                v.wait_ge(S["root_ready"], 1)
                own.did(v.reciprocal(scale[:, 0, :], scale[:, 1, :]))
                own.settle()
                if residual:
                    if residual != 1:
                        own.did(v.tensor_scalar(scale[:, 0, :], scale[:, 0, :], residual, None, ALU.mult))
                        own.settle()
                    own.did(v.tensor_tensor(squares[:, :, :], src[:, :, :], over(scale[:, 0, :], KT),
                                            ALU.mult))
                    own.settle()
                    for t in range(KT):
                        v.scalar_tensor_tensor(dst[:, t, :], squares[:, t, :], k.column(gain, t),
                                               dst[:, t, :], ALU.mult, ALU.add)
                else:
                    for t in range(KT):
                        v.scalar_tensor_tensor(dst[:, t, :], src[:, t, :], k.column(gain, t),
                                               scale[:, 0, :], ALU.mult, ALU.mult).then_inc(S["normed"], 1)
                    if parts:
                        v.wait_ge(S["normed"], KT)
                        for q in range(4):
                            part = slice(2 * q, 2 * q + 2)
                            v.wait_ge(S["high_ready"], q + 1)
                            v.tensor_tensor(parts.low[:, part, :], dst[:, part, :],
                                            parts.high[:, part, :].bitcast(F32), ALU.subtract)


def token_chunk(k, pe, moving, n, width):
    tiles, count = k.w.arrived(pe, width), CHUNK // width
    per_output = KT // count
    output, at = n // per_output, n % per_output
    for i in range(count):
        t = count * at + i
        for tb in range(TB):
            last = product(pe, k.ps[:, 4 + 2 * (output % 2) + tb, 0:width], moving[:, t, P * tb:P * tb + P],
                           tiles[:, i, :], start=t == 0, stop=t == KT - 1)
    last.then_inc(k.w.used, 1)


def feature_tiles(k, pe, bank, moving, tiles):
    for t in range(KT):
        last = product(pe, k.ps[:, bank, 0:T], tiles[:, t, :], moving[:, t, :], start=t == 0, stop=t == KT - 1)
    last.then_inc(k.w.used, 1)


def project_from(k, src, dst, parts, add):
    S, stale = k.stage()
    first = k.w.taken
    with k.nc.Block() as block:
        @block.sync
        def _(sp):
            clear(sp, stale)
            k.w.load_ahead(sp, first, KT)

        @block.scalar
        def _(act):
            for part in (slice(0, 4), slice(4, 8)):
                act.activation(parts.high[:, part, :], src[:, part, :], ACT.Copy).then_inc(S["high_ready"], 1)
            for i in range(KT):
                k.w.round_high(act, first + i + 1)

        @block.tensor
        def _(pe):
            for i in range(KT):
                if i >= 4:
                    pe.wait_ge(S["tile_out"], i - 3)
                tiles = k.w.arrived(pe)
                for t in range(KT):
                    if i == 0 and t % 4 == 0:
                        pe.wait_ge(S["low_ready"], t // 4 + 1)
                    last = product(pe, k.ps[:, i % 4, 0:T], tiles[:, t, :], parts[:, t, :],
                                   start=t == 0, stop=t == KT - 1)
                last.then_inc(k.w.used, 1)

        @block.vector
        def _(v):
            for half, part in enumerate((slice(0, 4), slice(4, 8))):
                v.wait_ge(S["high_ready"], half + 1)
                v.tensor_tensor(parts.low[:, part, :], src[:, part, :], parts.high[:, part, :].bitcast(F32),
                                ALU.subtract).then_inc(S["low_ready"], 1)
            for i in range(KT):
                v.wait_ge(k.w.used, first + i + 1)
                if add:
                    ins = v.tensor_tensor(dst[:, i, :], dst[:, i, :], k.ps[:, i % 4, 0:T], ALU.add)
                else:
                    ins = v.tensor_copy(dst[:, i, :], k.ps[:, i % 4, 0:T])
                ins.then_inc(S["tile_out"], 1)
                k.w.split_low(v, first + i + 1)


def project_in(k, m):
    S, stale = k.stage()
    first = k.w.taken
    CONV, QK, COPIED, Z, ALL = 12, 20, 24, 28, 44
    SUMS_AFTER = 30
    y, sq = m["qkv"], m["squares"]
    ring = lambda i: i if i < QK else i - (COPIED - QK)
    norm_bank = lambda i: k.ps[:, 4 + i // 2, T * (i % 2):T * (i % 2) + T]
    with k.nc.Block() as block:
        @block.sync
        def _(sp):
            clear(sp, stale)
            sp.dma_start(m["w_ba"][:, :, :], k.dram["w_ba"]).then_inc(S["small_loaded"], 16)
            sp.dma_start(m["rows"][:, :], k.dram["gdn_rows"]).then_inc(S["small_loaded"], 16)
            k.w.load_ahead(sp, first, ALL)

        @block.tensor
        def _(pe):
            pe.wait_ge(S["small_loaded"], 32)
            for tb in range(TB):
                for t in range(KT):
                    last = pe.matmul(k.ps[:, 6, 8 * tb:8 * tb + 8], k.xn[:, t, P * tb:P * tb + P],
                                     m["w_ba"][:, t, :], start=t == 0, stop=t == KT - 1)
            last.then_inc(S["ba_ready"], 1)
            for i in range(ALL):
                if QK <= i < COPIED:
                    token_chunk(k, pe, m["parts"], i - QK, 4 * P)
                    continue
                old = ring(i) - 4
                if old >= 0:
                    name, before = ("conv_in_out", 0) if old < CONV else ("copied", CONV) if old < QK else \
                        ("activated", QK)
                    pe.wait_ge(S[name], old - before + 1)
                feature_tiles(k, pe, ring(i) % 4, m["parts"], k.w.arrived(pe))
                if i == SUMS_AFTER:
                    pe.wait_ge(S["beta_in"], 1)
                    pe.wait_ge(S["decay_in"], 1)
                    pe.wait_ge(S["values_out"], TB)
                    pe.wait_ge(S["squares"], 2)
                    for t in range(KT):
                        pe.matmul(norm_bank(t), k.const("ones"), sq[:, t, :], start=True, stop=True)\
                          .then_inc(S["sums"], 1)

        @block.vector
        def _(v):
            own = Steps(v, S["vector_steps"])
            pad = CONV_TAPS - 1
            own.did(v.memset(m["conv_in"][:, :, 0:pad], 0.0))
            b, a = m["beta"], m["decay"]
            v.wait_ge(S["ba_ready"], 1)
            ba = k.ps[:, 6, 0:16].rearrange("p (b c) -> p b c", b=TB)
            v.tensor_copy(b[:, :, :], ba[:, :, 0:4]).then_inc(S["beta_in"], 1)
            v.tensor_tensor(a[:, 0], ba[:, :, 4:8], over(m["rows"][:, 4:8], TB), ALU.add).then_inc(S["decay_in"], 1)
            v.wait_ge(S["decay_in"], 1)
            own.did(v.tensor_scalar(a[:, 1], a[:, 0], -1.0, None, ALU.mult))
            own.settle()
            v.tensor_tensor(a[:, 2], a[:, 0], a[:, 1], ALU.min).then_inc(S["minus_abs"], 1)

            def convolve(i):
                own.settle()
                for j in range(CONV_TAPS):
                    tile = i - 1 - j
                    if not 0 <= tile < CONV:
                        continue
                    x, g = m["conv_in"][:, tile, j:j + T], k.column("gdn_conv", CONV_TAPS * tile + j)
                    if j == 0:
                        v.wait_ge(S["conv_in_out"], tile + 1)
                        own.did(v.tensor_scalar(y[:, tile, :], x, g, None, ALU.mult))
                    else:
                        ins = v.scalar_tensor_tensor(y[:, tile, :], x, g, y[:, tile, :], ALU.mult, ALU.add)
                        if j < CONV_TAPS - 1:
                            own.did(ins)
                        else:
                            ins.then_inc(S["convolved"], 1)

            def normalise(i):
                if i == SUMS_AFTER + 1:
                    for t in range(KT):
                        v.wait_ge(S["sums"], KT if t % 2 == 0 else t + 1)
                        v.tensor_scalar(sq[:, t, :], norm_bank(t), 1.0, EPS, ALU.mult, ALU.add)\
                         .then_inc(S["eps_added"], 1)
                t = i - SUMS_AFTER - 3
                if 0 <= t <= KT:
                    own.settle()
                if 0 <= t < KT:
                    v.wait_ge(S["roots"], 1)
                    own.did(v.reciprocal(sq[:, t, :], sq[:, t, :]))
                if 1 <= t <= KT:
                    factor = GDN_DIM ** -0.5 if t <= 4 else 1.0
                    v.scalar_tensor_tensor(y[:, t - 1, :], y[:, t - 1, :], factor, sq[:, t - 1, :], ALU.mult, ALU.mult)

            for i in range(ALL):
                v.wait_ge(k.w.used, first + i + 1)
                if CONV <= i < QK:
                    v.tensor_copy(m["sb_qk"][:, i - CONV, :], k.ps[:, i % 4, 0:T]).then_inc(S["copied"], 1)
                elif i == COPIED - 1:
                    for tb in range(TB):
                        v.tensor_copy(m["sb_v"][:, tb, :], k.ps[:, 4 + tb, :]).then_inc(S["values_out"], 1)
                k.w.split_low(v, first + i + 1)
                convolve(i)
                normalise(i)
                if i == COPIED:
                    v.wait_ge(S["softplus_log"], 1)
                    own.did(v.scalar_tensor_tensor(a[:, 0], a[:, 0], 0.0, a[:, 2], ALU.max, ALU.add))
                    own.settle()
                    own.did(v.scalar_tensor_tensor(a[:, 1], a[:, 0], -1.0, over(m["rows"][:, 0:4], TB),
                                                   ALU.mult, ALU.mult))

        @block.scalar
        def _(act):
            a = m["decay"]
            act.wait_ge(S["small_loaded"], 32)
            act.activation(m["rows"][:, 0:4], m["rows"][:, 0:4], ACT.Exp)
            act.wait_ge(S["minus_abs"], 1)
            act.activation(a[:, 2], a[:, 2], ACT.Exp).then_inc(S["softplus_exp"], 1)
            act.wait_ge(S["softplus_exp"], 1)
            act.activation(a[:, 2], a[:, 2], ACT.Ln, bias=1.0).then_inc(S["softplus_log"], 1)
            for i in range(COPIED):
                if i < CONV:
                    act.wait_ge(k.w.used, first + i + 1)
                    act.activation(m["conv_in"][:, i, CONV_TAPS - 1:], k.ps[:, i % 4, 0:T], ACT.Copy)\
                       .then_inc(S["conv_in_out"], 1)
                k.w.round_high(act, first + i + 1)
            for i in range(COPIED, Z):
                act.wait_ge(k.w.used, first + i + 1)
                act.activation(m["z"][:, i - COPIED, :], k.ps[:, ring(i) % 4, 0:T], ACT.Silu).then_inc(S["activated"], 1)
                k.w.round_high(act, first + i + 1)
            act.wait_ge(S["convolved"], CONV)
            for group in range(3):
                part = y[:, 4 * group:4 * group + 4, :]
                act.activation(part, part, ACT.Silu).then_inc(S["silu"], 1)
            for group in range(2):
                act.wait_ge(S["silu"], group + 1)
                act.activation(sq[:, 4 * group:4 * group + 4, :], y[:, 4 * group:4 * group + 4, :],
                               ACT.Square).then_inc(S["squares"], 1)
            act.wait_ge(S["beta_in"], 1)
            act.activation(m["beta"][:, :, :], m["beta"][:, :, :], ACT.Sigmoid)
            for i in range(Z, ALL):
                act.wait_ge(k.w.used, first + i + 1)
                act.activation(m["gates"][:, i - Z, :], k.ps[:, ring(i) % 4, 0:T], ACT.Sigmoid)\
                   .then_inc(S["activated"], 1)
                k.w.round_high(act, first + i + 1)
                if i == SUMS_AFTER + 1:
                    act.wait_ge(S["eps_added"], KT)
                    act.activation(sq[:, :, :], sq[:, :, :], ACT.Sqrt).then_inc(S["roots"], 1)


def stick_breaking(k, m):
    S, stale = k.stage()
    H, SEG = SB_HEADS, 3 * P
    with ExitStack() as ctx:
        z = k.sbuf(ctx, "z_scaled", H, SEG)
        w = k.sbuf(ctx, "softplus", H, SEG)
        a = k.sbuf(ctx, "weights", H, SEG)
        mask = k.sbuf(ctx, "segment_mask", SEG)

        def half(h):
            return slice(64 * (h % 2), 64 * (h % 2) + 64)

        with k.nc.Block() as block:
            @block.sync
            def _(sp):
                clear(sp, stale)

            @block.tensor
            def _(pe):
                for h in range(H):
                    if h >= 2:
                        pe.wait_ge(S["z_out"], h - 1)
                    q, kk = m["sb_qk"][half(h), h // 2, :], m["sb_qk"][half(h), 4 + h // 2, :]
                    pe.matmul(k.ps[:, h % 2, 0:T], kk[:, 0:P], q, start=True, stop=True)
                    pe.matmul(k.ps[:, h % 2, T:SEG], kk[:, P:T], q[:, P:T], start=True, stop=True)\
                      .then_inc(S["z_ready"], 1)
                for h in range(H):
                    pe.wait_ge(S["softplus_ready"], h + 1)
                    if h >= 2:
                        pe.wait_ge(S["logs_ready"], h - 1)
                    r = k.ps[:, 2 + h % 2, :]
                    pe.matmul(r[:, 0:P], k.const("neg_suffix"), w[:, h, 0:P], start=True, stop=True)
                    pe.matmul(r[:, P:T], k.const("neg_suffix"), w[:, h, P:T], start=True, stop=False)
                    pe.matmul(r[:, P:T], k.const("neg_ones"), w[:, h, T:SEG], start=False, stop=True)
                    pe.matmul(r[:, T:SEG], k.const("neg_suffix"), w[:, h, T:SEG], start=True, stop=True)\
                      .then_inc(S["sums_ready"], 1)
                for h in range(H):
                    pe.wait_ge(S["weights_ready"], h + 1)
                    if h >= 2:
                        pe.wait_ge(S["head_out"], h - 1)
                    o = k.ps[half(h), 4 + h % 2, :]
                    v0, v1 = (m["sb_v"][:, b, 64 * h:64 * h + 64] for b in range(TB))
                    pe.matmul(o[:, 0:P], v0, a[:, h, 0:P], start=True, stop=True)
                    pe.matmul(o[:, P:T], v0, a[:, h, P:T], start=True, stop=False)
                    pe.matmul(o[:, P:T], v1, a[:, h, T:SEG], start=False, stop=True)\
                      .then_inc(S["output_ready"], 1)

            @block.scalar
            def _(act):
                for h in range(H):
                    act.wait_ge(S["z_ready"], h + 1)
                    act.activation(z[:, h, :], k.ps[:, h % 2, 0:SEG], ACT.Copy, scale=SB_DIM ** -0.5)\
                       .then_inc(S["z_out"], 1)
                for h in range(H):
                    act.wait_ge(S["minus_abs"], h + 1)
                    act.activation(w[:, h, :], w[:, h, :], ACT.Exp).then_inc(S["exps"], 1)
                for h in range(H):
                    act.wait_ge(S["exps"], h + 1)
                    act.activation(w[:, h, :], w[:, h, :], ACT.Ln, bias=1.0).then_inc(S["log_ready"], 1)
                for h in range(H):
                    act.wait_ge(S["logs_ready"], h + 1)
                    act.activation(a[:, h, :], a[:, h, :], ACT.Exp).then_inc(S["exp_ready"], 1)
                for h in range(H):
                    act.wait_ge(S["output_ready"], h + 1)
                    act.activation(m["o_sb"][half(h), h // 2, :], k.ps[half(h), 4 + h % 2, 0:T], ACT.Copy)\
                       .then_inc(S["head_out"], 1)

            @block.vector
            def _(v):
                own = Steps(v, S["vector_steps"])
                own.did(v.tensor_copy(mask[:, 0:P], k.const("strict")))
                own.did(v.tensor_copy(mask[:, P:T], k.const("ones")))
                own.did(v.tensor_copy(mask[:, T:SEG], k.const("strict")))
                for h in range(H):
                    v.wait_ge(S["z_out"], h + 1)
                    own.did(v.tensor_scalar(w[:, h, :], z[:, h, :], -1.0, None, ALU.mult))
                    own.settle()
                    v.tensor_tensor(w[:, h, :], w[:, h, :], z[:, h, :], ALU.min)\
                     .then_inc(S["minus_abs"], 1)
                for h in range(H):
                    v.wait_ge(S["log_ready"], h + 1)
                    own.did(v.scalar_tensor_tensor(w[:, h, :], z[:, h, :], 0.0, w[:, h, :],
                                                   ALU.max, ALU.add))
                    own.settle()
                    v.tensor_tensor(w[:, h, :], w[:, h, :], mask[:, :], ALU.mult)\
                     .then_inc(S["softplus_ready"], 1)
                for h in range(H):
                    v.wait_ge(S["sums_ready"], h + 1)
                    v.tensor_tensor(a[:, h, :], z[:, h, :], k.ps[:, 2 + h % 2, 0:SEG], ALU.add)\
                     .then_inc(S["logs_ready"], 1)
                for h in range(H):
                    v.wait_ge(S["exp_ready"], h + 1)
                    v.scalar_tensor_tensor(a[:, h, :], a[:, h, :], 1.0, mask[:, :], ALU.min, ALU.mult)\
                     .then_inc(S["weights_ready"], 1)


def level_columns(ap, level, odd):
    return ap.rearrange("p h (n two b) -> p h n two b", two=2, b=1 << level)[:, :, :, int(odd), :]


def block_columns(ap, level, odd):
    return ap.rearrange("p (n two b) -> p n two b", two=2, b=1 << level)[:, :, int(odd), :]


START_BANKS = (1, 2, 4, 5)


def invert_tensor(k, pe, S, lt, x, u, pc, groups):
    n, size = (LEVELS - 1) * groups, u.shape[2]
    for g in range(groups):
        pe.wait_ge(S["level0"], g + 1)
        for h in range(size):
            last = pe.transpose(k.ps[:, START_BANKS[g], P * h:P * h + P], u[:, g, h, :], k.const("identity"))
        last.then_inc(S["level0_transposed"], 1)

    def product_step(i):
        g = i % groups
        if i < groups:
            pe.wait_ge(S["inverse_started"], i + 1)
        else:
            pe.wait_ge(S["inverse_updated"], i - groups + 1)
        if i >= 2:
            pe.wait_ge(S["product_masked"], i - 1)
        for h in range(size):
            last = pe.matmul(k.ps[:, 3 * (i % 2), P * h:P * h + P], lt[:, g, h, :], x[:, g, h, :],
                             start=True, stop=True)
        last.then_inc(S["product_ready"], 1)

    product_step(0)
    for i in range(n):
        g, level = i % groups, 1 + i // groups
        if i + 1 < n:
            product_step(i + 1)
        pe.wait_ge(S["product_masked"], i + 1)
        if i == 0:
            pe.wait_ge(S["inverse_started"], groups)
        if i >= 2:
            pe.wait_ge(S["inverse_updated"], i - 1)
        for h in range(size):
            half = slice(64 * h, 64 * h + 64)
            if level < LEVELS - 1:
                pe.matmul(k.ps[:, 3 * (i % 2) + 1, half], u[:, g, h, :], block_columns(pc[:, i % 2, h, :], level, 0),
                          start=True, stop=True)
            last = pe.matmul(k.ps[:, 3 * (i % 2) + 2, half], pc[:, i % 2, h, :],
                             block_columns(u[:, g, h, :], level, 1), start=True, stop=True)
        last.then_inc(S["updates_ready"], 1)


def invert_scalar(k, act, S, x, groups):
    size = x.shape[2]
    for g in range(groups):
        act.wait_ge(S["level0_transposed"], g + 1)
        act.activation(x[:, g, :, :], k.ps[:, START_BANKS[g], 0:P * size].rearrange("p (h n) -> p h n", n=P),
                       ACT.Copy).then_inc(S["inverse_started"], 1)


def level0(k, v, own, S, lt, u, g):
    size = u.shape[2]
    own.did(v.scalar_tensor_tensor(u[:, g, :, :], lt[:, g, :, :], -1.0, over(k.const("level0"), size),
                                   ALU.mult, ALU.mult))
    own.settle()
    v.tensor_tensor(u[:, g, :, :], u[:, g, :, :], over(k.const("identity"), size), ALU.add).then_inc(S["level0"], 1)


def invert_vector(k, v, S, x, u, pc, groups):
    n, size = (LEVELS - 1) * groups, u.shape[2]

    def mask_product(i):
        v.wait_ge(S["product_ready"], i + 1)
        if i >= 2:
            v.wait_ge(S["updates_ready"], i - 1)
        v.tensor_tensor(pc[:, i % 2, :, :], k.ps[:, 3 * (i % 2), 0:P * size].rearrange("p (h n) -> p h n", n=P),
                        over(k.const(f"level{1 + i // groups}"), size), ALU.mult).then_inc(S["product_masked"], 1)

    mask_product(0)
    for i in range(n):
        g, level = i % groups, 1 + i // groups
        if i + 1 < n:
            mask_product(i + 1)
        v.wait_ge(S["updates_ready"], i + 1)
        for odd, (dst, bank) in enumerate(((x, 1), (u, 2))):
            if odd or level < LEVELS - 1:
                part = level_columns(dst[:, g, :, :], level, odd)
                src = k.ps[:, 3 * (i % 2) + bank, 0:64 * size].rearrange("p (h n b) -> p h n b", h=size, b=1 << level)
                last = v.tensor_tensor(part, part, src, ALU.subtract)
        last.then_inc(S["inverse_updated"], 1)


def four(ap):
    return ap.rearrange("p (h n) -> p h n", h=4)


def gdn_chunks(k, m):
    S, stale = k.stage()
    H = GDN_HEADS
    q, kk, vv = (lambda h: m["qkv"][:, h, :]), (lambda h: m["qkv"][:, 4 + h, :]), (lambda h: m["qkv"][:, 8 + h, :])
    with ExitStack() as ctx:
        sb = lambda name, *shape: k.sbuf(ctx, name, *shape)
        wide_g, wide_b = sb("wide_g", 2, H, P), sb("wide_beta", 2, H, P)
        sums = sb("gc_columns", 2, H)
        edge = sb("exp_gc_columns", 2, H)
        decay = sb("decay_t", 2, H, P)
        grown = sb("exp_gc_rows", 2, H, P)
        lt, qk_t = sb("lt", 2, H, P), sb("qk_t", 2, H, P)
        x, pc = sb("inverse", 4, 2, P), sb("product", 2, 2, P)
        inverse_t = sb("inverse_t", 2, H, P)
        groups_of_two = lambda tile: tile[:, :, :, :].rearrange("p t (a b) n -> p (t a) b n", b=2)
        u, lt_groups = groups_of_two(inverse_t), groups_of_two(lt)
        k_beta, v_beta, k_dec = sb("k_beta", 2, H, P), sb("v_beta", 2, H, P), sb("k_dec", 2, H, P)
        w_t, uu = sb("w_t", H, P), sb("u", 2, H, P)
        q_dec, state = sb("q_dec", H, P), sb("state", H, P)

        with k.nc.Block() as block:
            @block.sync
            def _(sp):
                clear(sp, stale)

            @block.tensor
            def _(pe):
                for tb in range(TB):
                    tok = slice(P * tb, P * tb + P)
                    if tb:
                        pe.wait_ge(S["scores_read"], tb)
                    pe.wait_ge(S["wide"], tb + 1)
                    for h in range(H):
                        cols = slice(P * h, P * h + P)
                        pe.matmul(k.ps[:, 0, cols], wide_g[:, tb, h, :], k.const("upto"), start=True, stop=True)
                        pe.matmul(k.ps[:, 1, cols], wide_b[:, tb, h, :], k.const("identity"), start=True, stop=True)
                        pe.matmul(k.ps[:, 2, cols], kk(h)[:, tok], kk(h)[:, tok], start=True, stop=True)
                        pe.matmul(k.ps[:, 3, cols], kk(h)[:, tok], q(h)[:, tok], start=True, stop=True)
                    pe.matmul(k.ps[:, 4, 0:H], k.const("upto"), m["decay"][:, 1, tb, :],
                              start=True, stop=True).then_inc(S["scores_ready"], 1)
                for tb in range(TB):
                    tok = slice(P * tb, P * tb + P)
                    if tb:
                        pe.wait_ge(S["tokens_out"], tb)
                    for h in range(H):
                        cols = slice(P * h, P * h + P)
                        pe.transpose(k.ps[:, 6, cols], kk(h)[:, tok], k.const("identity"))
                        last = pe.transpose(k.ps[:, 7, cols], vv(h)[:, tok], k.const("identity"))
                    last.then_inc(S["tokens_ready"], 1)
                pe.wait_ge(S["scores_read"], TB)
                keep_warm(k, pe, 6, 0)
                invert_tensor(k, pe, S, lt_groups, x, u, pc, 4)
                pe.wait_ge(S["tokens_out"], TB)
                pe.wait_ge(S["inverse_updated"], 4 * (LEVELS - 1))
                for h in range(H):
                    cols = slice(P * h, P * h + P)
                    pe.matmul(k.ps[:, 0, cols], inverse_t[:, 0, h, :], v_beta[:, 0, h, :], start=True, stop=True)
                    pe.matmul(k.ps[:, 1, cols], inverse_t[:, 1, h, :], v_beta[:, 1, h, :], start=True, stop=True)
                    last = pe.matmul(k.ps[:, 2, cols], k_beta[:, 1, h, :], inverse_t[:, 1, h, :], start=True, stop=True)
                last.then_inc(S["solved"], 1)
                pe.wait_ge(S["solution_out"], 1)
                for h in range(H):
                    cols = slice(P * h, P * h + P)
                    pe.matmul(k.ps[:, 3, cols], uu[:, 0, h, :], qk_t[:, 0, h, :], start=True, stop=True)
                    last = pe.matmul(k.ps[:, 4, cols], k_dec[:, 0, h, :], uu[:, 0, h, :], start=True, stop=True)
                last.then_inc(S["state_ready"], 1)
                pe.wait_ge(S["state_out"], 1)
                for h in range(H):
                    last = pe.matmul(k.ps[:, 5, P * h:P * h + P], w_t[:, h, :], state[:, h, :], start=True, stop=True)
                last.then_inc(S["recalled"], 1)
                pe.wait_ge(S["corrected"], 1)
                for h in range(H):
                    cols = slice(P * h, P * h + P)
                    pe.matmul(k.ps[:, 6, cols], state[:, h, :], q_dec[:, h, :], start=True, stop=False)
                    last = pe.matmul(k.ps[:, 6, cols], uu[:, 1, h, :], qk_t[:, 1, h, :], start=False, stop=True)
                last.then_inc(S["outputs_ready"], 1)

            @block.scalar
            def _(act):
                for tb in range(TB):
                    act.wait_ge(S["scores_ready"], tb + 1)
                    act.activation(grown[:, tb, :, :], four(k.ps[:, 0, :]), ACT.Exp)\
                       .then_inc(S["grown"], 1)
                    act.wait_ge(S["log_decay"], tb + 1)
                    act.activation(decay[:, tb, :, :], decay[:, tb, :, :], ACT.Exp).then_inc(S["decays"], 1)
                    act.activation(edge[:, tb, :], sums[:, tb, :], ACT.Exp).then_inc(S["decays"], 1)
                invert_scalar(k, act, S, x, 4)
                act.wait_ge(S["solved"], 1)
                act.activation(uu[:, 0, :, :], four(k.ps[:, 0, :]), ACT.Copy)
                act.activation(uu[:, 1, :, :], four(k.ps[:, 1, :]), ACT.Copy)
                act.activation(w_t[:, :, :], four(k.ps[:, 2, :]), ACT.Copy).then_inc(S["solution_out"], 1)
                act.wait_ge(S["state_ready"], 1)
                act.activation(state[:, :, :], four(k.ps[:, 4, :]), ACT.Copy).then_inc(S["state_out"], 1)
                act.activation(m["o_gdn"][:, :, 0:P], four(k.ps[:, 3, :]), ACT.Copy)
                act.wait_ge(S["outputs_ready"], 1)
                act.activation(m["o_gdn"][:, :, P:T], four(k.ps[:, 6, :]), ACT.Copy)

            @block.vector
            def _(v):
                own = Steps(v, S["vector_steps"])
                for tb in range(TB):
                    for h in range(H):
                        v.tensor_scalar(wide_g[:, tb, h, :], k.const("ones"), m["decay"][:, 1, tb, h:h + 1],
                                        None, ALU.mult)
                        last = v.tensor_scalar(wide_b[:, tb, h, :], k.const("ones"),
                                               m["beta"][:, tb, h:h + 1], None, ALU.mult)
                    last.then_inc(S["wide"], 1)
                for tb in range(TB):
                    v.wait_ge(S["scores_ready"], tb + 1)
                    own.did(v.tensor_copy(sums[:, tb, :], k.ps[:, 4, 0:H]))
                    own.settle()
                    v.wait_ge(S["grown"], tb + 1)
                    for h in range(H):
                        last = v.tensor_scalar(decay[:, tb, h, :], k.ps[:, 0, P * h:P * h + P],
                                               sums[:, tb, h:h + 1], 0.0, ALU.subtract, ALU.min)
                    last.then_inc(S["log_decay"], 1)
                    v.wait_ge(S["decays"], 2 * tb + 1)
                    own.did(v.tensor_tensor(lt[:, tb, :, :], four(k.ps[:, 2, :]), decay[:, tb, :, :], ALU.mult))
                    own.did(v.tensor_tensor(qk_t[:, tb, :, :], four(k.ps[:, 3, :]), decay[:, tb, :, :], ALU.mult))
                    own.settle()
                    own.did(v.tensor_tensor(lt[:, tb, :, :], lt[:, tb, :, :], four(k.ps[:, 1, :]), ALU.mult))
                    own.did(v.tensor_tensor(qk_t[:, tb, :, :], qk_t[:, tb, :, :], over(k.const("upto"), H), ALU.mult))
                    own.settle()
                    v.tensor_tensor(lt[:, tb, :, :], lt[:, tb, :, :], over(k.const("strict"), H), ALU.mult)\
                     .then_inc(S["scores_read"], 1)
                    v.wait_ge(S["scores_read"], tb + 1)
                    level0(k, v, own, S, lt_groups, u, 2 * tb)
                    level0(k, v, own, S, lt_groups, u, 2 * tb + 1)
                for tb in range(TB):
                    v.wait_ge(S["tokens_ready"], tb + 1)
                    v.wait_ge(S["decays"], 2 * tb + 2)
                    own.did(v.tensor_tensor(edge[:, tb, :], edge[:, tb, :], m["beta"][:, tb, :], ALU.mult))
                    own.settle()
                    for h in range(H):
                        cols = slice(P * h, P * h + P)
                        v.tensor_scalar(k_beta[:, tb, h, :], k.ps[:, 6, cols], edge[:, tb, h:h + 1], None, ALU.mult)
                        v.tensor_scalar(k_dec[:, tb, h, :], k.ps[:, 6, cols], decay[:, tb, h, P - 1:P], None, ALU.mult)
                        last = v.tensor_scalar(v_beta[:, tb, h, :], k.ps[:, 7, cols], m["beta"][:, tb, h:h + 1],
                                               None, ALU.mult)
                    last.then_inc(S["tokens_out"], 1)
                v.tensor_tensor(q_dec[:, :, :], m["qkv"][:, 0:4, P:T], grown[:, 1, :, :], ALU.mult)
                invert_vector(k, v, S, x, u, pc, 4)
                v.wait_ge(S["recalled"], 1)
                v.tensor_tensor(uu[:, 1, :, :], uu[:, 1, :, :], four(k.ps[:, 5, :]), ALU.subtract)\
                 .then_inc(S["corrected"], 1)


def gdn_gate(k, m):
    S, stale = k.stage()
    o = m["o_gdn"]
    with ExitStack() as ctx:
        sq = k.sbuf(ctx, "squares", 4, T)
        with k.nc.Block() as block:
            @block.sync
            def _(sp):
                clear(sp, stale)

            @block.scalar
            def _(act):
                act.activation(sq[:, :, :], o[:, :, :], ACT.Square).then_inc(S["squares"], 1)
                act.wait_ge(S["means"], 4)
                act.activation(sq[:, :, :], sq[:, :, :], ACT.Sqrt).then_inc(S["roots"], 1)

            @block.tensor
            def _(pe):
                pe.wait_ge(S["squares"], 1)
                for i in range(4):
                    pe.matmul(k.ps[:, i, 0:T], k.const("ones"), sq[:, i, :], start=True, stop=True)\
                      .then_inc(S["sums"], 1)

            @block.vector
            def _(v):
                own = Steps(v, S["vector_steps"])
                for i in range(4):
                    v.wait_ge(S["sums"], i + 1)
                    v.tensor_scalar(sq[:, i, :], k.ps[:, i, 0:T], 1.0 / GDN_DIM, EPS, ALU.mult, ALU.add)\
                     .then_inc(S["means"], 1)
                v.wait_ge(S["roots"], 1)
                own.did(v.reciprocal(sq[:, :, :], sq[:, :, :]))
                own.settle()
                own.did(v.scalar_tensor_tensor(o[:, :, :], o[:, :, :], k.column("gdn_norm_g", 0), sq[:, :, :],
                                               ALU.mult, ALU.mult))
                own.settle()
                v.tensor_tensor(o[:, :, :], o[:, :, :], m["z"][:, :, :], ALU.mult)


def merge_branches(k, m):
    S, stale = k.stage()
    first = k.w.taken
    with ExitStack() as ctx:
        part = k.sbuf(ctx, "gated", 2, T)
        with k.nc.Block() as block:
            @block.sync
            def _(sp):
                clear(sp, stale)
                k.w.load_ahead(sp, first, KT)

            @block.tensor
            def _(pe):
                for i in range(KT):
                    if i >= 4:
                        pe.wait_ge(S["tile_merged"], i - 3)
                    tiles = k.w.arrived(pe)
                    for b, src in enumerate((m["parts"][:, 0:4, :], m["parts"][:, 4:8, :])):
                        if i == 0:
                            pe.wait_ge(S["low_ready"], b + 1)
                        for t in range(4):
                            last = product(pe, k.ps[:, i % 4, T * b:T * b + T], tiles[:, 4 * b + t, :],
                                           src[:, t, :], start=t == 0, stop=t == 3)
                    last.then_inc(k.w.used, 1)

            @block.vector
            def _(v):
                own = Steps(v, S["vector_steps"])
                for b, src in enumerate((m["o_sb"], m["o_gdn"])):
                    v.wait_ge(S["high_ready"], b + 1)
                    part_b = slice(4 * b, 4 * b + 4)
                    v.tensor_tensor(m["parts"].low[:, part_b, :], src[:, :, :],
                                    m["parts"].high[:, part_b, :].bitcast(F32), ALU.subtract)\
                     .then_inc(S["low_ready"], 1)
                for i in range(KT):
                    v.wait_ge(k.w.used, first + i + 1)
                    if i:
                        v.wait_ge(S["tile_merged"], i)
                    for b in range(2):
                        own.did(v.tensor_tensor(part[:, b, :], m["gates"][:, KT * b + i, :],
                                                k.ps[:, i % 4, T * b:T * b + T], ALU.mult))
                    own.settle()
                    v.tensor_tensor(k.xn[:, i, :], part[:, 0, :], part[:, 1, :], ALU.add)\
                     .then_inc(S["tile_merged"], 1)
                    k.w.split_low(v, first + i + 1)

            @block.scalar
            def _(act):
                for b, src in enumerate((m["o_sb"], m["o_gdn"])):
                    act.activation(m["parts"].high[:, 4 * b:4 * b + 4, :], src[:, :, :], ACT.Copy)\
                       .then_inc(S["high_ready"], 1)
                for i in range(KT):
                    k.w.round_high(act, first + i + 1)


def token_mixer(k):
    with ExitStack() as ctx:
        sb = lambda name, *shape: k.sbuf(ctx, name, *shape)
        m = {"parts": k.pair(ctx, "moving", KT, T), "w_ba": sb("w_ba", KT, 8), "rows": sb("gdn_rows", 8),
             "beta": sb("beta", TB, 4), "decay": sb("decay", 3, TB, 4),
             "z": sb("z_silu", 4, T), "o_sb": sb("o_sb", 4, T), "o_gdn": sb("o_gdn", 4, T),
             "gates": sb("gates", 16, T), "qkv": sb("qkv", 12, T)}
        with ExitStack() as early:
            eb = lambda name, *shape: k.sbuf(early, name, *shape)
            m |= {"sb_qk": eb("sb_qk", 8, T), "sb_v": eb("sb_v", TB, 512),
                  "conv_in": eb("conv_in", 12, T + CONV_TAPS - 1), "squares": eb("squares", KT, T)}
            rmsnorm(k, k.x, "g_mix", k.xn, parts=m["parts"])
            project_in(k, m)
            stick_breaking(k, m)
        gdn_chunks(k, m)
        gdn_gate(k, m)
        merge_branches(k, m)
        project_from(k, k.xn, k.x, m["parts"], add=True)


def cross_attention(k):
    with ExitStack() as ctx:
        q, kk = k.sbuf(ctx, "xq", KT, T), k.sbuf(ctx, "xk", KT, T)
        v_tok, o = k.sbuf(ctx, "xv", TB, D), k.sbuf(ctx, "xo", KT, T)
        mem = k.sbuf(ctx, "mem", KT, T)
        parts, mem_parts = k.pair(ctx, "moving", KT, T), k.pair(ctx, "moving_mem", KT, T)
        load_memory(k, mem)
        rmsnorm(k, mem, "g_mem", mem, parts=mem_parts)
        rmsnorm(k, k.x, "g_cross", k.xn, parts=parts)
        cross_project(k, q, kk, v_tok, parts, mem_parts)
        cross_heads(k, q, kk, v_tok, o)
        project_from(k, o, k.x, parts, add=True)


def load_memory(k, mem):
    S, stale = k.stage()
    with k.nc.Block() as block:
        @block.sync
        def _(sp):
            clear(sp, stale)
            sp.dma_start(mem[:, :, :], k.dram["mem"]).then_inc(S["loaded"], 16)
            sp.wait_ge(S["loaded"], 16)


def cross_project(k, q, kk, v_tok, parts, mem_parts):
    S, stale = k.stage()
    first = k.w.taken
    with k.nc.Block() as block:
        @block.sync
        def _(sp):
            clear(sp, stale)
            k.w.load_ahead(sp, first, 3 * KT)

        @block.tensor
        def _(pe):
            for i in range(2 * KT):
                if i >= 4:
                    pe.wait_ge(S["copied"], i - 3)
                feature_tiles(k, pe, i % 4, parts if i < KT else mem_parts, k.w.arrived(pe))
            for i in range(KT):
                token_chunk(k, pe, mem_parts, i, 4 * P)

        @block.scalar
        def _(act):
            for i in range(3 * KT):
                k.w.round_high(act, first + i + 1)

        @block.vector
        def _(v):
            for i in range(3 * KT):
                v.wait_ge(k.w.used, first + i + 1)
                if i < 2 * KT:
                    out = q[:, i, :] if i < KT else kk[:, i - KT, :]
                    v.tensor_copy(out, k.ps[:, i % 4, 0:T]).then_inc(S["copied"], 1)
                elif i % 4 == 3:
                    n = (i - 2 * KT) // 4
                    for tb in range(TB):
                        v.tensor_copy(v_tok[:, tb, 512 * n:512 * n + 512], k.ps[:, 4 + 2 * n + tb, :])
                k.w.split_low(v, first + i + 1)


def cross_heads(k, q, kk, v_tok, o):
    S, stale = k.stage()
    N = X_HEADS * TB
    with ExitStack() as ctx:
        p = k.sbuf(ctx, "probs", N, T)
        p_t = k.sbuf(ctx, "probs_t", X_HEADS, TB, T)
        top, total = k.sbuf(ctx, "row_max", N), k.sbuf(ctx, "row_sum", N)
        with k.nc.Block() as block:
            @block.sync
            def _(sp):
                clear(sp, stale)

            @block.tensor
            def _(pe):
                for i in range(N):
                    h, tb = i // TB, i % TB
                    if i >= 4:
                        pe.wait_ge(S["scores_out"], i - 3)
                    for c in range(2):
                        last = pe.matmul(k.ps[:, i % 4, 0:T], q[:, 2 * h + c, P * tb:P * tb + P],
                                         kk[:, 2 * h + c, :], start=c == 0, stop=c == 1)
                    last.then_inc(S["scores_ready"], 1)
                for i in range(N):
                    h, tb = i // TB, i % TB
                    pe.wait_ge(S["probs_ready"], i + 1)
                    if i >= 2:
                        pe.wait_ge(S["transposed_out"], i - 1)
                    for mb in range(TB):
                        last = pe.transpose(k.ps[:, 4 + i % 2, P * mb:P * mb + P],
                                            p[:, i, P * mb:P * mb + P], k.const("identity"))
                    last.then_inc(S["transposed"], 1)
                for h in range(X_HEADS):
                    pe.wait_ge(S["transposed_out"], TB * (h + 1))
                    for c in range(2):
                        n = 2 * h + c
                        if n >= 2:
                            pe.wait_ge(S["outputs_out"], n - 1)
                        for mb in range(TB):
                            last = pe.matmul(k.ps[:, 6 + n % 2, 0:T], v_tok[:, mb, P * n:P * n + P],
                                             p_t[:, h, mb, :], start=mb == 0, stop=mb == 1)
                        last.then_inc(S["outputs_ready"], 1)

            @block.vector
            def _(v):
                own = Steps(v, S["vector_steps"])
                for i in range(N):
                    v.wait_ge(S["scores_ready"], i + 1)
                    own.did(v.reduce_max(top[:, i:i + 1], k.ps[:, i % 4, 0:T], AX.X))
                    own.settle()
                    v.tensor_scalar(top[:, i:i + 1], top[:, i:i + 1], -X_DIM ** -0.5, None, ALU.mult)\
                     .then_inc(S["max_ready"], 1)
                for i in range(N):
                    v.wait_ge(S["scores_out"], i + 1)
                    own.did(v.reciprocal(total[:, i:i + 1], total[:, i:i + 1]))
                    own.settle()
                    v.tensor_scalar(p[:, i, :], p[:, i, :], total[:, i:i + 1], None, ALU.mult)\
                     .then_inc(S["probs_ready"], 1)
                for i in range(N):
                    h, tb = i // TB, i % TB
                    v.wait_ge(S["transposed"], i + 1)
                    v.tensor_copy(p_t[:, h, :, P * tb:P * tb + P],
                                  k.ps[:, 4 + i % 2, 0:T].rearrange("p (b n) -> p b n", b=TB))\
                     .then_inc(S["transposed_out"], 1)

            @block.scalar
            def _(act):
                for i in range(N):
                    act.wait_ge(S["max_ready"], i + 1)
                    act.activation(p[:, i, :], k.ps[:, i % 4, 0:T], ACT.Exp, bias=top[:, i:i + 1],
                                   scale=X_DIM ** -0.5, accum_out=total[:, i:i + 1])\
                       .then_inc(S["scores_out"], 1)
                for n in range(KT):
                    act.wait_ge(S["outputs_ready"], n + 1)
                    act.activation(o[:, n, :], k.ps[:, 6 + n % 2, 0:T], ACT.Copy)\
                       .then_inc(S["outputs_out"], 1)


def peer(k):
    with ExitStack() as ctx:
        sb = lambda name, *shape, dtype=F32: k.sbuf(ctx, name, *shape, dtype=dtype)
        tokens = sb("x_tokens", TB, D)
        top = sb("top", TB, 2 * PEER_HEADS, TOPK)
        top_at = sb("top_at", TB, 2 * PEER_HEADS, TOPK, dtype=U32)
        with ExitStack() as early:
            parts = k.pair(early, "moving", KT, T)
            rmsnorm(k, k.x, "g_peer", k.xn, parts=parts)
            peer_keys(k, parts, tokens, top, top_at)
        peer_experts(k, tokens, top, top_at)


def peer_keys(k, parts, tokens, top, top_at):
    S, stale = k.stage()
    first = k.w.taken
    N = 2 * PEER_HEADS
    with ExitStack() as ctx:
        q = k.sbuf(ctx, "peer_q", 2, T)
        keys = k.sbuf(ctx, "subkeys", N, PEER_KEYS)
        scores, spare = (k.sbuf(ctx, n, 2, TB, PEER_KEYS) for n in ("key_scores", "key_scores_spare"))
        with k.nc.Block() as block:
            @block.sync
            def _(sp):
                clear(sp, stale)
                sp.dma_start(keys[:, :, :], k.dram["subkeys"]).then_inc(S["keys_loaded"], 16)
                k.w.load_ahead(sp, first, N)

            @block.tensor
            def _(pe):
                for i in range(N + 1):
                    if i < N:
                        if i >= 2:
                            pe.wait_ge(S["queries_out"], i - 1)
                        feature_tiles(k, pe, i % 2, parts, k.w.arrived(pe))
                    if i == 0:
                        pe.wait_ge(S["keys_loaded"], 16)
                    else:
                        n = i - 1
                        pe.wait_ge(S["queries_out"], n + 1)
                        if n >= 2:
                            pe.wait_ge(S["scores_out"], n - 1)
                        for tb in range(TB):
                            last = pe.matmul(k.ps[:, 2 + n % 2, P * tb:P * tb + P], q[:, n % 2, P * tb:P * tb + P],
                                             keys[:, n, :], start=True, stop=True)
                        last.then_inc(S["scores_ready"], 1)
                for i in range(4):
                    for t in range(4):
                        last = pe.transpose(k.ps[:, 4 + i, P * t:P * t + P],
                                            k.xn[:, 4 * (i % 2) + t, P * (i // 2):P * (i // 2) + P],
                                            k.const("identity"))
                    last.then_inc(S["transposed"], 1)

            @block.scalar
            def _(act):
                for i in range(N + 1):
                    if i < N:
                        act.wait_ge(k.w.used, first + i + 1)
                        if i >= 2:
                            act.wait_ge(S["scores_ready"], i - 1)
                        act.activation(q[:, i % 2, :], k.ps[:, i % 2, 0:T], ACT.Copy).then_inc(S["queries_out"], 1)
                        k.w.round_high(act, first + i + 1)
                    if i:
                        act.wait_ge(S["scores_ready"], i)
                        if i >= 3:
                            act.wait_ge(S["tops_found"], i - 2)
                        act.activation(scores[:, (i - 1) % 2, :, :], k.ps[:, 2 + (i - 1) % 2, 0:T]
                                       .rearrange("p (b n) -> p b n", b=TB), ACT.Copy).then_inc(S["scores_out"], 1)
                for i in range(4):
                    act.wait_ge(S["transposed"], i + 1)
                    act.activation(tokens[:, i // 2, 512 * (i % 2):512 * (i % 2) + 512], k.ps[:, 4 + i, :],
                                   ACT.Copy)

            @block.vector
            def _(v):
                own = Steps(v, S["vector_steps"])
                k.w.split_low(v, first + 1)
                for i in range(N):
                    k.w.split_low(v, first + min(i + 2, N))
                    v.wait_ge(S["scores_out"], i + 1)
                    top16(v, own, lambda tb: scores[:, i % 2, tb, :], lambda tb: spare[:, i % 2, tb, :],
                          lambda tb: top[:, tb, i, :], lambda tb: top_at[:, tb, i, :], TB, S["tops_found"])


def top16(v, own, values, spare, top, index, count, found=None):
    for i in range(count):
        own.did(v.max(top(i)[:, 0:8], values(i)))
    own.settle()
    for i in range(count):
        own.did(v.max_index(index(i)[:, 0:8], top(i)[:, 0:8], values(i)))
        own.did(v.match_replace(spare(i), top(i)[:, 0:8], values(i), -3e38))
    own.settle()
    for i in range(count):
        own.did(v.max(top(i)[:, 8:16], spare(i)))
    own.settle()
    for i in range(count):
        last = v.max_index(index(i)[:, 8:16], top(i)[:, 8:16], spare(i))
        if found is not None and i == count - 1:
            last.then_inc(found, 1)
        else:
            own.did(last)
    if found is None:
        own.settle()


class Route:

    def __init__(self, k, ctx, tops, tops_at):
        H, K = PEER_HEADS, TOPK
        sb = lambda name, *shape, dtype=F32: k.sbuf(ctx, name, *shape, dtype=dtype)
        self.tops, self.tops_at, self.iota = tops, tops_at, k.const("misc")[:, 32:48]
        self.experts, self.gates = sb("experts", TB, SLOTS, dtype=U32), sb("expert_gates", TB, SLOTS)
        self.top_n = sb("top_numbers", 2 * H, K)
        self.sums, self.spare = sb("pair_sums", H, K * K), sb("pair_sums_spare", H, K * K)
        self.best, self.best_at = sb("best", H, K), sb("best_at", H, K, dtype=U32)
        self.place, self.place_f = sb("best_place", 2, H * K, dtype=U32), sb("best_place_f", 2, H * K)
        self.hot, self.key, self.total = sb("one_hot", H * K, K), sb("key_numbers", 2, H * K), sb("gate_sum", H)
        self.steps = [self.add_pairs, lambda *a: self.search(*a, 0), lambda *a: self.search(*a, 1), self.split_places,
                      lambda *a: self.number(*a, 0), lambda *a: self.number(*a, 1), self.finish]

    def shifted(self, tb):
        return self.gates[:, tb, :].rearrange("p (h i) -> p h i", h=PEER_HEADS)

    def add_pairs(self, v, own, S, tb):
        H, K = PEER_HEADS, TOPK
        own.did(v.tensor_copy(self.top_n[:, :, :], self.tops_at[:, tb, :, :]))
        halves = self.tops[:, tb, :, :].rearrange("p (h two) i -> p h two i", two=2)
        a = halves[:, :, 0, :].unsqueeze(3).broadcast_to([P, H, K, K])
        b = halves[:, :, 1, :].unsqueeze(2).broadcast_to([P, H, K, K])
        own.did(v.tensor_tensor(self.sums[:, :, :].rearrange("p h (i j) -> p h i j", i=K), a, b, ALU.add))
        own.settle()

    def search(self, v, own, S, tb, half):
        at = PEER_HEADS // 2 * half
        top16(v, own, lambda i: self.sums[:, at + i, :], lambda i: self.spare[:, at + i, :],
              lambda i: self.best[:, at + i, :], lambda i: self.best_at[:, at + i, :], PEER_HEADS // 2)

    def split_places(self, v, own, S, tb):
        v.tensor_tensor(self.shifted(tb), self.best[:, :, :],
                        self.best[:, :, 0:1].broadcast_to([P, PEER_HEADS, TOPK]), ALU.subtract)\
         .then_inc(S["shifted"], 1)
        flat_at = self.best_at[:, :, :].rearrange("p h i -> p (h i)")
        own.did(v.tensor_scalar(self.place[:, 0, :], flat_at, 4, None, ALU.logical_shift_right))
        own.did(v.tensor_scalar(self.place[:, 1, :], flat_at, TOPK - 1, None, ALU.bitwise_and))
        own.settle()
        own.did(v.tensor_copy(self.place_f[:, :, :], self.place[:, :, :]))
        own.settle()

    def number(self, v, own, S, tb, part):
        H, K = PEER_HEADS, TOPK
        hot4 = self.hot[:, :, :].rearrange("p (h n) j -> p h n j", h=H)
        numbers = self.top_n[:, :, :].rearrange("p (h two) i -> p h two i", two=2)[:, :, part, :]
        own.did(v.tensor_tensor(self.hot[:, :, :], self.place_f[:, part, :].unsqueeze(2).broadcast_to([P, H * K, K]),
                                over(self.iota, H * K), ALU.is_equal))
        own.settle()
        own.did(v.tensor_tensor(hot4, hot4, numbers.unsqueeze(2).broadcast_to([P, H, K, K]), ALU.mult))
        own.settle()
        own.did(v.tensor_reduce(self.key[:, part, :], self.hot[:, :, :], AX.X, ALU.add))
        own.settle()

    def finish(self, v, own, S, tb):
        own.did(v.scalar_tensor_tensor(self.key[:, 0, :], self.key[:, 0, :], float(PEER_KEYS), self.key[:, 1, :],
                                       ALU.mult, ALU.add))
        own.settle()
        v.tensor_copy(self.experts[:, tb, :], self.key[:, 0, :]).then_inc(S["routed"], 1)
        v.wait_ge(S["gate_exps"], tb + 1)
        own.did(v.tensor_reduce(self.total[:, :], self.shifted(tb), AX.X, ALU.add))
        own.settle()
        own.did(v.reciprocal(self.total[:, :], self.total[:, :]))
        own.settle()
        own.did(v.tensor_tensor(self.shifted(tb), self.shifted(tb),
                                self.total[:, :].unsqueeze(2).broadcast_to([P, PEER_HEADS, TOPK]), ALU.mult))


def peer_experts(k, tokens, top, top_at):
    S, stale = k.stage()
    R = GATHER_RING
    BETWEEN = 12
    with ExitStack() as ctx:
        route = Route(k, ctx, top, top_at)
        experts, gates = route.experts, route.gates
        rows = k.sbuf(ctx, "expert_rows", R, D)
        dots = k.sbuf(ctx, "expert_dots", TB, SLOTS)
        waste = k.sbuf(ctx, "products", 2, D)
        out = k.sbuf(ctx, "expert_sums", TB, 2, D)
        gathers = [(table, tb, s) for table in ("peer_u", "peer_v") for tb in range(TB) for s in range(SLOTS)]
        rows_ready = k.rows_ready
        with k.nc.Block() as block:
            @block.sync
            def _(sp):
                clear(sp, stale)

            @block.gpsimd
            def _(pool):
                for i, (table, tb, s) in enumerate(gathers):
                    if table == "peer_u" and s == 0:
                        pool.wait_ge(S["routed"], tb + 1)
                    if i >= R:
                        pool.wait_ge(S["rows_used"], i - R + 1)
                    pool.indirect_dma_start(
                        out=rows[:, i % R, :], out_offset=None, in_=k.dram[table],
                        in_offset=bass.IndirectOffsetOnAxis(ap=experts[:, tb, s:s + 1], axis=0),
                    ).then_inc(rows_ready[i % R], 16)

            @block.scalar
            def _(act):
                for tb in range(TB):
                    act.wait_ge(S["shifted"], tb + 1)
                    act.activation(gates[:, tb, :], gates[:, tb, :], ACT.Exp).then_inc(S["gate_exps"], 1)
                for tb in range(TB):
                    act.wait_ge(S["rows_used"], SLOTS * (tb + 1))
                    act.activation(dots[:, tb, :], dots[:, tb, :], ACT.Gelu).then_inc(S["gelus"], 1)

            @block.vector
            def _(v):
                own = Steps(v, S["vector_steps"])
                for step in route.steps:
                    step(v, own, S, 0)
                for i, (table, tb, s) in enumerate(gathers):
                    if i % BETWEEN == BETWEEN // 2 and i // BETWEEN < len(route.steps):
                        route.steps[i // BETWEEN](v, own, S, 1)
                    v.wait_ge(rows_ready[i % R], 16 * (i // R + 1))
                    row = rows[:, i % R, :]
                    if table == "peer_u":
                        if i >= 2:
                            v.wait_ge(S["rows_used"], i - 1)
                        v.tensor_tensor_reduce(out=waste[:, i % 2, :], in0=row, in1=tokens[:, tb, :], scale=1.0,
                                               scalar=0.0, op0=ALU.mult, op1=ALU.add,
                                               accum_out=dots[:, tb, s:s + 1]).then_inc(S["rows_used"], 1)
                        continue
                    if s == 0:
                        own.settle()
                        v.wait_ge(S["gelus"], tb + 1)
                        v.tensor_tensor(gates[:, tb, :], gates[:, tb, :], dots[:, tb, :], ALU.mult)\
                         .then_inc(S["weighted"], 1)
                        v.wait_ge(S["weighted"], tb + 1)
                    acc = out[:, tb, s % 2, :]
                    if s < 2:
                        ins = v.tensor_scalar(acc, row, gates[:, tb, s:s + 1], None, ALU.mult)
                    else:
                        v.wait_ge(S["rows_used"], i - 1)
                        ins = v.scalar_tensor_tensor(acc, row, gates[:, tb, s:s + 1], acc, ALU.mult, ALU.add)
                    ins.then_inc(S["rows_used"], 1)
                    if s == SLOTS - 1:
                        v.wait_ge(S["rows_used"], i + 1)
                        v.tensor_tensor(out[:, tb, 0, :], out[:, tb, 0, :], out[:, tb, 1, :], ALU.add)\
                         .then_inc(S["sums_ready"], 1)
                for tb in range(TB):
                    for half in range(2):
                        v.wait_ge(S["transposed"], 2 * tb + half + 1)
                        part = k.x[:, 4 * half:4 * half + 4, P * tb:P * tb + P]
                        v.tensor_tensor(part, part, four(k.ps[:, 2 * tb + half, :]), ALU.add)

            @block.tensor
            def _(pe):
                for tb in range(TB):
                    pe.wait_ge(S["sums_ready"], tb + 1)
                    for half in range(2):
                        for t in range(4):
                            at = P * (4 * half + t)
                            last = pe.transpose(k.ps[:, 2 * tb + half, P * t:P * t + P],
                                                out[:, tb, 0, at:at + P], k.const("identity"))
                        last.then_inc(S["transposed"], 1)


def ffn(k, name):
    S, stale = k.stage()
    first = k.w.taken

    def up_done(f):
        return first + 2 * (f + 1) + max(f - 1, 0)

    with ExitStack() as ctx:
        sb = lambda name, *shape: k.sbuf(ctx, name, *shape)
        x_parts, h_parts = k.pair(ctx, "moving", KT, T), k.pair(ctx, "hidden", 2, T)
        gate, up, hidden = sb("gate", 2, T), sb("up", 2, T), sb("hidden_full", 2, T)
        squares, y, scale = sb("squares", KT, T), sb("ffn_out", KT, T), sb("inverse_rms", 3, T)
        acc = k.ps[:, 4:8, :].rearrange("p b (two n) -> p (b two) n", two=2)
        with k.nc.Block() as block:
            @block.sync
            def _(sp):
                clear(sp, stale)
                k.w.load_ahead(sp, first, 3 * FT)

            @block.tensor
            def _(pe):
                def down(f):
                    tiles = k.w.arrived(pe)
                    pe.wait_ge(S["hidden_ready"], f + 1)
                    moving = h_parts[:, f % 2, :]
                    for o in range(KT):
                        for n, (w, m) in enumerate(((tiles.high, moving.high), (tiles.high, moving.low),
                                                    (tiles.low, moving.high))):
                            last = pe.matmul(acc[:, o, :], w[:, o, :], m, start=f == n == 0 and o % 2 == 0,
                                             stop=f == FT - 1 and n == 2, skip_group_check=True)
                    last.then_inc(k.w.used, 1)

                for f in range(FT):
                    if f >= 2:
                        pe.wait_ge(S["hidden_ready"], f - 1)
                    for b in range(2):
                        tiles = k.w.arrived(pe)
                        for t in range(KT):
                            if f == b == 0:
                                pe.wait_ge(S["parts_ready"], t + 1)
                            last = product(pe, k.ps[:, 2 * (f % 2) + b, 0:T], tiles[:, t, :], x_parts[:, t, :],
                                           start=t == 0, stop=t == KT - 1)
                        last.then_inc(k.w.used, 1)
                        if f == b == 0:
                            for t in range(KT):
                                if t % 4 == 0:
                                    pe.wait_ge(S["squares_ready"], t // 4 + 1)
                                last = pe.matmul(k.ps[:, 4, 0:T], k.const("ones"), squares[:, t, :],
                                                 start=t == 0, stop=t == KT - 1)
                            last.then_inc(S["sum_ready"], 1)
                    if f:
                        down(f - 1)
                down(FT - 1)
                for t in range(KT):
                    if t % 2 == 0:
                        pe.wait_ge(S["squares_ready"], 2 + t // 2 + 1)
                    last = pe.matmul(k.ps[:, 0, 0:T], k.const("ones"), squares[:, t, :],
                                     start=t == 0, stop=t == KT - 1)
                last.then_inc(S["sum_ready"], 1)

            @block.scalar
            def _(act):
                for half in range(2):
                    part = slice(4 * half, 4 * half + 4)
                    act.activation(squares[:, part, :], k.x[:, part, :], ACT.Square)\
                       .then_inc(S["squares_ready"], 1)
                k.w.round_high(act, first + 1)
                act.wait_ge(S["mean_ready"], 1)
                act.activation(scale[:, 1, :], scale[:, 0, :], ACT.Sqrt).then_inc(S["root_ready"], 1)
                for f in range(FT):
                    act.wait_ge(S["gate_scaled"], f + 1)
                    act.activation(gate[:, f % 2, :], gate[:, f % 2, :], ACT.Silu).then_inc(S["gate_ready"], 1)
                    k.w.round_high(act, up_done(f + 1) if f + 1 < FT else first + 3 * FT)
                for b in range(4):
                    act.wait_ge(k.w.used, first + 3 * FT)
                    act.activation(squares[:, 2 * b:2 * b + 2, :], acc[:, 2 * b:2 * b + 2, :], ACT.Square)\
                       .then_inc(S["squares_ready"], 1)
                act.wait_ge(S["mean_ready"], 2)
                act.activation(scale[:, 1, :], scale[:, 0, :], ACT.Sqrt).then_inc(S["root_ready"], 1)

            @block.vector
            def _(v):
                own = Steps(v, S["vector_steps"])
                for t in range(KT):
                    g = k.column(f"{name}_pre_g_2", t)
                    own.did(v.tensor_scalar(x_parts.high[:, t, :], k.x[:, t, :], g, None, ALU.mult))
                    own.settle()
                    v.scalar_tensor_tensor(x_parts.low[:, t, :], k.x[:, t, :], g, x_parts.high[:, t, :].bitcast(F32),
                                           ALU.mult, ALU.subtract).then_inc(S["parts_ready"], 1)
                k.w.split_low(v, first + 1)

                def inverse_rms(n, bank, factor):
                    v.wait_ge(S["sum_ready"], n)
                    v.tensor_scalar(scale[:, 0, :], k.ps[:, bank, 0:T], 1.0 / D, EPS, ALU.mult, ALU.add)\
                     .then_inc(S["mean_ready"], 1)
                    v.wait_ge(S["root_ready"], n)
                    own.did(v.reciprocal(scale[:, 2, :], scale[:, 1, :]))
                    own.settle()
                    if factor != 1:
                        own.did(v.tensor_scalar(scale[:, 2, :], scale[:, 2, :], factor, None, ALU.mult))
                        own.settle()

                inverse_rms(1, 4, 1)
                for f in range(FT):
                    v.wait_ge(k.w.used, up_done(f) - 1)
                    v.tensor_tensor(gate[:, f % 2, :], k.ps[:, 2 * (f % 2), 0:T], scale[:, 2, :], ALU.mult)\
                     .then_inc(S["gate_scaled"], 1)
                    k.w.split_low(v, up_done(f) - 1)
                    v.wait_ge(k.w.used, up_done(f))
                    own.did(v.tensor_tensor(up[:, f % 2, :], k.ps[:, 2 * (f % 2) + 1, 0:T], scale[:, 2, :], ALU.mult))
                    own.settle()
                    v.wait_ge(S["gate_ready"], f + 1)
                    own.did(v.tensor_tensor(hidden[:, f % 2, :], gate[:, f % 2, :], up[:, f % 2, :], ALU.mult))
                    own.settle()
                    if f >= 2:
                        v.wait_ge(k.w.used, first + 3 * (f - 2) + 5)
                    own.did(v.tensor_copy(h_parts.high[:, f % 2, :], hidden[:, f % 2, :]))
                    own.settle()
                    v.tensor_tensor(h_parts.low[:, f % 2, :], hidden[:, f % 2, :],
                                    h_parts.high[:, f % 2, :].bitcast(F32), ALU.subtract)\
                     .then_inc(S["hidden_ready"], 1)
                    k.w.split_low(v, up_done(f))
                    if f + 1 < FT:
                        k.w.split_low(v, up_done(f) + (f > 0))
                k.w.split_low(v, first + 3 * FT)
                for t in range(KT):
                    v.wait_ge(S["squares_ready"], 2 + t // 2 + 1)
                    own.did(v.tensor_scalar(y[:, t, :], acc[:, t, :], k.column(f"{name}_post_g_2", t), None, ALU.mult))
                inverse_rms(2, 0, 0.5)
                for half in range(2):
                    part = slice(4 * half, 4 * half + 4)
                    own.did(v.tensor_tensor(y[:, part, :], y[:, part, :], over(scale[:, 2, :], 4), ALU.mult))
                own.settle()
                v.tensor_tensor(k.x[:, :, :], k.x[:, :, :], y[:, :, :], ALU.add)


def nsa_mixer(k):
    with ExitStack() as ctx:
        sb = lambda name, *shape: k.sbuf(ctx, name, *shape)
        m = {"q": sb("nsa_q", 4, T), "cmp_in": sb("cmp_in", 2, 2, T), "k_sw": sb("nsa_k", 2, T),
             "v_sw": sb("nsa_v", TB, 2, P), "conv": sb("conv_in2", 12, T), "w_g": sb("w_g", KT, 24),
             "gates": sb("nsa_gates", TB, 24), "o": sb("nsa_o", KT, T),
             "kc": sb("kc", N_CMP), "vc": sb("vc", P), "parts": k.pair(ctx, "moving", KT, T)}
        rmsnorm(k, k.x, "l0_mix_pre_g_2", k.xn, parts=m["parts"])
        nsa_project(k, m)
        nsa_compress(k, m)
        nsa_heads(k, m)
        short_conv(k, m)
        project_from(k, m["o"], k.xn, m["parts"], add=False)
        rmsnorm(k, k.xn, "l0_mix_post_g_2", k.x, residual=1)


def nsa_project(k, m):
    S, stale = k.stage()
    first = k.w.taken
    ring = lambda i: i if i < 10 else i - 2
    with k.nc.Block() as block:
        @block.sync
        def _(sp):
            clear(sp, stale)
            sp.dma_start(m["w_g"][:, :, :], k.dram["w_g"]).then_inc(S["small_loaded"], 16)
            k.w.load_ahead(sp, first, NSA_CHUNKS)

        @block.tensor
        def _(pe):
            pe.wait_ge(S["small_loaded"], 16)
            for tb in range(TB):
                for t in range(KT):
                    last = pe.matmul(k.ps[:, 6, 24 * tb:24 * tb + 24], k.xn[:, t, P * tb:P * tb + P],
                                     m["w_g"][:, t, :], start=t == 0, stop=t == KT - 1)
            last.then_inc(S["gates_ready"], 1)
            for i in range(NSA_CHUNKS):
                if i in (10, 11):
                    token_chunk(k, pe, m["parts"], i - 10, 2 * P)
                    continue
                if ring(i) >= 4:
                    pe.wait_ge(S["copied"], ring(i) - 3)
                feature_tiles(k, pe, ring(i) % 4, m["parts"], k.w.arrived(pe))

        @block.scalar
        def _(act):
            act.wait_ge(S["gates_ready"], 1)
            act.activation(m["gates"][:, :, :], k.ps[:, 6, 0:48].rearrange("p (b n) -> p b n", b=TB), ACT.Sigmoid)
            for i in range(NSA_CHUNKS):
                k.w.round_high(act, first + i + 1)

        @block.vector
        def _(v):
            for i in range(NSA_CHUNKS):
                v.wait_ge(k.w.used, first + i + 1)
                src = k.ps[:, ring(i) % 4, 0:T]
                if i < 4:
                    ins = v.tensor_scalar(m["q"][:, i, :], src, NSA_DIM ** -0.5, None, ALU.mult)
                elif i < 8:
                    ins = v.tensor_copy(m["cmp_in"][:, (i - 4) // 2, i % 2, :], src)
                elif i < 10:
                    ins = v.tensor_copy(m["k_sw"][:, i % 2, :], src)
                elif i >= 12:
                    ins = v.tensor_copy(m["conv"][:, i - 12, :], src)
                if i in (10, 11):
                    if i == 11:
                        v.tensor_copy(m["v_sw"][:, :, :, :].rearrange("p b two n -> p b (two n)"),
                                      k.ps[:, 4:6, 0:2 * P])
                else:
                    ins.then_inc(S["copied"], 1)
                k.w.split_low(v, first + i + 1)


def nsa_compress(k, m):
    S, stale = k.stage()
    TAPS = CMP_STRIDE
    with ExitStack() as ctx:
        sb = lambda name, *shape: k.sbuf(ctx, name, *shape)
        w1, w2, pos = sb("cmp_w1", 2, TAPS, P), sb("cmp_w2", 2, NSA_DIM), sb("cmp_pos", 2, TAPS)
        blocks, hidden = sb("cmp_blocks", 2, TAPS, NSA_GROUPS, N_CMP), sb("cmp_hidden", 4, N_CMP)
        with k.nc.Block() as block:
            @block.sync
            def _(sp):
                clear(sp, stale)
                sp.dma_start(pos[:, :, :], k.dram["cmp_pos"]).then_inc(S["pos_loaded"], 16)
                sp.dma_start(w1[:, :, :, :], k.dram["cmp_w1"]).then_inc(S["w1_loaded"], 16)
                sp.dma_start(w2[:, :, :], k.dram["cmp_w2"]).then_inc(S["w2_loaded"], 16)

            @block.vector
            def _(v):
                v.wait_ge(S["pos_loaded"], 16)
                for kv in range(2):
                    for g in range(NSA_GROUPS):
                        taps = m["cmp_in"][:, kv, g, :].rearrange("p (n s) -> p s n", s=TAPS)
                        for a in range(2):
                            half = slice(64 * a, 64 * a + 64)
                            v.tensor_tensor(blocks[half, kv, :, g, :], taps[half, :, a:a + N_CMP],
                                            pos[half, kv, :].unsqueeze(2).broadcast_to([64, TAPS, N_CMP]), ALU.add)\
                             .then_inc(S["blocks_ready"], 1)
                v.wait_ge(S["keys_ready"], 1)
                for g in range(NSA_GROUPS):
                    half = slice(64 * g, 64 * g + 64)
                    v.tensor_copy(m["kc"][half, :], k.ps[half, 4 + g, 0:N_CMP])
                v.tensor_copy(m["vc"][0:N_CMP, :], k.ps[0:N_CMP, 6, 0:P])

            @block.tensor
            def _(pe):
                pe.wait_ge(S["w1_loaded"], 16)
                for kv in range(2):
                    pe.wait_ge(S["blocks_ready"], 4 * kv + 4)
                    for i in range(TAPS):
                        last = pe.matmul(k.ps[:, kv, 0:NSA_GROUPS * N_CMP], w1[:, kv, i, :],
                                         blocks[:, kv, i, :, :].rearrange("p g n -> p (g n)"),
                                         start=i == 0, stop=i == TAPS - 1)
                    last.then_inc(S["hidden_ready"], 1)
                pe.wait_ge(S["w2_loaded"], 16)
                pe.wait_ge(S["gelus"], 2)
                for g in range(NSA_GROUPS):
                    pe.matmul(k.ps[64 * g:64 * g + 64, 4 + g, 0:N_CMP], w2[:, 0, :], hidden[:, g, :],
                              start=True, stop=True)
                    last = pe.matmul(k.ps[0:N_CMP, 6, 64 * g:64 * g + 64], hidden[:, 2 + g, :], w2[:, 1, :],
                                     start=True, stop=True)
                last.then_inc(S["keys_ready"], 1)

            @block.scalar
            def _(act):
                for kv in range(2):
                    act.wait_ge(S["hidden_ready"], kv + 1)
                    act.activation(hidden[:, 2 * kv:2 * kv + 2, :],
                                   k.ps[:, kv, 0:NSA_GROUPS * N_CMP].rearrange("p (g n) -> p g n", n=N_CMP),
                                   ACT.Gelu_apprx_tanh).then_inc(S["gelus"], 1)


def nsa_heads(k, m):
    S, stale = k.stage()
    N = NSA_HEADS * TB
    CMP = 2 * T
    with ExitStack() as ctx:
        p = k.sbuf(ctx, "nsa_probs", N, CMP + 16)
        p_t = k.sbuf(ctx, "nsa_probs_t", 4, 4, P)
        c_t = k.sbuf(ctx, "nsa_cmp_t", 4, P)
        top, total = k.sbuf(ctx, "nsa_max", N, 3), k.sbuf(ctx, "nsa_sum", N, 3)

        def at(i):
            h, tb = i // TB, i % TB
            g = h // NSA_REP
            return h, tb, P * (tb + 1), slice(64 * g, 64 * g + 64), h % NSA_REP, slice(P * tb, P * tb + P)

        def wide(i, ap):
            return ap.rearrange("p (two n) -> p two n", two=2)[:, :, 0:at(i)[2]]

        with k.nc.Block() as block:
            @block.sync
            def _(sp):
                clear(sp, stale)

            @block.tensor
            def _(pe):
                for i in range(N):
                    h, tb, keys, half, j, tok = at(i)
                    if i >= 2:
                        pe.wait_ge(S["biased"], i - 1)
                    q = m["q"][half, j, tok]
                    for b in range(2):
                        pe.matmul(k.ps[:, i % 2, T * b:T * b + keys], q, m["k_sw"][half, b, 0:keys],
                                  start=True, stop=True)
                    pe.matmul(k.ps[:, 2 + i % 2, 0:N_CMP], q, m["kc"][half, :], start=True, stop=True)\
                      .then_inc(S["scores_ready"], 1)
                pe.wait_ge(S["biased"], N)
                for i in range(N + 1):
                    if i < N:
                        h, tb, keys, half, j, tok = at(i)
                        pe.wait_ge(S["probs_ready"], i + 1)
                        if i >= 2:
                            pe.wait_ge(S["transposed_out"], i - 1)
                        for b in range(2):
                            for c in range(tb + 1):
                                pe.transpose(k.ps[:, 4 + i % 2, P * (2 * b + c):P * (2 * b + c) + P],
                                             p[:, i, T * b + P * c:T * b + P * c + P], k.const("identity"))
                        pe.transpose(k.ps[0:N_CMP, 2 + i % 2, 0:P], p[:, i, CMP:CMP + N_CMP],
                                     k.const("identity")).then_inc(S["transposed"], 1)
                    if i:
                        n = i - 1
                        h, tb, keys, half, j, tok = at(n)
                        pe.wait_ge(S["transposed_out"], n + 1)
                        if n >= 2:
                            pe.wait_ge(S["outputs_out"], n - 1)
                        out = k.ps[half, 6 + n % 2, 0:P]
                        pe.matmul(out, m["vc"][0:N_CMP, half], c_t[0:N_CMP, n % 4, :], start=True, stop=False)
                        for b in range(2):
                            for c in range(tb + 1):
                                last = pe.matmul(out, m["v_sw"][:, c, b, half], p_t[:, n % 4, 2 * b + c, :],
                                                 start=False, stop=b == 1 and c == tb)
                        last.then_inc(S["outputs_ready"], 1)

            @block.vector
            def _(v):
                own = Steps(v, S["vector_steps"])
                for i in range(N):
                    h, tb, keys, half, j, tok = at(i)
                    slope = 2.0 ** -(h + 1)
                    v.wait_ge(S["scores_ready"], i + 1)
                    delta = k.consts[:, CONST_ROWS.index("causal0"), :] if tb == 0 else \
                        k.consts[:, CONST_ROWS.index("causal1a"):CONST_ROWS.index("causal1b") + 1, :]\
                         .rearrange("p a n -> p (a n)")
                    far = k.const("misc")[:, N_CMP * tb:N_CMP * tb + N_CMP]
                    v.scalar_tensor_tensor(wide(i, p[:, i, 0:CMP]), over(delta, 2), slope,
                                           wide(i, k.ps[:, i % 2, :]), ALU.mult, ALU.add)
                    v.scalar_tensor_tensor(p[:, i, CMP:CMP + N_CMP], far, slope, k.ps[:, 2 + i % 2, 0:N_CMP],
                                           ALU.mult, ALU.add).then_inc(S["biased"], 1)
                    v.wait_ge(S["biased"], i + 1)
                    own.did(v.reduce_max(top[:, i, 1:3], wide(i, p[:, i, 0:CMP]), AX.X))
                    own.did(v.reduce_max(top[:, i, 0:1], p[:, i, CMP:CMP + N_CMP], AX.X))
                    own.settle()
                    v.tensor_scalar(top[:, i, :], top[:, i, :], CLAMP, -1.0, ALU.max, ALU.mult)\
                     .then_inc(S["max_ready"], 1)
                for i in range(N):
                    h, tb, keys, half, j, tok = at(i)
                    v.wait_ge(S["exps_ready"], i + 1)
                    own.did(v.tensor_scalar(total[:, i, :], total[:, i, :], 1e-30, None, ALU.max))
                    own.settle()
                    own.did(v.reciprocal(total[:, i, :], total[:, i, :]))
                    own.settle()
                    own.did(v.tensor_tensor(total[:, i, :], total[:, i, :], m["gates"][:, tb, 3 * h:3 * h + 3], ALU.mult))
                    own.settle()
                    for b in range(2):
                        part = p[:, i, T * b:T * b + keys]
                        v.tensor_scalar(part, part, total[:, i, b + 1:b + 2], None, ALU.mult)
                    part = p[:, i, CMP:CMP + N_CMP]
                    v.tensor_scalar(part, part, total[:, i, 0:1], None, ALU.mult).then_inc(S["probs_ready"], 1)

            @block.scalar
            def _(act):
                for i in range(N):
                    h, tb, keys, half, j, tok = at(i)
                    act.wait_ge(S["max_ready"], i + 1)
                    for b, part in enumerate((p[:, i, CMP:CMP + N_CMP], p[:, i, 0:keys], p[:, i, T:T + keys])):
                        last = act.activation(part, part, ACT.Exp, bias=top[:, i, b:b + 1],
                                              accum_out=total[:, i, b:b + 1])
                    last.then_inc(S["exps_ready"], 1)
                for i in range(N + 1):
                    if i < N:
                        h, tb, keys, half, j, tok = at(i)
                        act.wait_ge(S["transposed"], i + 1)
                        if i >= 4:
                            act.wait_ge(S["outputs_ready"], i - 3)
                        act.activation(p_t[:, i % 4, :, :].rearrange("p (b c) n -> p b c n", b=2)[:, :, 0:tb + 1, :],
                                       k.ps[:, 4 + i % 2, :].rearrange("p (b c n) -> p b c n", b=2, c=2)[:, :, 0:tb + 1, :],
                                       ACT.Copy)
                        act.activation(c_t[0:N_CMP, i % 4, :], k.ps[0:N_CMP, 2 + i % 2, 0:P], ACT.Copy)\
                           .then_inc(S["transposed_out"], 1)
                    if i:
                        h, tb, keys, half, j, tok = at(i - 1)
                        act.wait_ge(S["outputs_ready"], i)
                        act.activation(m["o"][half, j, tok], k.ps[half, 6 + (i - 1) % 2, 0:P], ACT.Copy)\
                           .then_inc(S["outputs_out"], 1)


def short_conv(k, m):
    S, stale = k.stage()
    pad = CONV2_TAPS - 1
    c, o = m["conv"], m["o"]
    with ExitStack() as ctx:
        z = k.sbuf(ctx, "conv_z", 4, T + pad)
        with k.nc.Block() as block:
            @block.sync
            def _(sp):
                clear(sp, stale)

            @block.vector
            def _(v):
                own = Steps(v, S["vector_steps"])
                own.did(v.memset(z[:, :, 0:pad], 0.0))
                own.did(v.tensor_tensor(z[:, :, pad:pad + T], c[:, 4:8, :], c[:, 8:12, :], ALU.mult))
                for tap in range(CONV2_TAPS):
                    own.settle()
                    for i in range(4):
                        w, x, y = k.column("l0_conv_w_2", CONV2_TAPS * i + tap), z[:, i, tap:tap + T], o[:, 4 + i, :]
                        if tap == 0:
                            own.did(v.tensor_scalar(y, x, w, k.column("l0_conv_b_2", i), ALU.mult, ALU.add))
                        else:
                            own.did(v.scalar_tensor_tensor(y, x, w, y, ALU.mult, ALU.add))
                own.settle()
                v.tensor_tensor(o[:, 4:8, :], o[:, 4:8, :], c[:, 0:4, :], ALU.mult)


def rwkv_mixer(k):
    with ExitStack() as ctx:
        sb = lambda name, *shape: k.sbuf(ctx, name, *shape)
        m = {"v_tok": sb("v_tok", TB, D), "g": sb("rwkv_g", KT, T), "bonus": sb("bonus", KT, T),
             "ar": sb("a_and_r", KT, TB, 2, P), "bk": sb("b_and_k", 2, KT, T), "carry": sb("carry", KT)}
        m |= {"a": m["bk"][:, 0, :, :], "k": m["bk"][:, 1, :, :], "r": m["ar"][:, :, :, 1, :]}
        with ExitStack() as early:
            eb = lambda name, *shape: k.sbuf(early, name, *shape)
            m |= {"sig": eb("decay_sigmoid", KT, T), "v": eb("rwkv_v", KT, T)}
            with ExitStack() as shifted:
                m["h"] = k.sbuf(shifted, "h_shifted", KT, T + 1)
                rmsnorm(k, k.x, "l1_mix_pre_g_2", m["h"][:, :, 1:T + 1])
                rwkv_project(k, m)
            rwkv_prepare(k, m)
            m["bk_tok"] = m["sig"][:, :, :].rearrange("p k n -> p (k n)").rearrange("p (i d) -> p i d", i=2)
            rwkv_transpose(k, m)
            rwkv_chunks(k, m)
        rwkv_norm(k, m)
        with ExitStack() as late:
            parts = k.pair(late, "moving", KT, T)
            project_from(k, k.xn, m["g"], parts, add=False)
        rmsnorm(k, m["g"], "l1_mix_post_g_2", k.x, residual=1)


def rwkv_project(k, m):
    S, stale = k.stage()
    first = k.w.taken
    MU = (1, 4, 5, 0, 2, 3)
    with ExitStack() as ctx:
        sb = lambda name, *shape: k.sbuf(ctx, name, *shape)
        down = [sb("w_dec1", KT, LORA), sb("w_a1", KT, LORA), sb("w_g1", KT, GATE_LORA)]
        up = [sb("w_dec2", D), sb("w_a2", D), sb("w_g2", D)]
        hidden = sb("lora_hidden", 3, T)
        full = m["bonus"][:, :, :], m["v_tok"][:, :, :].rearrange("p b n -> p (b n)").rearrange("p (k n) -> p k n", n=T)
        delta, mix = k.xn, [k.pair(ctx, f"mixed{i}", KT, T) for i in range(2)]
        width = (LORA, LORA, GATE_LORA)
        with k.nc.Block() as block:
            @block.sync
            def _(sp):
                clear(sp, stale)
                for n, name in enumerate(("dec", "a", "g")):
                    sp.dma_start(down[n][:, :, :], k.dram[f"w_{name}1"]).then_inc(S["lora_loaded"], 16)
                    sp.dma_start(up[n][0:width[n], :], k.dram[f"w_{name}2"]).then_inc(S["lora_loaded"], 16)
                k.w.load_ahead(sp, first, 3 * KT)

            @block.vector
            def _(v):
                own = Steps(v, S["vector_steps"])
                h = m["h"]

                def make_full(n):
                    for t in range(KT):
                        last = v.scalar_tensor_tensor(full[n % 2][:, t, :], delta[:, t, :],
                                                      k.column("l1_mu_2", KT * MU[n] + t), h[:, t, 1:T + 1],
                                                      ALU.mult, ALU.add)
                    last.then_inc(S["mixed"], 1)

                def make_low(n):
                    v.wait_ge(S["high_ready"], n - 2)
                    v.tensor_tensor(mix[n % 2].low[:, :, :], full[n % 2], mix[n % 2].high[:, :, :].bitcast(F32),
                                    ALU.subtract).then_inc(S["low_ready"], 1)

                own.did(v.memset(h[:, :, 0:1], 0.0))
                own.settle()
                own.did(v.tensor_tensor(delta[:, :, :], h[:, :, 0:T], h[:, :, 1:T + 1], ALU.subtract))
                own.settle()
                for n in range(5):
                    if n >= 2:
                        v.wait_ge(S["mix_used"], n - 1)
                    make_full(n)
                    if n >= 3:
                        make_low(n)
                for c in range(3 * KT):
                    v.wait_ge(k.w.used, first + c + 1)
                    k.w.split_low(v, first + c + 1)
                    if c == KT - 1:
                        make_full(5)
                        make_low(5)

            @block.tensor
            def _(pe):
                pe.wait_ge(S["lora_loaded"], 6 * 16)
                for n in range(3):
                    pe.wait_ge(S["mixed"], n + 1)
                    for t in range(KT):
                        last = pe.matmul(k.ps[0:width[n], 4 + n % 2, 0:T], down[n][:, t, :], full[n % 2][:, t, :],
                                         start=t == 0, stop=t == KT - 1)
                    last.then_inc(S["mix_used"], 1)
                    pe.wait_ge(S["hidden_ready"], n + 1)
                    for t in range(KT):
                        c = KT * n + t
                        if c >= 2:
                            pe.wait_ge(S["lora_out"], c - 1)
                        pe.matmul(k.ps[:, 6 + c % 2, 0:T], up[n][0:width[n], P * t:P * t + P], hidden[0:width[n], n, :],
                                  start=True, stop=True).then_inc(S["lora_ready"], 1)
                for c in range(3 * KT):
                    n = 3 + c // KT
                    pe.wait_ge(S["low_ready"], n - 2)
                    if c >= 4:
                        pe.wait_ge(S["copied"], c - 3)
                    feature_tiles(k, pe, c % 4, mix[n % 2], k.w.arrived(pe))

            @block.scalar
            def _(act):
                def make_high(n):
                    act.wait_ge(S["mixed"], n + 1)
                    if n == 5:
                        act.wait_ge(k.w.used, first + KT)
                    act.activation(mix[n % 2].high[:, :, :], full[n % 2], ACT.Copy).then_inc(S["high_ready"], 1)

                for n in range(3):
                    act.wait_ge(S["mix_used"], n + 1)
                    act.activation(hidden[0:width[n], n, :], k.ps[0:width[n], 4 + n % 2, 0:T],
                                   (ACT.Tanh, ACT.Copy, ACT.Sigmoid)[n]).then_inc(S["hidden_ready"], 1)
                    if n == 2:
                        make_high(3)
                    for t in range(KT):
                        c = KT * n + t
                        act.wait_ge(S["lora_ready"], c + 1)
                        src = k.ps[:, 6 + c % 2, 0:T]
                        if n == 0:
                            ins = act.activation(m["sig"][:, t, :], src, ACT.Sigmoid, bias=k.column("l1_w0_2", t))
                        elif n == 1:
                            ins = act.activation(m["a"][:, t, :], src, ACT.Sigmoid, bias=k.column("l1_a0_2", t))
                        else:
                            ins = act.activation(m["g"][:, t, :], src, ACT.Copy)
                        ins.then_inc(S["lora_out"], 1)
                make_high(4)
                for c in range(3 * KT):
                    act.wait_ge(k.w.used, first + c + 1)
                    src, t = k.ps[:, c % 4, 0:T], c % KT
                    if c < KT:
                        src, out = src.rearrange("p (b n) -> p b n", b=TB), m["r"][:, t, :, :]
                    else:
                        out = m["k" if c < 2 * KT else "v"][:, t, :]
                    act.activation(out, src, ACT.Copy).then_inc(S["copied"], 1)
                    k.w.round_high(act, first + c + 1)
                    if c == KT - 1:
                        make_high(5)


def make_spread(k, v, spread):
    return v.tensor_copy(spread[0:RW_HEADS, :, :], k.const("identity")[0:RW_HEADS, 0:RW_HEADS].unsqueeze(2)
                         .broadcast_to([RW_HEADS, RW_HEADS, RW_DIM]))


def spread_rows(k, pe, spread, rows, bank):
    for t in range(KT):
        last = pe.matmul(k.ps[:, bank + t // 2, T * (t % 2):T * (t % 2) + T],
                         spread[0:RW_HEADS, 2 * t:2 * t + 2, :].rearrange("p h n -> p (h n)"),
                         rows[0:RW_HEADS, :], start=True, stop=True)
    return last


def rwkv_prepare(k, m):
    S, stale = k.stage()
    RATE = -float(np.exp(-0.5))
    with ExitStack() as ctx:
        sb = lambda name, *shape: k.sbuf(ctx, name, *shape)
        kk, squares, rk, run = sb("kk", KT, T), sb("squares", KT, T), sb("r_times_k", KT, T), k.xn
        before, inverse = sb("decay_before", KT, T), sb("inverse_decay", KT, T)
        middle, spread, norm = sb("middle", KT, TB), sb("spread", RW_HEADS, RW_DIM), sb("norms", 2, T)
        c3 = lambda ap: ap.rearrange("p (b n) -> p b n", b=TB)
        c4 = lambda ap: ap.rearrange("p k (b n) -> p k b n", b=TB)
        two = lambda tile, q: tile[:, 2 * q:2 * q + 2, :].rearrange("p k n -> p (k n)")
        ar = m["ar"]
        with k.nc.Block() as block:
            @block.sync
            def _(sp):
                clear(sp, stale)

            @block.vector
            def _(v):
                own = Steps(v, S["vector_steps"])
                for t in range(KT):
                    v.tensor_scalar(kk[:, t, :], m["k"][:, t, :], k.column("l1_k_k_2", t), None, ALU.mult)\
                     .then_inc(S["kk_raw"], 1)
                for c in range(2 * KT):
                    t, b = c // 2, slice(P * (c % 2), P * (c % 2) + P)
                    own.did(v.tensor_tensor_scan(run[:, t, b], k.const("ones"), m["sig"][:, t, b], 0.0,
                                                 ALU.mult, ALU.add))
                own.settle()
                own.did(v.tensor_tensor(m["carry"][:, :], run[:, :, P - 1], run[:, :, P + 63], ALU.add))
                own.did(v.tensor_copy(middle[:, :, :], c4(run[:, :, :])[:, :, :, 63]))
                own.settle()
                own.did(v.tensor_tensor(m["carry"][:, :], m["carry"][:, :], middle[:, :, 0], ALU.subtract))
                own.settle()
                v.tensor_tensor(c4(run[:, :, :]), c4(run[:, :, :]),
                                middle[:, :, :].unsqueeze(3).broadcast_to([P, KT, TB, P]), ALU.subtract)\
                 .then_inc(S["run_ready"], 1)
                for t in range(KT):
                    own.did(v.tensor_scalar(rk[:, t, :], m["a"][:, t, :], -1.0, k.column("l1_k_a_2", t),
                                            ALU.add, ALU.mult))
                own.did(make_spread(k, v, spread))
                v.wait_ge(S["kk_raw"], KT)
                own.settle()
                v.scalar_tensor_tensor(m["k"][:, :, :], rk[:, :, :], 1.0, m["k"][:, :, :],
                                       ALU.add, ALU.mult).then_inc(S["k_gated"], 1)
                v.wait_ge(S["sums"], 1)
                v.tensor_scalar(norm[0:RW_HEADS, 0, :], k.ps[0:RW_HEADS, 4, 0:T], 1e-12, None, ALU.max)\
                 .then_inc(S["norms"], 1)
                v.wait_ge(S["k_gated"], 1)
                for t in range(KT):
                    v.scalar_tensor_tensor(c3(rk[:, t, :]), m["r"][:, t, :, :], k.column("l1_r_k_2", t),
                                           c3(m["k"][:, t, :]), ALU.mult, ALU.mult).then_inc(S["rk_ready"], 1)
                v.wait_ge(S["roots"], 1)
                v.reciprocal(norm[0:RW_HEADS, 1, :], norm[0:RW_HEADS, 0, :]).then_inc(S["inverses"], 1)
                v.wait_ge(S["bonus_sums"], 1)
                for q in range(4):
                    v.tensor_tensor(two(m["bonus"], q), two(m["v"], q), k.ps[:, q, :], ALU.mult)
                v.wait_ge(S["spread"], 1)
                for q in range(4):
                    own.did(v.tensor_tensor(two(kk, q), two(kk, q), k.ps[:, 4 + q, :], ALU.mult))
                own.settle()
                own.did(v.tensor_tensor(m["a"], m["a"], kk[:, :, :], ALU.mult))
                v.wait_ge(S["exps_ready"], 3)
                v.tensor_tensor(ar[:, :, :, 0, :], c4(kk[:, :, :]), c4(before[:, :, :]), ALU.mult)
                own.settle()
                v.tensor_tensor(m["a"], m["a"], inverse[:, :, :], ALU.mult)

            @block.gpsimd
            def _(pool):
                pool.wait_ge(S["run_ready"], 1)
                pool.tensor_tensor(before[:, :, :], run[:, :, :], m["sig"][:, :, :], ALU.subtract)\
                    .then_inc(S["before_ready"], 1)
                pool.wait_ge(S["exps_ready"], 3)
                pool.wait_ge(S["rk_ready"], KT)
                pool.tensor_tensor(ar[:, :, :, 1, :], m["r"], c4(run[:, :, :]), ALU.mult)
                pool.tensor_tensor(m["k"], m["k"], inverse[:, :, :], ALU.mult)

            @block.scalar
            def _(act):
                for t in range(KT):
                    act.wait_ge(S["kk_raw"], t + 1)
                    act.activation(squares[:, t, :], kk[:, t, :], ACT.Square).then_inc(S["squares"], 1)
                act.wait_ge(S["run_ready"], 1)
                act.activation(inverse[:, :, :], run[:, :, :], ACT.Exp, scale=-RATE).then_inc(S["inverse_exp"], 1)
                act.activation(m["carry"][:, :], m["carry"][:, :], ACT.Exp, scale=RATE)
                act.wait_ge(S["norms"], 1)
                act.activation(norm[0:RW_HEADS, 0, :], norm[0:RW_HEADS, 0, :], ACT.Sqrt).then_inc(S["roots"], 1)
                act.wait_ge(S["before_ready"], 1)
                act.activation(before[:, :, :], before[:, :, :], ACT.Exp, scale=RATE).then_inc(S["exps_ready"], 1)
                act.wait_ge(S["inverse_exp"], 1)
                act.activation(run[:, :, :], run[:, :, :], ACT.Exp, scale=RATE).then_inc(S["exps_ready"], 2)

            @block.tensor
            def _(pe):
                for t in range(KT):
                    pe.wait_ge(S["squares"], t + 1)
                    last = pe.matmul(k.ps[0:RW_HEADS, 4, 0:T], k.head_select(t), squares[:, t, :],
                                     start=t == 0, stop=t == KT - 1)
                last.then_inc(S["sums"], 1)
                for t in range(KT):
                    pe.wait_ge(S["rk_ready"], t + 1)
                    last = pe.matmul(k.ps[:, t // 2, T * (t % 2):T * (t % 2) + T], k.const("head_ones"), rk[:, t, :],
                                     start=True, stop=True)
                last.then_inc(S["bonus_sums"], 1)
                pe.wait_ge(S["inverses"], 1)
                spread_rows(k, pe, spread, norm[:, 1, :], 4).then_inc(S["spread"], 1)


def rwkv_transpose(k, m):
    S, stale = k.stage()
    jobs = [(m["v"], m["v_tok"][:, tb, :], tb) for tb in range(TB)] + \
           [(m["bk"][:, i, :, :], m["bk_tok"][:, i, :], 0) for i in range(2)]
    with k.nc.Block() as block:
        @block.sync
        def _(sp):
            clear(sp, stale)

        @block.tensor
        def _(pe):
            for n, (src, _, tb) in enumerate(jobs):
                for half in range(2):
                    for t in range(4):
                        last = pe.transpose(k.ps[:, 2 * n + half, P * t:P * t + P],
                                            src[:, 4 * half + t, P * tb:P * tb + P], k.const("identity"))
                    last.then_inc(S["transposed"], 1)

        @block.vector
        def _(v):
            for n, (_, dst, _) in enumerate(jobs):
                for half in range(2):
                    v.wait_ge(S["transposed"], 2 * n + half + 1)
                    v.tensor_copy(dst[:, 512 * half:512 * half + 512], k.ps[:, 2 * n + half, :])


def rwkv_chunks(k, m):
    with ExitStack() as ctx:
        sb = lambda name, *shape: k.sbuf(ctx, name, *shape)
        m["scores"] = sb("scores_t", RW_HEADS, 4, P)
        m["quad_mask"] = sb("quad_mask", 4, P)
        m["inverse"], m["inverse_t"] = sb("inverse", 4, 4, P), sb("inverse_t", 4, 4, P)
        m["product"] = sb("product", 2, 4, P)
        free = m["v"][:, :, :].rearrange("p k n -> p (k n)")
        m["rhs"] = free[:, 0:D].rearrange("p (i h n) -> p i h n", i=2, n=RW_DIM)
        m["x"] = free[:, D:2 * D].rearrange("p (h n) -> p h n", n=RW_DIM)
        m["state"] = sb("rwkv_state", KT, RW_DIM)
        for tb in range(TB):
            rwkv_chunk(k, m, tb)


def rwkv_chunk(k, m, tb):
    S, stale = k.stage()
    H, W = RW_HEADS, RW_DIM
    tok = slice(P * tb, P * tb + P)
    sc, x, u = m["scores"], m["inverse"], m["inverse_t"]
    lt = sc[:, :, 0, :].rearrange("p (g h) n -> p g h n", h=4)
    half = lambda h: slice(64 * (h % 2), 64 * (h % 2) + 64)
    with k.nc.Block() as block:
        @block.sync
        def _(sp):
            clear(sp, stale)

        @block.gpsimd
        def _(pool):
            if tb == 0:
                pool.memset(sc[:, :, :, :], 0.0).then_inc(S["scores_cleared"], 1)

        @block.tensor
        def _(pe):
            for h in range(H):
                if h >= 2:
                    pe.wait_ge(S["scores_out"], h - 1)
                ar = m["ar"][half(h), h // 2, tb, :, :].rearrange("p a n -> p (a n)")
                for i in range(2):
                    last = pe.matmul(k.ps[:, 6 + h % 2, T * i:T * i + T], m["bk"][half(h), i, h // 2, tok], ar,
                                     start=True, stop=True)
                last.then_inc(S["scores_ready"], 1)
            invert_tensor(k, pe, S, lt, x, u, m["product"], 4)
            pe.wait_ge(S["inverse_updated"], 4 * (LEVELS - 1))
            for h in range(H):
                out = k.ps[:, h % 2, W * (h // 2):W * (h // 2) + W]
                last = pe.matmul(out, sc[:, h, 2, :], m["v_tok"][:, tb, W * h:W * h + W], start=True, stop=tb == 0)
                if tb:
                    last = pe.matmul(out, m["ar"][half(h), h // 2, tb, 0, :], m["state"][half(h), h // 2, :],
                                     start=False, stop=True)
            last.then_inc(S["rhs_ready"], 1)
            pe.wait_ge(S["rhs_out"], 1)
            for h in range(H):
                last = pe.matmul(k.ps[:, 2 + h // 8, W * (h % 8):W * (h % 8) + W], u[:, h // 4, h % 4, :],
                                 m["rhs"][:, h % 2, h // 2, :], start=True, stop=True)
            last.then_inc(S["x_ready"], 1)
            pe.wait_ge(S["x_out"], 1)
            for h in range(H):
                j = h // 2
                out = k.ps[half(h), 4 + j // 4, P * (j % 4):P * (j % 4) + P]
                pe.matmul(out, m["x"][:, h, :], sc[:, h, 1, :], start=True, stop=False)
                last = pe.matmul(out, m["v_tok"][:, tb, W * h:W * h + W], sc[:, h, 3, :], start=False, stop=tb == 0)
                if tb:
                    last = pe.matmul(out, m["state"][half(h), j, :], m["ar"][half(h), j, tb, 1, :],
                                     start=False, stop=True)
            last.then_inc(S["outputs_ready"], 1)
            if tb == 0:
                for h in range(H):
                    out = k.ps[half(h), 6, W * (h // 2):W * (h // 2) + W]
                    pe.matmul(out, m["bk_tok"][:, 0, W * h:W * h + W], m["x"][:, h, :], start=True, stop=False)
                    last = pe.matmul(out, m["bk_tok"][:, 1, W * h:W * h + W], m["v_tok"][:, 0, W * h:W * h + W],
                                     start=False, stop=True)
                last.then_inc(S["state_ready"], 1)

        @block.scalar
        def _(act):
            invert_scalar(k, act, S, x, 4)
            act.wait_ge(S["x_ready"], 1)
            for i in range(2):
                last = act.activation(m["x"][:, 8 * i:8 * i + 8, :].rearrange("p h n -> p (h n)"), k.ps[:, 2 + i, :],
                                      ACT.Copy, scale=-1.0)
            last.then_inc(S["x_out"], 1)
            act.wait_ge(S["outputs_ready"], 1)
            for i in range(2):
                act.activation(k.xn[:, 4 * i:4 * i + 4, tok], four(k.ps[:, 4 + i, :]), ACT.Copy)

        @block.vector
        def _(v):
            own = Steps(v, S["vector_steps"])
            if tb == 0:
                for i, name in enumerate(("strict", "upto", "strict", "upto")):
                    own.did(v.tensor_copy(m["quad_mask"][:, i, :], k.const(name)))
            own.settle()
            if tb == 0:
                v.wait_ge(S["scores_cleared"], 1)
            for h in range(H):
                v.wait_ge(S["scores_ready"], h + 1)
                v.copy_predicated(sc[:, h, :, :], m["quad_mask"][:, :, :].bitcast(U32), four(k.ps[:, 6 + h % 2, :]))\
                 .then_inc(S["scores_out"], 1)
                if h % 4 == 3:
                    v.wait_ge(S["scores_out"], h + 1)
                    level0(k, v, own, S, lt, u, h // 4)
            invert_vector(k, v, S, x, u, m["product"], 4)
            v.wait_ge(S["rhs_ready"], 1)
            for i in range(2):
                last = v.tensor_copy(m["rhs"][:, i, :, :].rearrange("p h n -> p (h n)"), k.ps[:, i, :])
            last.then_inc(S["rhs_out"], 1)
            if tb == 0:
                v.wait_ge(S["state_ready"], 1)
                v.tensor_tensor(m["state"][:, :, :], k.ps[:, 6, :].rearrange("p (k n) -> p k n", n=W),
                                m["carry"][:, :].unsqueeze(2).broadcast_to([P, KT, W]), ALU.mult)


def rwkv_norm(k, m):
    S, stale = k.stage()
    y = k.xn
    with ExitStack() as ctx:
        sb = lambda name, *shape: k.sbuf(ctx, name, *shape)
        squares, spread, norm = sb("squares", KT, T), sb("spread", RW_HEADS, RW_DIM), sb("norms", 2, T)
        with k.nc.Block() as block:
            @block.sync
            def _(sp):
                clear(sp, stale)

            @block.tensor
            def _(pe):
                for q in range(4):
                    for t in (2 * q, 2 * q + 1):
                        last = pe.matmul(k.ps[:, q, T * (t % 2):T * (t % 2) + T], k.const("head_ones"), y[:, t, :],
                                         start=True, stop=True)
                    last.then_inc(S["sums"], 1)
                for t in range(KT):
                    pe.wait_ge(S["squares"], t // 2 + 1)
                    last = pe.matmul(k.ps[0:RW_HEADS, 4, 0:T], k.head_select(t), squares[:, t, :],
                                     start=t == 0, stop=t == KT - 1)
                last.then_inc(S["square_sums"], 1)
                pe.wait_ge(S["inverses"], 1)
                spread_rows(k, pe, spread, norm[:, 1, :], 0).then_inc(S["spread"], 1)

            @block.scalar
            def _(act):
                for q in range(4):
                    act.wait_ge(S["centred"], q + 1)
                    act.activation(squares[:, 2 * q:2 * q + 2, :], y[:, 2 * q:2 * q + 2, :], ACT.Square)\
                       .then_inc(S["squares"], 1)
                for t in range(KT):
                    last = act.activation(m["bonus"][:, t, :], m["bonus"][:, t, :], ACT.Identity,
                                          bias=k.column("l1_lnx_b_2", t))
                last.then_inc(S["biased"], 1)
                act.wait_ge(S["variances"], 1)
                act.activation(norm[0:RW_HEADS, 0, :], norm[0:RW_HEADS, 0, :], ACT.Sqrt).then_inc(S["roots"], 1)

            @block.vector
            def _(v):
                own = Steps(v, S["vector_steps"])
                pair = lambda tile, q: tile[:, 2 * q:2 * q + 2, :]
                bank = lambda q: k.ps[:, q, :].rearrange("p (k n) -> p k n", k=2)
                own.did(make_spread(k, v, spread))
                for q in range(4):
                    v.wait_ge(S["sums"], q + 1)
                    v.scalar_tensor_tensor(pair(y, q), bank(q), -1.0 / RW_DIM, pair(y, q), ALU.mult, ALU.add)\
                     .then_inc(S["centred"], 1)
                v.wait_ge(S["centred"], 4)
                v.wait_ge(S["square_sums"], 1)
                v.tensor_scalar(norm[0:RW_HEADS, 0, :], k.ps[0:RW_HEADS, 4, 0:T], 1.0 / RW_DIM, LNX_EPS, ALU.mult, ALU.add)\
                 .then_inc(S["variances"], 1)
                v.wait_ge(S["roots"], 1)
                own.settle()
                v.reciprocal(norm[0:RW_HEADS, 1, :], norm[0:RW_HEADS, 0, :]).then_inc(S["inverses"], 1)
                v.wait_ge(S["spread"], 1)
                for q in range(4):
                    own.did(v.tensor_tensor(pair(y, q), pair(y, q), bank(q), ALU.mult))
                own.settle()
                v.wait_ge(S["biased"], 1)
                for t in range(KT):
                    own.did(v.scalar_tensor_tensor(y[:, t, :], y[:, t, :], k.column("l1_lnx_g_2", t),
                                                   m["bonus"][:, t, :], ALU.mult, ALU.add))
                own.settle()
                v.tensor_tensor(y[:, :, :], y[:, :, :], m["g"][:, :, :], ALU.mult)


def store_output(k):
    S, stale = k.stage()
    with k.nc.Block() as block:
        @block.sync
        def _(sp):
            clear(sp, stale)
            sp.dma_start(k.dram["out"], k.x[:, :, :]).then_inc(k.output_stored, 16)
            sp.wait_ge(k.output_stored, 16)


def build(nc, dram):
    with ExitStack() as ctx:
        k = Kernel(nc, ctx, dram)
        load_constants(k)
        token_mixer(k)
        cross_attention(k)
        peer(k)
        rmsnorm(k, k.x, "g_final", k.x)
        ffn(k, "l0_ffn1")
        nsa_mixer(k)
        ffn(k, "l0_ffn2")
        ffn(k, "l1_ffn1")
        rwkv_mixer(k)
        ffn(k, "l1_ffn2")
        store_output(k)



def features(a):
    return a.reshape(-1, KT, P).transpose(2, 1, 0)


def column_tiles(w):
    return w.reshape(KT, P, -1, P).transpose(2, 1, 0, 3)


def chunks(tiles):
    return tiles.reshape(len(tiles), P, CHUNK)


def token_chunks(w, width):
    count = CHUNK // width
    return chunks(w.reshape(KT // count, count, P, -1, width).transpose(3, 0, 2, 1, 4).reshape(-1, P, count, width))


def ffn_chunks(gate, up, down):
    g, u, d = column_tiles(gate), column_tiles(up), down.reshape(FT, P, KT, P)
    order = [g[0], u[0]]
    for f in range(1, FT):
        order += [g[f], u[f], d[f - 1]]
    return np.stack(order + [d[FT - 1]])


def layouts(a):
    first = {n: v[0] for n, v in a.items() if v.ndim > 1 and v.shape[0] == 1}
    out = {"x": features(first["x"]), "mem": features(first["mem"]), "consts": const_tiles()}

    columns = []
    for name, tiles in COLUMNS:
        v = first[name] if name in first else a[name]
        if name == "gdn_conv":
            columns.append(v.reshape(CONV_TAPS, 12, P).transpose(2, 1, 0).reshape(P, -1))
        elif name == "l0_conv_w_2":
            columns.append(v.reshape(CONV2_TAPS, 4, P).transpose(2, 1, 0).reshape(P, -1))
        else:
            columns.append(v.reshape(tiles, P).T)
    out["columns"] = np.concatenate(columns, axis=1)

    w = first["w_in"]
    sq, sk, sv, gq, gk, gv, gz = (w[:, 512 * i:512 * i + 512] for i in range(7))
    ba, gates = w[:, 3584:3592], w[:, 3592:]
    out["w_in"] = np.concatenate([chunks(column_tiles(np.concatenate([gq, gk, gv, sq, sk], axis=1))),
                                  token_chunks(sv, 4 * P),
                                  chunks(column_tiles(np.concatenate([gz, gates], axis=1)))])
    out["w_ba"] = ba.reshape(KT, P, 8).transpose(1, 0, 2)
    rows = np.concatenate([first["gdn_a_log"], first["gdn_dt_bias"]])
    out["gdn_rows"] = np.broadcast_to(rows, (P, 8))
    out["w_up_pair"] = np.concatenate([first[n].reshape(4, P, KT, P).transpose(2, 1, 0, 3)
                                       for n in ("w_sb_up", "w_gdn_up")], axis=2)
    for name in ("w_mix_out", "w_cq", "w_co", "w_pq"):
        out[name] = column_tiles(first[name])
    out["w_ckv"] = np.concatenate([chunks(column_tiles(first["w_ckv"][:, :D])),
                                   token_chunks(first["w_ckv"][:, D:], 4 * P)])
    out["subkeys"] = first["peer_subkeys"].reshape(2 * PEER_HEADS, P, P).transpose(2, 0, 1)
    out["peer_u"], out["peer_v"] = first["peer_u"], first["peer_v"]

    for f in ("l0_ffn1", "l0_ffn2", "l1_ffn1", "l1_ffn2"):
        out[f] = ffn_chunks(a[f"{f}_w_gate_2"], a[f"{f}_w_up_2"], a[f"{f}_w_down_2"])

    w = a["l0_w_in_2"]
    q = w[:, :512].reshape(D, 2, 4, 64).transpose(0, 2, 1, 3).reshape(D, 512)
    kc, vc, ks, vs, kw, vw = (w[:, 536 + P * i:664 + P * i] for i in range(6))
    groups = lambda c: np.concatenate([c[:, :64], c[:, :64], c[:, 64:], c[:, 64:]], axis=1)
    out["l0_in"] = np.concatenate([chunks(column_tiles(np.concatenate([q, groups(kc), groups(vc), ks, kw], axis=1))),
                                   token_chunks(np.concatenate([vs, vw], axis=1), 2 * P),
                                   chunks(column_tiles(w[:, 1304:]))])
    out["w_g"] = w[:, 512:536].reshape(KT, P, 24).transpose(1, 0, 2)
    w = a["l0_w_out_2"]
    nsa_rows = w[:512].reshape(2, 4, 64, D).transpose(1, 0, 2, 3).reshape(512, D)
    out["l0_out"] = column_tiles(np.concatenate([nsa_rows, w[512:]]))
    out["cmp_w1"] = np.stack([a[f"l0_cmp_w1_{n}_2"].reshape(2, CMP_STRIDE, 64, P).transpose(0, 2, 1, 3)
                              .reshape(P, CMP_STRIDE, P) for n in "kv"], axis=1)
    out["cmp_w2"] = np.stack([a[f"l0_cmp_w2_{n}_2"] for n in "kv"], axis=1)
    out["cmp_pos"] = np.stack([a[f"l0_cmp_pe_{n}_2"].reshape(2, CMP_STRIDE, 64).transpose(0, 2, 1)
                               .reshape(P, CMP_STRIDE) for n in "kv"], axis=1)

    out["l1_rkv"] = np.concatenate([column_tiles(a[f"l1_w_{n}_2"]) for n in "rkv"])
    out["l1_o"] = column_tiles(a["l1_w_o_2"])
    for n in ("dec", "a", "g"):
        out[f"w_{n}1"] = a[f"l1_w_{n}1_2"].reshape(KT, P, -1).transpose(1, 0, 2)
        out[f"w_{n}2"] = a[f"l1_w_{n}2_2"]
    for name, n in STREAM:
        assert out[name].shape[0] == n, name
        out[name] = out[name].reshape(n, P, CHUNK)
    return {n: np.ascontiguousarray(v) for n, v in out.items()}


def kernel(**inputs):
    from concourse import bacc
    from concourse.bass_utils import run_bass_kernel_spmd

    arrays = layouts({n: np.asarray(v) for n, v in inputs.items()})
    nc = bacc.Bacc("TRN2", target_bir_lowering=False, num_devices=1)
    dram = {n: nc.dram_tensor(f"in_{n}", v.shape, mybir.dt.from_np(v.dtype), kind="ExternalInput").ap()
            for n, v in arrays.items()}
    dram["out"] = nc.dram_tensor("out_x", (P, KT, T), F32, kind="ExternalOutput").ap()
    build(nc, dram)
    result = run_bass_kernel_spmd(nc, [{f"in_{n}": v for n, v in arrays.items()}], core_ids=[0])
    x = np.asarray(result.results[0]["out_x"])
    return np.ascontiguousarray(x.transpose(2, 1, 0).reshape(1, T, D))
```
